# Optimizing a Trainium2 kernel written in Bass

```python
import jax, jax.numpy as jnp
from jax import lax
import numpy as np

D_MODEL = 2048
BATCH = 1
SEQ = 1024
DEPTH = 1
DEC_BATCH = 1
DEC_SEQ = 64
PAST_LEN = 1024

CHUNK = 64
WINDOW = 128
WIN_CHUNKS = WINDOW // CHUNK
HEAD_DIM = 64
N_Q_HEADS = 16
N_KV_HEADS = 4
GQA_GROUP = N_Q_HEADS // N_KV_HEADS
ATTN_WIDTH = N_Q_HEADS * HEAD_DIM
KV_WIDTH = N_KV_HEADS * HEAD_DIM
GLA_HEADS = 4
GLA_DK = 512
GLA_DV = 1024
GLA_HK = GLA_DK // GLA_HEADS
GLA_HV = GLA_DV // GLA_HEADS
GLA_RANK = 16
GLA_TAU = 16.0
NORM_EPS = 1e-6
IN_SIZES = (ATTN_WIDTH, KV_WIDTH, KV_WIDTH, ATTN_WIDTH,
            GLA_DK, GLA_DK, GLA_DV, GLA_DV, GLA_RANK, D_MODEL, D_MODEL)
IN_COLS = sum(IN_SIZES)

kernel_name = 'hybrid_swa_sink_gla_stream_step'

def rms_norm(x, g):
    xf = x.astype(jnp.float32)
    y = xf * lax.rsqrt(jnp.mean(xf * xf, axis=-1, keepdims=True) + NORM_EPS)
    return (y * g.astype(jnp.float32)).astype(x.dtype)

def split_cols(p):
    idx = []
    acc = 0
    for s in IN_SIZES[:-1]:
        acc += s
        idx.append(acc)
    return jnp.split(p, idx, axis=-1)

def alibi_slopes():
    h = jnp.arange(1, N_Q_HEADS + 1, dtype=jnp.float32)
    return jnp.exp2(-8.0 * h / N_Q_HEADS).reshape(N_KV_HEADS, GQA_GROUP)

def banded_attention(q, k, v, sinks, q_pos, k_pos, k_valid):
    s = jnp.einsum('bnqkgd,bnskd->bnkgqs', q, k).astype(jnp.float32) * (HEAD_DIM ** -0.5)
    dist = jnp.abs(q_pos[:, None] - k_pos[None, :]).astype(jnp.float32)
    s = s - alibi_slopes()[:, :, None, None] * dist
    s = jnp.where(k_valid[None, :, None, None, None, :], s, -jnp.inf)
    sink = sinks.astype(jnp.float32).reshape(N_KV_HEADS, GQA_GROUP)[None, None, :, :, None, None]
    m = jnp.maximum(jnp.max(s, axis=-1, keepdims=True), sink)
    p = jnp.exp(s - m)
    p = p / (jnp.sum(p, axis=-1, keepdims=True) + jnp.exp(sink - m))
    return jnp.einsum('bnkgqs,bnskd->bnqkgd', p.astype(v.dtype), v)

def attn_prompt(q, k, v, sinks):
    B, S = q.shape[:2]
    nc = S // CHUNK
    qb = q.reshape(B, nc, CHUNK, N_KV_HEADS, GQA_GROUP, HEAD_DIM)
    pad = ((0, 0), (WIN_CHUNKS, 0), (0, 0), (0, 0), (0, 0))
    kp = jnp.pad(k.reshape(B, nc, CHUNK, N_KV_HEADS, HEAD_DIM), pad)
    vp = jnp.pad(v.reshape(B, nc, CHUNK, N_KV_HEADS, HEAD_DIM), pad)
    kb = jnp.concatenate([kp[:, j:j + nc] for j in range(WIN_CHUNKS + 1)], axis=2)
    vb = jnp.concatenate([vp[:, j:j + nc] for j in range(WIN_CHUNKS + 1)], axis=2)
    q_pos = WIN_CHUNKS * CHUNK + jnp.arange(CHUNK)
    k_pos = jnp.arange((WIN_CHUNKS + 1) * CHUNK)
    k_valid = (jnp.arange(nc)[:, None] - WIN_CHUNKS + k_pos[None, :] // CHUNK) >= 0
    o = banded_attention(qb, kb, vb, sinks, q_pos, k_pos, k_valid)
    return o.reshape(B, S, ATTN_WIDTH)

def attn_sample(q, k, v, cache_k, cache_v, sinks):
    B, T = q.shape[:2]
    L = cache_k.shape[1]
    k_all = jnp.concatenate([cache_k.astype(k.dtype), k], axis=1)
    v_all = jnp.concatenate([cache_v.astype(v.dtype), v], axis=1)
    q_pos = L + jnp.arange(T)
    k_pos = jnp.arange(L + T)
    k_valid = jnp.ones((1, L + T), dtype=bool)
    o = banded_attention(q[:, None], k_all[:, None], v_all[:, None], sinks, q_pos, k_pos, k_valid)
    return o.reshape(B, T, ATTN_WIDTH), k_all[:, T:], v_all[:, T:]

def gla_block(s0, blk):
    q, k, v, la = blk
    c = q.shape[2]
    b = jnp.cumsum(la, axis=2)
    causal = jnp.tril(jnp.ones((c, c), dtype=bool))[None, None, :, :, None]
    decay = jnp.where(causal, jnp.exp(jnp.minimum(b[:, :, :, None, :] - b[:, :, None, :, :], 0.0)), 0.0)
    scores = jnp.einsum('bhtd,bhsd,bhtsd->bhts', q, k, decay)
    o = jnp.einsum('bhts,bhsv->bhtv', scores, v) + jnp.einsum('bhtd,bhdv->bhtv', q * jnp.exp(b), s0)
    b_end = b[:, :, -1, :]
    s1 = jnp.exp(b_end)[..., None] * s0 + jnp.einsum('bhsd,bhsv->bhdv', k * jnp.exp(b_end[:, :, None, :] - b), v)
    return s1, o

def gla_mix(q, k, v, log_a, state):
    B, T, _ = q.shape
    blk = min(CHUNK, T)
    nb = T // blk

    def to_blocks(a, d):
        return a.astype(jnp.float32).reshape(B, nb, blk, GLA_HEADS, d).transpose(1, 0, 3, 2, 4)

    qb = to_blocks(q, GLA_HK) * (GLA_HK ** -0.5)
    kb = to_blocks(k, GLA_HK)
    vb = to_blocks(v, GLA_HV)
    lb = to_blocks(log_a, GLA_HK)
    if state is None:
        s0 = jnp.zeros((B, GLA_HEADS, GLA_HK, GLA_HV), jnp.float32)
    else:
        s0 = state.astype(jnp.float32)
    s1, ob = lax.scan(gla_block, s0, (qb, kb, vb, lb))
    o = ob.transpose(1, 0, 3, 2, 4).reshape(B, T, GLA_HEADS, GLA_HV)
    return o, s1

def trunk_layer(h, norm_pre, norm_post, w_in, b_gate, attn_sinks, w_forget_up, b_forget,
                gla_norm, w_branch_attn, w_branch_gla, w_out, cache_k, cache_v, state):
    B, T, _ = h.shape
    u = rms_norm(h, norm_pre)
    qa, ka, va, za, qg, kg, vg, zg, lr, ga, gg = split_cols(u @ w_in)
    qa = qa.reshape(B, T, N_KV_HEADS, GQA_GROUP, HEAD_DIM)
    ka = ka.reshape(B, T, N_KV_HEADS, HEAD_DIM)
    va = va.reshape(B, T, N_KV_HEADS, HEAD_DIM)
    if cache_k is None:
        oa = attn_prompt(qa, ka, va, attn_sinks)
        keep = min(WINDOW, T)
        new_k, new_v = ka[:, T - keep:], va[:, T - keep:]
    else:
        oa, new_k, new_v = attn_sample(qa, ka, va, cache_k, cache_v, attn_sinks)
    y_a = (oa * jax.nn.silu(za)) @ w_branch_attn
    log_a = jax.nn.log_sigmoid((lr @ w_forget_up + b_forget).astype(jnp.float32)) / GLA_TAU
    og, new_state = gla_mix(qg, kg, vg, log_a, state)
    og = rms_norm(og.astype(h.dtype), gla_norm).reshape(B, T, GLA_DV)
    y_g = (og * jax.nn.silu(zg)) @ w_branch_gla
    merged = jax.nn.sigmoid(ga + b_gate[:D_MODEL]) * y_a + jax.nn.sigmoid(gg + b_gate[D_MODEL:]) * y_g
    h = h + rms_norm(merged @ w_out, norm_post)
    return h, new_k, new_v, new_state.astype(h.dtype)

def setup_inputs(seed: int = 0) -> dict:
    key = jax.random.key(seed)
    ks = jax.random.split(key, 18)
    f32 = jnp.float32
    L = min(WINDOW, PAST_LEN)
    nrm = lambda k, shape: jax.random.normal(k, shape, f32)
    return {
        'x_prompt': nrm(ks[0], (BATCH, SEQ, D_MODEL)),
        'x_sample': nrm(ks[1], (DEC_BATCH, DEC_SEQ, D_MODEL)),
        'cache_k': nrm(ks[2], (DEPTH, DEC_BATCH, L, N_KV_HEADS, HEAD_DIM)),
        'cache_v': nrm(ks[3], (DEPTH, DEC_BATCH, L, N_KV_HEADS, HEAD_DIM)),
        'state_gla': nrm(ks[4], (DEPTH, DEC_BATCH, GLA_HEADS, GLA_HK, GLA_HV)),
        'norm_pre': 1.0 + 0.05 * nrm(ks[5], (DEPTH, D_MODEL)),
        'norm_post': 1.0 + 0.05 * nrm(ks[6], (DEPTH, D_MODEL)),
        'w_in': nrm(ks[7], (DEPTH, D_MODEL, IN_COLS)) * D_MODEL ** -0.5,
        'b_gate': 0.01 * nrm(ks[8], (DEPTH, 2 * D_MODEL)),
        'attn_sinks': 0.5 * nrm(ks[9], (DEPTH, N_Q_HEADS)),
        'w_forget_up': nrm(ks[10], (DEPTH, GLA_RANK, GLA_DK)) * GLA_RANK ** -0.5,
        'b_forget': 0.1 * nrm(ks[11], (DEPTH, GLA_DK)),
        'gla_norm': 1.0 + 0.05 * nrm(ks[12], (DEPTH, GLA_HV)),
        'w_branch_attn': nrm(ks[13], (DEPTH, ATTN_WIDTH, D_MODEL)) * ATTN_WIDTH ** -0.5,
        'w_branch_gla': nrm(ks[14], (DEPTH, GLA_DV, D_MODEL)) * GLA_DV ** -0.5,
        'w_out': nrm(ks[15], (DEPTH, D_MODEL, D_MODEL)) * D_MODEL ** -0.5,
    }

def reference(x_prompt, x_sample, cache_k, cache_v, state_gla, norm_pre, norm_post, w_in, b_gate,
              attn_sinks, w_forget_up, b_forget, gla_norm, w_branch_attn, w_branch_gla, w_out):
    h_p, h_s = x_prompt, x_sample
    kp_l, vp_l, sp_l, ks_l, vs_l, ss_l = [], [], [], [], [], []
    for l in range(DEPTH):
        w = (norm_pre[l], norm_post[l], w_in[l], b_gate[l], attn_sinks[l], w_forget_up[l],
             b_forget[l], gla_norm[l], w_branch_attn[l], w_branch_gla[l], w_out[l])
        h_p, kp, vp, sp = trunk_layer(h_p, *w, None, None, None)
        h_s, ks, vs, ss = trunk_layer(h_s, *w, cache_k[l], cache_v[l], state_gla[l])
        kp_l.append(kp); vp_l.append(vp); sp_l.append(sp)
        ks_l.append(ks); vs_l.append(vs); ss_l.append(ss)
    return (h_p, h_s, jnp.stack(kp_l), jnp.stack(vp_l), jnp.stack(sp_l),
            jnp.stack(ks_l), jnp.stack(vs_l), jnp.stack(ss_l))


_drawn_inputs = setup_inputs


def setup_inputs(seed=0):
    import zlib

    import numpy as np

    out = dict(_drawn_inputs(seed))
    spreads = {}
    factors = {'b_gate': 8.0, 'attn_sinks': 8.0}
    for name, (base, spread) in spreads.items():
        noise = np.random.default_rng([zlib.crc32(name.encode()), seed]).standard_normal(out[name].shape)
        drawn = base * np.exp(spread * noise) if base else spread * noise
        out[name] = __import__('jax').numpy.asarray(drawn.astype(out[name].dtype))
    for name, factor in factors.items():
        out[name] = (out[name] * factor).astype(out[name].dtype)
    return out
```

```python
import concourse.bass as bass
from concourse import mybir
from contextlib import ExitStack

D_MODEL, SEQ, DEC, WINDOW = 2048, 1024, 64, 128
TOKENS = SEQ + DEC
HEADS, KV_HEADS, HEAD_DIM = 16, 4, 64
GROUP = HEADS // KV_HEADS
GLA_HEADS, GLA_DK, GLA_DV, RANK = 4, 128, 256, 16
TAU, EPS = 16.0, 1e-6
CHUNK = 64
P = 128
KT = D_MODEL // P
HK = KT // 2
GRP = [(0, 364), (364, 362), (726, 362)]
GW = 364
T_Q, T_V, T_ZA, T_K, T_GQ, T_GK, T_GV, T_ZG = 0, 8, 10, 18, 20, 24, 28, 36
N_P = 44
N_GATE = 32
N_OUT = D_MODEL // P
W_GATE, W_BRANCH, W_OUT = N_P, N_P + N_GATE, N_P + N_GATE + N_OUT
N_IT = SEQ // P + 1
BLOCKS = 8
N_T = 15
MASKED = -1e30


def alibi_slope(h):
    return 2.0 ** (-8.0 * (h + 1) / HEADS)


def build_trunk(nc, xT, w_tiles, w_lr, w_up, norms, bgate, sinks, gnorm, kT_cache, v_cache, state_in,
                ident_c, dist_c, decay_c, mask_c,
                yT, k_prompt, v_prompt, state_prompt, k_sample, v_old, v_new, state_sample):
    f32, f32r = mybir.dt.float32, mybir.dt.float32r
    ALU = mybir.AluOpType
    ACT = mybir.ActivationFunctionType
    AX = mybir.AxisListType

    p_dram = nc.dram_tensor("p_scratch", [N_P, P, TOKENS], f32).ap()
    g_dram = nc.dram_tensor("gate_scratch", [N_GATE, P, TOKENS], f32).ap()
    o_dram = nc.dram_tensor("o_scratch", [KT, P, TOKENS], f32).ap()
    m_dram = nc.dram_tensor("m_scratch", [KT, P, TOKENS], f32).ap()
    la_dram = nc.dram_tensor("la_scratch", [N_IT, P, GLA_HEADS * GLA_DK], f32).ap()

    with ExitStack() as ctx:
        def sb(name, shape, dt=f32, to=None):
            return (to or ctx).enter_context(nc.sbuf_tensor(name, shape, dt))

        def sem(name):
            return ctx.enter_context(nc.semaphore(name))

        w_raw = sb("w_raw", [P, 2, HK, P])
        w_hi = sb("w_hi", [P, 2, HK, P], f32r)
        w_lo = sb("w_lo", [P, 2, HK, P], f32r)
        stage = sb("stage", [P, TOKENS])
        stage2 = sb("stage2", [P, TOKENS])
        norm_sb = sb("norm_sb", [P, 2, KT])
        bg_sb = sb("bg_sb", [P, N_GATE])
        bg_half = sb("bg_half", [P, N_GATE])
        gn_sb = sb("gn_sb", [P, 2])
        gn_half = sb("gn_half", [P, 2])
        sink_sb = sb("sink_sb", [P, HEADS])
        nsink_sb = sb("nsink_sb", [P, HEADS])
        ident = sb("ident", [P, P])
        ones = sb("ones", [P, P])
        lr = sb("lr", [2 * RANK + 1, TOKENS])
        minus_half = sb("minus_half", [P, 1])
        mean = sb("mean", [P, 3])
        root = sb("root", [P, 3])

        with ExitStack() as ph:
            uh = [sb(f"uh{g}", [P, KT, GW], f32r, ph) for g in range(3)]
            ul = [sb(f"ul{g}", [P, KT, GW], f32r, ph) for g in range(3)]
            xr = sb("xr", [P, 2, 2, GW], f32, ph)
            sqx = sb("sqx", [P, 2, 2, GW], f32, ph)
            rstd = sb("rstd", [P, 3, GW], f32, ph)
            ssq = sb("ssq", [P, 3, GW], f32, ph)
            wlr_raw = sb("wlr_raw", [P, KT, RANK], f32, ph)
            wlr = sb("wlr", [P, KT, P], f32r, ph)
        with ExitStack() as ph:
            wup = sb("wup", [2 * RANK + 1, GLA_HEADS * GLA_DK], f32, ph)
            lmin = sb("lmin", [P, N_IT, 512], f32, ph)
            lexp = sb("lexp", [P, N_IT, 512], f32, ph)
        with ExitStack() as ph:
            qa = sb("qa", [P, 18, P], f32, ph)
            kw = sb("kw", [P, 2, 2 * P], f32, ph)
            gl = sb("gl", [P, 24, P], f32, ph)
            lac = sb("lac", [P, 512], f32, ph)
            bias = sb("bias", [P, HEADS, 2 * P], f32, ph)
            dist = sb("dist", [P, 2 * P], f32, ph)
            decay = sb("decay", [P, BLOCKS * CHUNK], f32, ph)
            mask = sb("mask", [P, 7, CHUNK], f32, ph)
            th = sb("th", [P, 8, P], f32, ph)
            zs = sb("zs", [P, 8, P], f32, ph)
            v_prev = sb("v_prev", [P, KV_HEADS * HEAD_DIM], f32, ph)
            v_cur = sb("v_cur", [P, KV_HEADS * HEAD_DIM], f32, ph)
            s8 = sb("s8", [P, 2, 2, 2 * P], f32, ph)
            pb = sb("pb", [P, 2, 2, 2 * P], f32, ph)
            m8 = sb("m8", [P, 2, 2], f32, ph)
            nm = sb("nm", [P, 2, 2], f32, ph)
            snm = sb("snm", [P, 2, 2], f32, ph)
            rsum = sb("rsum", [P, 2, 2], f32, ph)
            esink = sb("esink", [P, 2, 2], f32, ph)
            den = sb("den", [P, 2, 2], f32, ph)
            rden = sb("rden", [P, 2, 2], f32, ph)
            pT = sb("pT", [P, 2, 2, GROUP, P], f32, ph)
            oa = sb("oa", [P, 8, P], f32, ph)
            vg = sb("vg", [P, GLA_HEADS * GLA_DV], f32, ph)
            ex = sb("ex", [P, GLA_HEADS, 2, BLOCKS, CHUNK], f32, ph)
            qe = sb("qe", [P, GLA_HEADS, 2, 7, CHUNK], f32, ph)
            ke = sb("ke", [P, 2, 2, 6, CHUNK], f32, ph)
            kend = sb("kend", [P, 2, 2, CHUNK], f32, ph)
            tm = sb("tm", [P, 7, CHUNK], f32, ph)
            gsc = sb("gsc", [P, GLA_HEADS, CHUNK], f32, ph)
            kt_tok = sb("kt_tok", [P, GLA_HEADS, GLA_DK], f32, ph)
            st = sb("st", [P, 2, GLA_HEADS, GLA_DV], f32, ph)
            os_ = sb("os_", [P, GLA_HEADS, 2, P], f32, ph)
            sq = sb("sq", [P, GLA_HEADS, 2, P], f32, ph)
            gmean = sb("gmean", [P, GLA_HEADS], f32, ph)
            groot = sb("groot", [P, GLA_HEADS], f32, ph)
            gdiag = sb("gdiag", [P, GLA_HEADS, P], f32, ph)
            t1 = sb("t1", [P, GLA_HEADS, 2, P], f32, ph)
            thg = sb("thg", [P, 8, P], f32, ph)
            zg2 = sb("zg2", [P, 8, P], f32, ph)
            og = sb("og", [P, GLA_HEADS, 2, P], f32, ph)
        with ExitStack() as ph:
            bh = [sb(f"bh{g}", [P, KT, GW], f32r, ph) for g in range(3)]
            bl = [sb(f"bl{g}", [P, KT, GW], f32r, ph) for g in range(3)]
            br = sb("br", [P, 2, 2, GW], f32, ph)
            gate = sb("gate", [P, 2, TOKENS], f32, ph)
            ya = sb("ya", [P, TOKENS], f32, ph)
        with ExitStack() as ph:
            mh, ml = [None] * 3, [None] * 3
            mh[0] = sb("mh0", [P, KT, GW], f32r, ph)
            mh[1] = sb("mh1", [P, KT, GW], f32r, ph)
            mh[2] = sb("mh2", [P, KT, GW], f32r, ph)
            for g in range(3):
                ml[g] = sb(f"ml{g}", [P, KT, GW], f32r, ph)
            mr = sb("mr", [P, 2, 2, GW], f32, ph)
            out_sb = [sb("out0", [P, KT, GW], f32, ph)]
            rso = sb("rso", [P, GW], f32, ph)
            ssqo = sb("ssqo", [P, GW], f32, ph)
            sqo = sb("sqo", [P, GW], f32, ph)
        with ExitStack() as ph:
            out_sb.append(sb("out1", [P, KT, GW], f32, ph))
            out_sb.append(sb("out2", [P, KT, GW], f32, ph))

        diag_x = xr[:].rearrange("p a b t -> p (a b t)")[:, 0:3 * P].rearrange("p (n q) -> p n q", n=3)
        diag_m = mr[:].rearrange("p a b t -> p (a b t)")[:, 0:3 * P].rearrange("p (n q) -> p n q", n=3)

        def blocks(w):
            return [(n, n * P, min(P, w - n * P)) for n in range(-(-w // P))]

        bank = [ctx.enter_context(nc.psum_tensor(f"bank{i}", [P, 512], f32)) for i in range(8)]

        s_const = sem("consts_loaded")
        s_cset = sem("consts_set")
        s_w = [sem("w_half0_loaded"), sem("w_half1_loaded")]
        s_whi = sem("w_hi_done")
        s_wlo = sem("w_lo_done")
        s_mm = sem("half_products_done")
        s_x = [sem("operand_slot0_loaded"), sem("operand_slot1_loaded")]
        s_uhi = sem("operand_hi_done")
        s_ulo = sem("operand_lo_done")
        s_sqx = sem("x_squared")
        s_ssq = sem("square_sums_done")
        s_ones = sem("ones_product_done")
        s_rst = sem("mean_squares_ready")
        s_dg = sem("root_diagonals_ready")
        s_spread = sem("roots_spread")
        s_rstd = sem("rstd_ready")
        s_lrhi = sem("lr_weights_hi_done")
        s_lrlo = sem("lr_weights_lo_done")
        s_lrp = sem("lr_product_done")
        s_lr = sem("lr_scaled")
        s_ev = sem("tile_chunks_evacuated")
        s_st = sem("tiles_stored")
        s_th = sem("gate_tanh_done")
        s_pass = {e.engine: sem(f"{n}_waits_passed") for n, e in (("sync", nc.sync), ("scalar", nc.scalar), ("vector", nc.vector))}
        s_rsp = sem("roots_ready")
        s_pset = sem("gpsimd_constants_set")
        s_var = sem("gla_mean_squares_ready")
        s_gdg = sem("gla_root_diagonals_ready")
        s_rb = sem("gla_roots_spread")
        s_t1 = sem("gla_output_scaled")
        s_z2 = sem("gla_gate_silu")
        s_gpw = sem("gla_rstd_ready")
        s_y2 = sem("gla_branch_weighted")
        s_ssz = sem("square_sums_cleared")

        s_lap = sem("forget_product_done")
        s_lmin = sem("forget_min_done")
        s_labs = sem("forget_abs_done")
        s_lexp = sem("forget_exp_done")
        s_lln = sem("forget_log_done")
        s_la = sem("forget_logs_ready")
        s_wup = sem("forget_weights_loaded")
        s_last = sem("forget_logs_stored")
        s_bc = sem("attention_consts_loaded")
        s_bias = sem("alibi_tables_ready")
        s_kv = sem("cache_outputs_stored")

        s_qa = sem("attention_inputs_loaded")
        s_kw = sem("key_window_loaded")
        s_gl = sem("gla_inputs_loaded")
        s_lac = sem("forget_block_loaded")
        s_vp = sem("cached_values_loaded")
        s_pt = sem("transposes_done")
        s_tev = sem("transposes_evacuated")
        s_sc = sem("scores_done")
        s_a = sem("scores_biased")
        s_nm = sem("negated_maxima_ready")
        s_snm = sem("sink_minus_max_ready")
        s_ep = sem("exponentials_done")
        s_den = sem("denominators_ready")
        s_rden = sem("reciprocals_ready")
        s_pr = sem("probabilities_ready")
        s_pv = sem("weighted_values_done")
        s_tz = sem("attention_gate_tanh")
        s_zs = sem("attention_gate_silu")
        s_oa = sem("attention_output_ready")
        s_oast = sem("attention_output_stored")
        s_e = sem("decay_sums_done")
        s_ex = sem("decay_exps_done")
        s_qk = sem("decayed_qk_ready")
        s_gs = sem("gla_scores_done")
        s_gm = sem("gla_scores_masked")
        s_gr = sem("gla_scores_ready")
        s_o = sem("gla_output_products_done")
        s_oev = sem("gla_output_evacuated")
        s_ds = sem("state_product_done")
        s_su = sem("state_updated")
        s_rm = sem("gla_square_sums_done")
        s_tg = sem("gla_gate_tanh")
        s_og = sem("gla_output_ready")
        s_ogst = sem("gla_output_stored")
        s_vsh = sem("values_shifted")
        s_s0 = sem("state_cleared")
        s_sst = sem("state_stored")
        s_sld = sem("state_loaded")

        s_g = [sem("gate_a_loaded"), sem("gate_b_loaded")]
        s_ya = sem("branch_chunks_weighted")
        s_yg = sem("gla_chunks_weighted")
        s_mst = sem("merged_stored")
        s_oev2 = sem("output_tiles_evacuated")
        s_sqo = sem("output_squares_summed")
        s_xo = sem("residual_loaded")
        s_fin = sem("output_steps")
        s_y = sem("output_stored")

        def half_done(tile, h):
            return 6 * tile + 3 * h + 3

        def out_half_done(tile, h):
            return 6 * W_OUT + 2 * (tile - W_OUT) + h + 1

        def ge(eng, s, value):
            if not isinstance(value, int) or value > 0:
                eng.wait_ge(s, value)

        def settle(eng):
            eng.sem_inc(s_pass[eng.engine], 1)

        BY_HALF = [(h, g, j) for h in range(2) for g in range(3) for j in range(HK // 2)]
        BY_GROUP = [(h, g, j) for g in range(3) for h in range(2) for j in range(HK // 2)]
        NB = len(BY_HALF)

        def w_src(tile, h):
            return w_tiles[tile, :, h * HK * P:(h + 1) * HK * P].rearrange("p (k c) -> p k c", c=P)

        block = ctx.enter_context(nc.Block())

        @block.sync
        def _(sp):
            def load_w(tile, h, index=None):
                ge(sp, s_wlo, 2 * (tile - 1) + h + 1)
                if not isinstance(tile, int):
                    settle(sp)
                sp.dma_start(w_raw[:, h], w_src(tile if index is None else index, h)).then_inc(s_w[h], 16)

            def load_operand(src, ring, order, base, squares):
                view = src.rearrange("(k p) t -> p k t", p=P)
                for b, (h, g, j) in enumerate(order):
                    n = base + b
                    k, (a, w) = h * HK + 2 * j, GRP[g]
                    if b >= 2:
                        sp.wait_ge(s_ulo, n - 1)
                        if squares:
                            sp.wait_ge(s_sqx, n - 1)
                    settle(sp)
                    sp.dma_start(ring[:, b % 2, :, 0:w], view[:, k:k + 2, a:a + w]).then_inc(s_x[b % 2], 16)

            sp.dma_start(norm_sb[:], norms).then_inc(s_const, 16)
            load_w(0, 0)
            sp.dma_start(wlr_raw[:], w_lr).then_inc(s_const, 16)
            sp.dma_start(bg_sb[:], bgate).then_inc(s_const, 16)
            sp.dma_start(gn_sb[:], gnorm).then_inc(s_const, 16)
            sp.dma_start(sink_sb[:], sinks).then_inc(s_const, 16)
            sp.dma_start(ident[:], ident_c).then_inc(s_const, 16)
            load_w(0, 1)
            load_operand(xT, xr, BY_HALF, 0, True)
            load_w(1, 0)
            load_w(1, 1)

            def store_p(tile):
                sp.wait_ge(s_ev, 3 * tile + 3)
                settle(sp)
                sp.dma_start(p_dram[tile], stage[:]).then_inc(s_st, 16)

            with sp.Fori(1, N_P) as t:
                load_w(t + 1, 0)
                store_p(t - 1)
                load_w(t + 1, 1)
            store_p(N_P - 1)

            def store_gate(m):
                sp.wait_ge(s_th, 3 * m + 3)
                settle(sp)
                sp.dma_start(g_dram[m], stage2[:]).then_inc(s_st, 16)

            load_w(W_GATE + 1, 0)
            load_w(W_GATE + 1, 1)
            with sp.Fori(W_GATE + 1, W_BRANCH) as t:
                load_w(t + 1, 0)
                store_gate(t - 1 - W_GATE)
                load_w(t + 1, 1)
            store_gate(N_GATE - 1)

            sp.wait_ge(s_mm, half_done(W_BRANCH - 1, 1))
            sp.wait_ge(s_ev, 3 * W_BRANCH)
            settle(sp)
            sp.dma_start(wup[:], w_up).then_inc(s_wup, 16)
            sp.wait_ge(s_st, 16 * W_BRANCH)
            last = SEQ - WINDOW
            sp.dma_start(k_prompt, p_dram[T_K:T_K + 2, :, last:SEQ]).then_inc(s_kv, 16)
            sp.dma_start(v_prompt, p_dram[T_V:T_V + 2, :, last:SEQ]).then_inc(s_kv, 16)
            sp.dma_start(k_sample[:, :, 0:WINDOW - DEC], kT_cache[:, :, DEC:WINDOW]).then_inc(s_kv, 16)
            sp.dma_start(k_sample[:, :, WINDOW - DEC:WINDOW], p_dram[T_K:T_K + 2, :, SEQ:TOKENS]).then_inc(s_kv, 16)
            sp.dma_start(v_old, v_cache[DEC:WINDOW, :]).then_inc(s_kv, 16)
            sp.dma_start(v_new, p_dram[T_V:T_V + 2, :, SEQ:TOKENS]).then_inc(s_kv, 16)
            sp.wait_ge(s_la, 2)
            sp.dma_start(la_dram[0:N_IT - 1].rearrange("n p d -> p n d"), lmin[:, 0:N_IT - 1]).then_inc(s_last, 16)
            sp.dma_start(la_dram[N_IT - 1, 0:DEC], lmin[0:DEC, N_IT - 1]).then_inc(s_last, 16)
            sp.wait_ge(s_last, 32)

            sp.dma_start(dist[:], dist_c).then_inc(s_bc, 16)
            sp.dma_start(decay[:], decay_c).then_inc(s_bc, 16)
            sp.dma_start(mask[:], mask_c.rearrange("p (l t) -> p l t", l=7)).then_inc(s_bc, 16)

            def tokens(it, n):
                return slice(it * P, it * P + n) if isinstance(it, int) else bass.ds(it * P, n)

            def load_attention(it, nq=P, first=False, sample=False):
                ge(sp, s_sc, 8 * it)
                ge(sp, s_pt, N_T * (it - 1) + 1)
                ge(sp, s_zs, it)
                settle(sp)
                sp.dma_start(qa[:, :, 0:nq], p_dram[T_Q:T_K, :, tokens(it, nq)].rearrange("t p n -> p t n")).then_inc(s_qa, 16)
                keys = p_dram[T_K:T_GQ].rearrange("t p n -> p t n")
                if first:
                    sp.dma_start(kw[:, :, P:2 * P], keys[:, :, 0:P]).then_inc(s_kw, 16)
                elif sample:
                    sp.dma_start(kw[:, :, 0:P], kT_cache.rearrange("t p n -> p t n")).then_inc(s_kw, 16)
                    sp.dma_start(kw[:, :, P:P + nq], keys[:, :, tokens(it, nq)]).then_inc(s_kw, 16)
                    sp.wait_ge(s_pv, 4 * it)
                    settle(sp)
                    sp.dma_start(v_prev[:], v_cache).then_inc(s_vp, 16)
                else:
                    sp.dma_start(kw[:], keys[:, :, bass.ds((it - 1) * P, 2 * P)]).then_inc(s_kw, 16)

            def load_gla(it, nq=P, nch=2):
                ge(sp, s_og, 2 * it)
                settle(sp)
                sp.dma_start(gl[:, :, 0:nq], p_dram[T_GQ:N_P, :, tokens(it, nq)].rearrange("t p n -> p t n")).then_inc(s_gl, 16)
                sp.dma_start(lac[0:nq], la_dram[it, 0:nq]).then_inc(s_lac, 16)

            def store_attention(it, nq=P):
                sp.wait_ge(s_oa, 2 * it + 2)
                settle(sp)
                sp.dma_start(o_dram[0:HK, :, tokens(it, nq)].rearrange("t p n -> p t n"), oa[:, :, 0:nq]).then_inc(s_oast, 16)

            def store_gla(it, nq=P):
                sp.wait_ge(s_og, 2 * it + 2)
                settle(sp)
                sp.dma_start(o_dram[HK:KT, :, tokens(it, nq)].rearrange("t p n -> p t n"),
                             og[:, :, :, 0:nq].rearrange("p a b n -> p (a b) n")).then_inc(s_ogst, 16)

            load_attention(0, first=True)
            load_gla(0)

            with sp.Fori(0, N_IT - 2) as it:
                load_attention(it + 1)
                store_attention(it)
                load_gla(it + 1)
                store_gla(it)
            it = N_IT - 1
            load_attention(it, DEC, sample=True)
            store_attention(it - 1)
            load_gla(it, DEC, 1)
            store_gla(it - 1)
            sp.wait_ge(s_su, 8 * it)
            settle(sp)
            sp.dma_start(state_prompt.rearrange("h d v -> d h v"), st[:, 0]).then_inc(s_sst, 16)
            sp.wait_ge(s_sst, 16)
            settle(sp)
            sp.dma_start(st[:, 0], state_in.rearrange("h d v -> d h v")).then_inc(s_sld, 16)
            store_attention(it, DEC)
            store_gla(it, DEC)
            sp.wait_ge(s_su, 8 * it + 4)
            settle(sp)
            sp.dma_start(state_sample.rearrange("h d v -> d h v"), st[:, 1]).then_inc(s_sst, 16)
            sp.wait_ge(s_sst, 32)

            sp.wait_ge(s_oast, 16 * N_IT)
            sp.wait_ge(s_ogst, 16 * N_IT)
            load_operand(o_dram.rearrange("k p t -> (k p) t"), br, BY_HALF, NB, False)

            def load_gate(m, i):
                ge(sp, (s_ya, s_yg)[i], 3 * m)
                settle(sp)
                sp.dma_start(gate[:, i], g_dram[m + i * N_OUT]).then_inc(s_g[i], 16)

            def store_merged(m):
                sp.wait_ge(s_yg, 3 * m + 3)
                settle(sp)
                sp.dma_start(m_dram[m], stage[:]).then_inc(s_mst, 16)

            load_gate(0, 0)
            load_gate(0, 1)
            with sp.Fori(0, N_OUT - 1) as m:
                load_w(m + W_BRANCH + 1, 0)
                load_gate(m + 1, 0)
                load_w(m + W_BRANCH + 1, 1)
                store_merged(m)
                load_gate(m + 1, 1)
            m = N_OUT - 1
            load_w(m + W_BRANCH + 1, 0)
            load_w(m + W_BRANCH + 1, 1)
            store_merged(m)

            sp.wait_ge(s_mst, 16 * N_OUT)
            load_operand(m_dram.rearrange("k p t -> (k p) t"), mr, BY_GROUP, 2 * NB, False)

            def load_x(g, n, k):
                a, w = GRP[g]
                ge(sp, s_fin, 2 * (n - 1) + 2)
                settle(sp)
                sp.dma_start(stage[:, 0:w], xT.rearrange("(k p) t -> k p t", p=P)[k, :, a:a + w]).then_inc(s_xo, 16)

            def store_y(g, n, k):
                a, w = GRP[g]
                sp.wait_ge(s_fin, 2 * n + 2)
                settle(sp)
                sp.dma_start(yT.rearrange("(k p) t -> k p t", p=P)[k, :, a:a + w], stage2[:, 0:w]).then_inc(s_y, 16)

            for g in range(3):
                base = W_OUT + g * KT

                def pair(i, last=False):
                    for r in range(2):
                        m = 2 * i + r
                        nxt = 0 if last and r == 1 else m + 1
                        if g > 0:
                            load_x(g - 1, (g - 1) * KT + m, m)
                        if not (last and r == 1 and g == 2):
                            load_w(base + m + 1, 0, W_OUT + nxt)
                            load_w(base + m + 1, 1, W_OUT + nxt)
                        if g > 0:
                            store_y(g - 1, (g - 1) * KT + m, m)

                pair(0)
                with sp.Fori(1, KT // 2 - 1) as i:
                    pair(i)
                pair(KT // 2 - 1, last=True)
            with sp.Fori(0, KT) as m:
                load_x(2, 2 * KT + m, m)
                store_y(2, 2 * KT + m, m)
            sp.wait_ge(s_kv, 16 * 6)
            sp.wait_ge(s_y, 16 * 3 * KT)

        @block.scalar
        def _(act):
            def hi_w(tile, h, freed):
                act.wait_ge(s_w[h], 16 * tile + 16)
                ge(act, s_mm, freed)
                act.activation(w_hi[:, h], w_raw[:, h], ACT.Copy).then_inc(s_whi, 1)

            def hi_tile(tile):
                hi_w(tile, 1, half_done(tile - 1, 1))
                hi_w(tile + 1, 0, half_done(tile, 0))

            def hi_piece(b, order, base, ring, out, scale, before=None):
                h, g, j = order[b]
                n, w = base + b, GRP[g][1]
                act.wait_ge(s_x[b % 2], 16 * (n // 2 + 1))
                if before:
                    before(b)
                for q in range(2):
                    k = h * HK + 2 * j + q
                    i = act.activation(out[g][:, k, 0:w], ring[:, b % 2, q, 0:w], ACT.Copy, scale=scale(k))
                i.then_inc(s_uhi, 1)

            act.wait_ge(s_const, 16 * 6)
            hi_w(0, 0, 0)
            act.wait_ge(s_cset, 2)
            act.activation(wlr[:, :, 0:RANK], wlr_raw[:], ACT.Copy).then_inc(s_lrhi, 1)
            for b in range(NB):
                hi_piece(b, BY_HALF, 0, xr, uh, lambda k: norm_sb[:, 0, k:k + 1])
                if b >= 2:
                    act.wait_ge(s_ssq, 2 * b - 1)
                w = GRP[BY_HALF[b][1]][1]
                act.activation(sqx[:, b % 2, :, 0:w], xr[:, b % 2, :, 0:w], ACT.Square).then_inc(s_sqx, 1)
                if b == NB // 2:
                    hi_w(0, 1, 0)
            hi_w(1, 0, half_done(0, 0))
            with act.Fori(1, N_P) as t:
                hi_tile(t)

            def gate_tanh(tile):
                m = tile - W_GATE
                ge(act, s_st, 16 * tile)
                for c, (a, w) in enumerate(GRP):
                    act.wait_ge(s_ev, 3 * tile + c + 1)
                    settle(act)
                    act.activation(stage2[:, a:a + w], stage[:, a:a + w], ACT.Tanh,
                                   bias=bg_half[:, bass.ds(m, 1)], scale=0.5).then_inc(s_th, 1)

            act.wait_ge(s_cset, 4)
            with act.Fori(W_GATE, W_BRANCH) as t:
                hi_tile(t)
                gate_tanh(t)

            for it in range(N_IT):
                nq = P if it < N_IT - 1 else DEC
                act.wait_ge(s_lmin, it + 1)
                act.activation(lexp[0:nq, it], bank[it % 2][0:nq, :], ACT.Abs).then_inc(s_labs, 1)
                act.wait_ge(s_labs, it + 1)
                act.activation(lexp[0:nq, it], lexp[0:nq, it], ACT.Exp, scale=-1.0).then_inc(s_lexp, 1)
            act.wait_ge(s_lexp, N_IT)
            act.activation(lexp[:, 0:N_IT - 1], lexp[:, 0:N_IT - 1], ACT.Ln, bias=1.0).then_inc(s_lln, 1)
            act.activation(lexp[0:DEC, N_IT - 1], lexp[0:DEC, N_IT - 1], ACT.Ln, bias=1.0).then_inc(s_lln, 1)

            def attend(it, nq=P, kts=(0, 1), nch=2):
                nk = (P, nq)
                lo, hi = kts[0] * P, P + nq
                tanh_gate(it, nq)
                act.wait_ge(s_pt, N_T * it + 1)
                if not isinstance(it, int):
                    ge(act, s_pv, 4 * it)
                    act.activation(v_prev[:], v_cur[:], ACT.Copy).then_inc(s_vsh, 1)
                    act.wait_ge(s_vsh, it)
                else:
                    ge(act, s_pv, 4 * it)
                act.activation(v_cur[0:nq], bank[2][0:nq, 0:256], ACT.Copy).then_inc(s_tev, 1)

                def exps(u):
                    act.wait_ge(s_snm, 8 * it + u + 1)
                    ge(act, s_pt, N_T * it + u if u >= 2 else N_T * it)
                    for i in range(2):
                        act.activation(pb[0:nq, u % 2, i, lo:hi], s8[0:nq, u % 2, i, lo:hi], ACT.Exp,
                                       bias=nm[0:nq, u % 2, i:i + 1], scale=HEAD_DIM ** -0.5,
                                       accum_out=rsum[0:nq, u % 2, i:i + 1])
                    act.activation(esink[0:nq, u % 2], snm[0:nq, u % 2], ACT.Exp).then_inc(s_ep, 1)

                def probs_out(u):
                    act.wait_ge(s_pt, N_T * it + 2 + u)
                    gi = u // 2
                    if gi >= 2:
                        act.wait_ge(s_pv, 4 * it + gi - 1)
                    for kt in kts:
                        i = act.activation(pT[0:nk[kt], gi % 2, kt, 2 * (u % 2):2 * (u % 2) + 2, 0:nq],
                                           bank[2][0:nk[kt], :].rearrange("p (k i q) -> p k i q", k=2, i=2)[:, kt, :, 0:nq],
                                           ACT.Copy)
                    i.then_inc(s_tev, 1)

                exps(0)
                for u in range(1, 8):
                    exps(u)
                    probs_out(u - 1)
                probs_out(7)
                for half in range(2):
                    act.wait_ge(s_pt, N_T * it + 10 + half)
                    act.activation(vg[0:nq, half * 512:half * 512 + 512], bank[2][0:nq, :], ACT.Copy).then_inc(s_tev, 1)

                def decay_exps(hh):
                    ge(act, s_su, 8 * it)
                    for c in range(nch):
                        act.wait_ge(s_e, 8 * it + nch * hh + c + 1)
                        act.activation(ex[:, hh, c], bank[c][:, :].rearrange("p (b t) -> p b t", t=CHUNK),
                                       ACT.Exp).then_inc(s_ex, 1)

                def keys_out(hh):
                    act.wait_ge(s_pt, N_T * it + 12 + hh)
                    act.activation(kt_tok[0:nq, hh], bank[2][0:nq, 0:GLA_DK], ACT.Copy).then_inc(s_tev, 1)

                decay_exps(0)
                decay_exps(1)
                keys_out(0)
                decay_exps(2)
                keys_out(1)
                decay_exps(3)
                keys_out(2)
                keys_out(3)
                act.activation(thg[:, :, 0:nq], gl[:, 16:24, 0:nq], ACT.Tanh, scale=0.5).then_inc(s_tg, 1)
                for c in range(nch):
                    act.wait_ge(s_o, 2 * it + c + 1)
                    ge(act, s_og, 2 * it)
                    ps = bank[3][:, :].rearrange("p (a b t) -> p a b t", a=GLA_HEADS, b=2)
                    act.activation(os_[:, :, :, c * CHUNK:(c + 1) * CHUNK], ps, ACT.Copy, scale=GLA_DK ** -0.5)
                    act.activation(sq[:, :, :, c * CHUNK:(c + 1) * CHUNK], ps, ACT.Square,
                                   scale=GLA_DK ** -0.5).then_inc(s_oev, 1)

            def tanh_gate(it, nq):
                act.wait_ge(s_qa, 16 * it + 16)
                ge(act, s_zs, it)
                act.activation(th[:, :, 0:nq], qa[:, 10:18, 0:nq], ACT.Tanh, scale=0.5).then_inc(s_tz, 1)

            attend(0, kts=(1,))
            with act.Fori(1, N_IT - 1) as it:
                attend(it)
            attend(N_IT - 1, DEC, nch=1)

            for b in range(NB):
                hi_piece(b, BY_HALF, NB, br, bh, lambda k: 1.0)
            with act.Fori(W_BRANCH, W_OUT - 1) as t:
                hi_tile(t)
            hi_w(W_OUT - 1, 1, half_done(W_OUT - 2, 1))

            hi_w(W_OUT, 0, half_done(W_OUT - 1, 0))
            for b in range(NB):
                hi_piece(b, BY_GROUP, 2 * NB, mr, mh, lambda k: 0.5,
                         before=lambda b: b == 0 and act.wait_ge(s_mm, half_done(W_OUT - 1, 1)))
                if b == 8:
                    hi_w(W_OUT, 1, half_done(W_OUT - 1, 1))
            for g in range(3):
                base = W_OUT + g * KT

                def pair(i, last=False):
                    for r in range(2):
                        m = 2 * i + r
                        tile = base + m
                        if not (g == 0 and r == 0 and isinstance(i, int) and i == 0):
                            hi_w(tile, 1, out_half_done(tile - 1, 1))
                        if not (last and r == 1 and g == 2):
                            hi_w(tile + 1, 0, out_half_done(tile, 0))
                        n = g * KT + m
                        act.wait_ge(s_mm, out_half_done(tile, 1))
                        settle(act)
                        act.activation(out_sb[g][:, bass.ds(m, 1), 0:GRP[g][1]], bank[r][:, 0:GRP[g][1]].unsqueeze(1),
                                       ACT.Copy).then_inc(s_oev2, 1)

                pair(0)
                with act.Fori(1, KT // 2 - 1) as i:
                    pair(i)
                pair(KT // 2 - 1, last=True)

        @block.gpsimd
        def _(pool):
            pool.memset(ssq[:], 0.0).then_inc(s_ssq, 1)
            pool.wait_ge(s_ssq, 1)
            for b, (h, g, j) in enumerate(BY_HALF):
                w = GRP[g][1]
                pool.wait_ge(s_sqx, b + 1)
                for q in range(2):
                    pool.tensor_tensor(ssq[:, g, 0:w], ssq[:, g, 0:w], sqx[:, b % 2, q, 0:w], ALU.add).then_inc(s_ssq, 1)
                    pool.wait_ge(s_ssq, 2 * b + q + 2)
            pool.memset(minus_half[:], -0.5).then_inc(s_pset, 1)
            pool.memset(mean[:], 1.0).then_inc(s_pset, 1)
            pool.wait_ge(s_pset, 2)

            def roots(n):
                pool.wait_ge(s_rst, 3 * n + 3)
                pool.tensor_tensor(root[:], mean[:], minus_half[:].to_broadcast([P, 3]), ALU.pow).then_inc(s_rsp, 1)

            def gla_roots(it, nq=P):
                pool.wait_ge(s_var, it + 1)
                ge(pool, s_gdg, it)
                pool.tensor_tensor(groot[0:nq], gmean[0:nq], minus_half[0:nq].to_broadcast([nq, GLA_HEADS]), ALU.pow).then_inc(s_gpw, 1)

            for n in range(3):
                roots(n)
            gla_roots(0)
            with pool.Fori(1, N_IT - 1) as it:
                gla_roots(it)
            gla_roots(N_IT - 1, DEC)
            for n in range(3, 6):
                roots(n)

        @block.vector
        def _(dve):
            def lo_w(tile, h):
                dve.wait_ge(s_whi, 2 * tile + h + 1)
                dve.tensor_tensor(w_lo[:, h], w_raw[:, h], w_hi[:, h].bitcast(f32), ALU.subtract).then_inc(s_wlo, 1)

            def lo_piece(b, order, base, ring, hi_t, out, scale):
                h, g, j = order[b]
                n, w = base + b, GRP[g][1]
                dve.wait_ge(s_uhi, n + 1)
                for q in range(2):
                    k = h * HK + 2 * j + q
                    i = dve.scalar_tensor_tensor(out=out[g][:, k, 0:w], in0=ring[:, b % 2, q, 0:w], scalar=scale(k),
                                                 in1=hi_t[g][:, k, 0:w].bitcast(f32), op0=ALU.mult, op1=ALU.subtract)
                i.then_inc(s_ulo, 1)

            dve.memset(ones[:], 1.0).then_inc(s_cset, 1)
            dve.memset(wlr[:].bitcast(f32), 0.0).then_inc(s_cset, 1)
            dve.memset(lr[2 * RANK:2 * RANK + 1, :], 1.0).then_inc(s_cset, 1)
            dve.wait_ge(s_const, 16 * 6)
            dve.tensor_scalar(bg_half[:], bg_sb[:], 0.5, None, ALU.mult).then_inc(s_cset, 1)
            dve.tensor_scalar(gn_half[:], gn_sb[:], 0.5, None, ALU.mult).then_inc(s_cset, 1)
            dve.tensor_scalar(nsink_sb[:], sink_sb[:], -1.0, None, ALU.mult).then_inc(s_cset, 1)
            lo_w(0, 0)
            dve.wait_ge(s_lrhi, 1)
            dve.tensor_tensor(wlr[:, :, RANK:2 * RANK], wlr_raw[:], wlr[:, :, 0:RANK].bitcast(f32), ALU.subtract).then_inc(s_lrlo, 1)
            for b in range(NB):
                lo_piece(b, BY_HALF, 0, xr, uh, ul, lambda k: norm_sb[:, 0, k:k + 1])
                if b == NB // 2:
                    lo_w(0, 1)
            def token_rstd(n, w, ps, diag, out):
                if n == 0:
                    dve.wait_ge(s_pset, 2)
                dve.wait_ge(s_ones, n + 1)
                for i, t, size in blocks(w):
                    dve.tensor_scalar(mean[0:size, i:i + 1], ps[0:size, i:i + 1], 1.0 / D_MODEL, EPS, ALU.mult, ALU.add).then_inc(s_rst, 1)
                dve.wait_ge(s_rsp, n + 1)
                for i, t, size in blocks(w):
                    dve.tensor_scalar(diag[0:size, i], ident[0:size], root[0:size, i:i + 1], None, ALU.mult).then_inc(s_dg, 1)
                dve.wait_ge(s_spread, n + 1)
                dve.tensor_copy(out, ps[:, 0:w]).then_inc(s_rstd, 1)

            for g, (a, w) in enumerate(GRP):
                token_rstd(g, w, bank[3 + g % 2], diag_x, rstd[:, g, 0:w])
                dve.wait_ge(s_rstd, g + 1)
                dve.tensor_tensor(lr[0:2 * RANK, a:a + w], bank[5 + g][0:2 * RANK, 0:w], rstd[0:2 * RANK, g, 0:w], ALU.mult).then_inc(s_lr, 1)

            def evacuate(tile):
                for c, (a, w) in enumerate(GRP):
                    dve.wait_ge(s_mm, 6 * tile + 4 + c)
                    dve.tensor_tensor(stage[:, a:a + w], bank[c][:, 0:w], rstd[:, c, 0:w], ALU.mult).then_inc(s_ev, 1)

            lo_w(1, 0)
            evacuate(0)
            with dve.Fori(1, N_P) as t:
                lo_w(t, 1)
                lo_w(t + 1, 0)
                dve.wait_ge(s_st, 16 * t)
                evacuate(t)

            def evacuate_gate(tile, first=False):
                for c, (a, w) in enumerate(GRP):
                    dve.wait_ge(s_mm, 6 * tile + 4 + c)
                    if not first:
                        dve.wait_ge(s_th, 3 * (tile - W_GATE) + c - 2)
                    dve.tensor_tensor(stage[:, a:a + w], bank[c][:, 0:w], rstd[:, c, 0:w], ALU.mult).then_inc(s_ev, 1)

            lo_w(W_GATE, 1)
            lo_w(W_GATE + 1, 0)
            dve.wait_ge(s_st, 16 * N_P)
            evacuate_gate(W_GATE, True)
            with dve.Fori(W_GATE + 1, W_BRANCH) as t:
                lo_w(t, 1)
                lo_w(t + 1, 0)
                evacuate_gate(t)

            for it in range(N_IT):
                nq = P if it < N_IT - 1 else DEC
                dve.wait_ge(s_lap, it + 1)
                dve.tensor_scalar(lmin[0:nq, it], bank[it % 2][0:nq, :], 0.0, 1.0 / TAU, ALU.min, ALU.mult).then_inc(s_lmin, 1)
            dve.wait_ge(s_lmin, N_IT)
            for i, (n, sl) in enumerate(((P, slice(0, N_IT - 1)), (DEC, slice(N_IT - 1, N_IT)))):
                dve.wait_ge(s_lln, i + 1)
                dve.scalar_tensor_tensor(out=lmin[0:n, sl], in0=lexp[0:n, sl], scalar=-1.0 / TAU, in1=lmin[0:n, sl],
                                         op0=ALU.mult, op1=ALU.add).then_inc(s_la, 1)

            dve.wait_ge(s_bc, 48)
            for h in range(HEADS):
                dve.tensor_scalar(bias[:, h], dist[:], -alibi_slope(h) * HEAD_DIM ** 0.5, None, ALU.mult).then_inc(s_bias, 1)
            dve.memset(st[:, 0], 0.0).then_inc(s_s0, 1)
            dve.wait_ge(s_bias, HEADS)

            def attend(it, nq=P, kts=(0, 1), nch=2):
                lo, hi = kts[0] * P, P + nq
                dve.wait_ge(s_tz, it + 1)
                dve.scalar_tensor_tensor(out=zs[:, :, 0:nq], in0=th[:, :, 0:nq], scalar=1.0, in1=qa[:, 10:18, 0:nq],
                                         op0=ALU.add, op1=ALU.mult).then_inc(s_zs, 1)

                def biased(u):
                    h0 = head0(u)
                    dve.wait_ge(s_sc, 8 * it + u + 1)
                    ge(dve, s_ep, 8 * it + u - 1)
                    settle(dve)
                    for i in range(2):
                        ins = dve.tensor_tensor_reduce(
                            out=s8[0:nq, u % 2, i, lo:hi], in0=bank[u % 2][0:nq, :].rearrange("p (i k) -> p i k", i=2)[:, i, lo:hi],
                            in1=bias[0:nq, h0 + i, lo:hi], scale=1.0, scalar=-3e38, op0=ALU.add, op1=ALU.max,
                            accum_out=m8[0:nq, u % 2, i:i + 1])
                    ins.then_inc(s_a, 1)
                    dve.wait_ge(s_a, 8 * it + u + 1)
                    dve.scalar_tensor_tensor(out=nm[0:nq, u % 2], in0=m8[0:nq, u % 2], scalar=-HEAD_DIM ** -0.5,
                                             in1=nsink_sb[0:nq, h0:h0 + 2], op0=ALU.mult, op1=ALU.min).then_inc(s_nm, 1)
                    dve.wait_ge(s_nm, 8 * it + u + 1)
                    dve.tensor_tensor(snm[0:nq, u % 2], nm[0:nq, u % 2], sink_sb[0:nq, h0:h0 + 2], ALU.add).then_inc(s_snm, 1)

                def normed(u):
                    dve.wait_ge(s_ep, 8 * it + u + 1)
                    dve.tensor_tensor(den[0:nq, u % 2], rsum[0:nq, u % 2], esink[0:nq, u % 2], ALU.add).then_inc(s_den, 1)
                    dve.wait_ge(s_den, 8 * it + u + 1)
                    dve.reciprocal(rden[0:nq, u % 2], den[0:nq, u % 2]).then_inc(s_rden, 1)
                    dve.wait_ge(s_rden, 8 * it + u + 1)
                    for i in range(2):
                        ins = dve.tensor_scalar(pb[0:nq, u % 2, i, lo:hi], pb[0:nq, u % 2, i, lo:hi],
                                                rden[0:nq, u % 2, i:i + 1], None, ALU.mult)
                    ins.then_inc(s_pr, 1)

                def gated(tt):
                    dve.wait_ge(s_pv, 4 * it + 2 * tt + 2)
                    ge(dve, s_oast, 16 * it)
                    dve.scalar_tensor_tensor(out=oa[:, 4 * tt:4 * tt + 4, 0:nq],
                                             in0=bank[3][:, :].rearrange("p (j q) -> p j q", j=GROUP)[:, :, 0:nq],
                                             scalar=0.5, in1=zs[:, 4 * tt:4 * tt + 4, 0:nq],
                                             op0=ALU.mult, op1=ALU.mult).then_inc(s_oa, 1)

                dve.wait_ge(s_zs, it + 1)
                biased(0)
                for u in range(1, 8):
                    biased(u)
                    normed(u - 1)
                    if u == 5:
                        gated(0)
                normed(7)

                def decayed(hh):
                    dve.wait_ge(s_ex, 8 * it + nch * (hh + 1))
                    ge(dve, s_pt, N_T * it + 10 + hh if hh >= 2 else N_T * it)
                    ge(dve, s_o, 2 * it)
                    if hh == 0:
                        dve.wait_ge(s_gl, 16 * it + 16)
                    for t, dst, e0, nb in ((0, qe[:, hh], 0, 7), (4, ke[:, hh % 2], 1, 6)):
                        src = gl[:, t + hh, 0:nq].rearrange("p (c t) -> p c t", t=CHUNK)
                        dve.tensor_tensor(dst[:, 0:nch], ex[:, hh, 0:nch, e0:e0 + nb, :],
                                          src.unsqueeze(2).to_broadcast([P, nch, nb, CHUNK]), ALU.mult)
                    ins = dve.tensor_tensor(kend[:, hh % 2, 0:nch], ex[:, hh, 0:nch, 7, :], src, ALU.mult)
                    ins.then_inc(s_qk, 1)

                def masked(hh):
                    dve.wait_ge(s_gs, 4 * it + hh + 1)
                    ge(dve, s_gr, 4 * it + hh)
                    dve.tensor_tensor(tm[0:nq], bank[4][0:nq, 0:7 * CHUNK].rearrange("p (l t) -> p l t", l=7),
                                      mask[0:nq], ALU.mult).then_inc(s_gm, 1)
                    dve.wait_ge(s_gm, 4 * it + hh + 1)
                    dve.tensor_reduce(gsc[0:nq, hh], tm[0:nq].rearrange("p l t -> p t l"), AX.X, ALU.add).then_inc(s_gr, 1)

                decayed(0)
                decayed(1)
                gated(1)
                masked(0)
                decayed(2)
                masked(1)
                decayed(3)
                masked(2)
                masked(3)
                dve.wait_ge(s_tg, it + 1)
                dve.scalar_tensor_tensor(out=zg2[:, :, 0:nq], in0=thg[:, :, 0:nq], scalar=1.0, in1=gl[:, 16:24, 0:nq],
                                         op0=ALU.add, op1=ALU.mult).then_inc(s_z2, 1)
                if isinstance(it, int) and it == N_IT - 1:
                    dve.wait_ge(s_sld, 16)
                for c in range(nch):
                    for hh in range(GLA_HEADS):
                        dve.wait_ge(s_ds, 4 * it + 2 * c + hh // 2 + 1)
                        ge(dve, s_o, 2 * it + c)
                        if c == 1 or not isinstance(it, int) or it == 0:
                            ge(dve, s_su, 8 * it + 4 * (c - 1) + hh + 1)
                        if isinstance(it, int) and it == 0 and c == 0:
                            dve.wait_ge(s_s0, 1)
                        dve.scalar_tensor_tensor(
                            out=st[:, 1 - c, hh], in0=st[:, c, hh], scalar=ex[:, hh, c, 0, CHUNK - 1:CHUNK],
                            in1=bank[(5, 4)[hh // 2]][:, :].rearrange("p (i v) -> p i v", i=2)[:, hh % 2],
                            op0=ALU.mult, op1=ALU.add).then_inc(s_su, 1)
                dve.wait_ge(s_rm, it + 1)
                ge(dve, s_gpw, it)
                dve.tensor_scalar(gmean[0:nq], bank[0][0:nq, 0:GLA_HEADS], 1.0 / GLA_DV, EPS, ALU.mult, ALU.add).then_inc(s_var, 1)
                dve.wait_ge(s_gpw, it + 1)
                ge(dve, s_rb, it)
                for hh in range(GLA_HEADS):
                    ins = dve.tensor_scalar(gdiag[0:nq, hh], ident[0:nq], groot[0:nq, hh:hh + 1], None, ALU.mult)
                ins.then_inc(s_gdg, 1)
                dve.wait_ge(s_rb, it + 1)
                ps = bank[1][:, :].rearrange("p (a q) -> p a q", a=GLA_HEADS)[:, :, 0:nq]
                dve.tensor_tensor(t1[:, :, :, 0:nq], os_[:, :, :, 0:nq],
                                  ps.unsqueeze(2).to_broadcast([P, GLA_HEADS, 2, nq]), ALU.mult).then_inc(s_t1, 1)
                dve.wait_ge(s_t1, it + 1)
                dve.wait_ge(s_z2, it + 1)
                ge(dve, s_ogst, 16 * it)
                for vh in range(2):
                    dve.scalar_tensor_tensor(out=og[:, :, vh, 0:nq],
                                             in0=zg2[:, :, 0:nq].rearrange("p (a b) q -> p a b q", b=2)[:, :, vh],
                                             scalar=gn_half[:, vh:vh + 1], in1=t1[:, :, vh, 0:nq],
                                             op0=ALU.mult, op1=ALU.mult).then_inc(s_og, 1)

            attend(0, kts=(1,))
            with dve.Fori(1, N_IT - 1) as it:
                attend(it)
            attend(N_IT - 1, DEC, nch=1)

            for b in range(NB):
                lo_piece(b, BY_HALF, NB, br, bh, bl, lambda k: 1.0)

            def merge(m):
                tile = m + W_BRANCH
                dve.wait_ge(s_g[0], 16 * m + 16)
                for c, (a, w) in enumerate(GRP):
                    dve.wait_ge(s_mm, 6 * tile + 1 + c)
                    ge(dve, s_yg, 3 * m)
                    dve.scalar_tensor_tensor(out=ya[:, a:a + w], in0=gate[:, 0, a:a + w], scalar=1.0, in1=bank[c][:, 0:w],
                                             op0=ALU.add, op1=ALU.mult).then_inc(s_ya, 1)
                lo_w(tile + 1, 0)
                dve.wait_ge(s_g[1], 16 * m + 16)
                ge(dve, s_mst, 16 * m)
                for c, (a, w) in enumerate(GRP):
                    dve.wait_ge(s_mm, 6 * tile + 4 + c)
                    dve.scalar_tensor_tensor(out=stage2[:, a:a + w], in0=gate[:, 1, a:a + w], scalar=1.0,
                                             in1=bank[3 + c][:, 0:w], op0=ALU.add, op1=ALU.mult).then_inc(s_y2, 1)
                    dve.wait_ge(s_y2, 3 * m + c + 1)
                    dve.wait_ge(s_ya, 3 * m + c + 1)
                    dve.tensor_tensor(stage[:, a:a + w], ya[:, a:a + w], stage2[:, a:a + w], ALU.add).then_inc(s_yg, 1)

            lo_w(W_BRANCH, 1)
            merge(0)
            lo_w(W_BRANCH + 1, 1)
            with dve.Fori(1, N_OUT - 1) as m:
                merge(m)
                lo_w(m + W_BRANCH + 1, 1)
            merge(N_OUT - 1)

            for b in range(NB):
                lo_piece(b, BY_GROUP, 2 * NB, mr, mh, ml, lambda k: 0.5)
                if b == 8:
                    lo_w(W_OUT, 1)

            def finish(g, k, n):
                w = GRP[g][1]
                ge(dve, s_y, 16 * n)
                dve.scalar_tensor_tensor(out=stage2[:, 0:w], in0=out_sb[g][:, bass.ds(k, 1), 0:w].squeeze(1) if not isinstance(k, int) else out_sb[g][:, k, 0:w],
                                         scalar=norm_sb[:, 1, bass.ds(k, 1)], in1=rso[:, 0:w],
                                         op0=ALU.mult, op1=ALU.mult).then_inc(s_fin, 1)
                dve.wait_ge(s_fin, 2 * n + 1)
                dve.wait_ge(s_xo, 16 * n + 16)
                dve.tensor_tensor(stage2[:, 0:w], stage2[:, 0:w], stage[:, 0:w], ALU.add).then_inc(s_fin, 1)

            for g in range(3):
                base = W_OUT + g * KT
                w = GRP[g][1]
                if g:
                    dve.wait_ge(s_ones, 3 + g)
                dve.memset(ssqo[:], 0.0).then_inc(s_ssz, 1)
                dve.wait_ge(s_ssz, g + 1)

                def pair(i, last=False):
                    for r in range(2):
                        m = 2 * i + r
                        tile = base + m
                        n = g * KT + m
                        if not (g == 0 and r == 0 and isinstance(i, int) and i == 0):
                            lo_w(tile, 1)
                        if not (last and r == 1 and g == 2):
                            lo_w(tile + 1, 0)
                        if g > 0:
                            finish(g - 1, m, (g - 1) * KT + m)
                        dve.wait_ge(s_oev2, n + 1)
                        src = out_sb[g][:, bass.ds(m, 1), 0:w]
                        dve.tensor_tensor(sqo[:, 0:w].unsqueeze(1), src, src, ALU.mult).then_inc(s_sqo, 1)
                        dve.wait_ge(s_sqo, 2 * n + 1)
                        dve.tensor_tensor(ssqo[:, 0:w], ssqo[:, 0:w], sqo[:, 0:w], ALU.add).then_inc(s_sqo, 1)
                        dve.wait_ge(s_sqo, 2 * n + 2)

                pair(0)
                with dve.Fori(1, KT // 2 - 1) as i:
                    pair(i)
                pair(KT // 2 - 1, last=True)
                token_rstd(3 + g, w, bank[2], diag_m, rso[:, 0:w])
                dve.wait_ge(s_rstd, 4 + g)
            with dve.Fori(0, KT) as k:
                finish(2, k, 2 * KT + k)

        @block.tensor
        def _(pe):
            def products(out, h, hi_t, lo_t, g, start, stop):
                w = GRP[g][1]
                for k in range(HK):
                    for j, (wt, ut) in enumerate(((w_hi, hi_t), (w_hi, lo_t), (w_lo, hi_t))):
                        ins = pe.matmul(out[:, 0:w], wt[:, h, k, :], ut[g][:, h * HK + k, 0:w],
                                        start=start and k == 0 and j == 0, stop=stop and k == HK - 1 and j == 2)
                ins.then_inc(s_mm, 1)

            pe.wait_ge(s_cset, 6)
            pe.wait_ge(s_lrlo, 1)
            for h in range(2):
                pe.wait_ge(s_wlo, h + 1)
                for g in range(3):
                    pe.wait_ge(s_ulo, 4 * (3 * h + g) + 4)
                    w = GRP[g][1]
                    for k in range(HK):
                        for j, ut in enumerate((uh, ul)):
                            ins = pe.matmul(bank[5 + g][:, 0:w], wlr[:, h * HK + k, :], ut[g][:, h * HK + k, 0:w],
                                            start=h == 0 and k == 0 and j == 0, stop=h == 1 and k == HK - 1 and j == 1)
                    ins.then_inc(s_lrp, 1)
                    products(bank[g], h, uh, ul, g, h == 0, h == 1)
            pe.wait_ge(s_ssq, 2 * NB + 1)
            def token_sums(n, w, ps, sums):
                for i, t, size in blocks(w):
                    ins = pe.matmul(ps[0:size, i:i + 1], sums[:, t:t + size], ones[:, 0:1], start=True, stop=True)
                ins.then_inc(s_ones, 1)

            def spread(n, w, ps, diag):
                pe.wait_ge(s_dg, 3 * n + 3)
                for i, t, size in blocks(w):
                    ins = pe.matmul(ps[:, t:t + size], ones[0:size, :], diag[0:size, i, 0:size], start=True, stop=True)
                ins.then_inc(s_spread, 1)

            for g, (a, w) in enumerate(GRP):
                if g == 2:
                    pe.wait_ge(s_rstd, 1)
                token_sums(g, w, bank[3 + g % 2], ssq[:, g])
                spread(g, w, bank[3 + g % 2], diag_x)

            def project(tile):
                for h in range(2):
                    pe.wait_ge(s_wlo, 2 * tile + h + 1)
                    for g in range(3):
                        if h == 0:
                            pe.wait_ge(s_ev, 3 * (tile - 1) + g + 1)
                        products(bank[g], h, uh, ul, g, h == 0, h == 1)

            with pe.Fori(1, W_BRANCH) as t:
                project(t)

            pe.wait_ge(s_wup, 16)
            pe.wait_ge(s_lr, 3)
            pe.wait_ge(s_ev, 3 * W_BRANCH)
            for it in range(N_IT):
                nq = P if it < N_IT - 1 else DEC
                if it >= 2:
                    pe.wait_ge(s_labs, it - 1)
                pe.matmul(bank[it % 2][0:nq, :], lr[:, it * P:it * P + nq], wup[:], start=True, stop=True).then_inc(s_lap, 1)
            pe.wait_ge(s_labs, N_IT)

            pe.wait_ge(s_bc, 48)

            def attend(it, nq=P, kts=(0, 1), nch=2):
                nk = (P, nq)
                pe.wait_ge(s_qa, 16 * it + 16)
                ge(pe, s_tev, N_T * it)
                for i in range(2):
                    ins = pe.transpose(bank[2][0:nq, i * P:(i + 1) * P], qa[:, T_V + i, 0:nq], ident[:])
                ins.then_inc(s_pt, 1)
                last = isinstance(it, int) and it == N_IT - 1
                pe.wait_ge(s_kw, 16 * it + (32 if last else 16))

                def scores(u):
                    tile, half = tiles(u)
                    if u >= 2:
                        pe.wait_ge(s_a, 8 * it + u - 1)
                    elif u == 0:
                        ge(pe, s_var, it)
                    else:
                        ge(pe, s_t1, it)
                    r = slice(half * HEAD_DIM, (half + 1) * HEAD_DIM)
                    c0 = kts[0] * P
                    for i in range(2):
                        ins = pe.matmul(bank[u % 2][0:nq, :].rearrange("p (i k) -> p i k", i=2)[:, i, c0:P + nq],
                                        qa[r, tile + i, 0:nq], kw[r, tile // 4, c0:P + nq], start=True, stop=True)
                    ins.then_inc(s_sc, 1)

                def transposed(u):
                    pe.wait_ge(s_pr, 8 * it + u + 1)
                    pe.wait_ge(s_tev, N_T * it + 1 + u)
                    dst = bank[2][:, :].rearrange("p (k i q) -> p k i q", k=2, i=2)
                    for kt in kts:
                        for i in range(2):
                            ins = pe.transpose(dst[0:nk[kt], kt, i, 0:nq], pb[0:nq, u % 2, i, kt * P:kt * P + nk[kt]], ident[0:nq, 0:nq])
                    ins.then_inc(s_pt, 1)

                def weighted(gi):
                    half, tt = gi % 2, gi // 2
                    g = 2 * tt + half
                    pe.wait_ge(s_tev, N_T * it + 3 + 2 * gi)
                    if gi == 0:
                        ge(pe, s_oev, 2 * it)
                        if last:
                            pe.wait_ge(s_vp, 16)
                    if gi == 2:
                        pe.wait_ge(s_oa, 2 * it + 1)
                    for kt in kts:
                        v = (v_prev, v_cur)[kt]
                        ins = pe.matmul(bank[3][half * HEAD_DIM:(half + 1) * HEAD_DIM, :].rearrange("p (j q) -> p j q", j=GROUP)[:, :, 0:nq],
                                        v[0:nk[kt], g * HEAD_DIM:(g + 1) * HEAD_DIM], pT[0:nk[kt], gi % 2, kt, :, 0:nq],
                                        start=kt == kts[0], stop=kt == kts[-1])
                    ins.then_inc(s_pv, 1)

                scores(0)
                scores(1)
                for u in range(8):
                    transposed(u)
                    if u < 6:
                        scores(u + 2)
                    if u % 2:
                        weighted(u // 2)

                pe.wait_ge(s_gl, 16 * it + 16)
                pe.wait_ge(s_lac, 16 * it + 16)
                for half in range(2):
                    pe.wait_ge(s_tev, N_T * it + 9 + half)
                    for i in range(4):
                        ins = pe.transpose(bank[2][0:nq, i * P:(i + 1) * P], gl[:, 8 + 4 * half + i, 0:nq], ident[:])
                    ins.then_inc(s_pt, 1)

                def decays(hh):
                    for c in range(nch):
                        if hh == 0:
                            pe.wait_ge(s_a, 8 * it + 7 + c)
                        else:
                            pe.wait_ge(s_ex, 8 * it + nch * (hh - 1) + c + 1)
                        r = slice(c * CHUNK, (c + 1) * CHUNK)
                        pe.matmul(bank[c][:, :], lac[r, hh * GLA_DK:(hh + 1) * GLA_DK], decay[r, :], start=True, stop=True).then_inc(s_e, 1)

                def gla_scores(hh):
                    pe.wait_ge(s_qk, 4 * it + hh + 1)
                    if hh:
                        pe.wait_ge(s_gm, 4 * it + hh)
                    else:
                        ge(pe, s_su, 8 * it)
                    for c in range(nch):
                        r = slice(c * CHUNK, (c + 1) * CHUNK)
                        for l in range(6):
                            pe.matmul(bank[4][r, l * CHUNK:(l + 1) * CHUNK], ke[:, hh % 2, c, l], qe[:, hh, c, l + 1], start=True, stop=True)
                        ins = pe.matmul(bank[4][r, 6 * CHUNK:7 * CHUNK], gl[:, 4 + hh, r], gl[:, hh, r], start=True, stop=True)
                    ins.then_inc(s_gs, 1)
                    pe.wait_ge(s_tev, N_T * it + 11 + hh)
                    pe.transpose(bank[2][0:nq, 0:GLA_DK], kend[:, hh % 2, 0:nch].rearrange("p c t -> p (c t)"), ident[:]).then_inc(s_pt, 1)

                decays(0)
                decays(1)
                gla_scores(0)
                decays(2)
                gla_scores(1)
                decays(3)
                gla_scores(2)
                gla_scores(3)
                pe.wait_ge(s_gr, 4 * it + 4)
                pe.wait_ge(s_tev, N_T * it + 15)
                if last:
                    pe.wait_ge(s_sld, 16)
                if isinstance(it, int) and it == 0:
                    pe.wait_ge(s_s0, 1)
                for c in range(nch):
                    r = slice(c * CHUNK, (c + 1) * CHUNK)
                    if c == 0:
                        pe.wait_ge(s_oa, 2 * it + 2)
                    else:
                        pe.wait_ge(s_oev, 2 * it + 1)
                    dst = bank[3][:, :].rearrange("p (a b t) -> p a b t", a=GLA_HEADS, b=2)
                    for hh in range(GLA_HEADS):
                        if c == 0:
                            if hh == 0 and not last:
                                ge(pe, s_su, 8 * it)
                        else:
                            pe.wait_ge(s_su, 8 * it + hh + 1)
                        for vh in range(2):
                            v0 = hh * GLA_DV + vh * P
                            pe.matmul(dst[:, hh, vh], vg[r, v0:v0 + P], gsc[r, hh], start=True, stop=False)
                            ins = pe.matmul(dst[:, hh, vh], st[:, c, hh, vh * P:(vh + 1) * P], qe[:, hh, c, 0], start=False, stop=True)
                    ins.then_inc(s_o, 1)
                    for pair in range(2):
                        if pair == 0:
                            ge(pe, s_su, 8 * it + 4 * c if c == 0 else 8 * it + 2)
                        elif c == 0:
                            pe.wait_ge(s_gm, 4 * it + 4)
                        else:
                            pe.wait_ge(s_su, 8 * it + 4)
                        for i in range(2):
                            hh = 2 * pair + i
                            ins = pe.matmul(bank[(5, 4)[pair]][:, i * GLA_DV:(i + 1) * GLA_DV], kt_tok[r, hh],
                                            vg[r, hh * GLA_DV:(hh + 1) * GLA_DV], start=True, stop=True)
                        ins.then_inc(s_ds, 1)
                pe.wait_ge(s_oev, 2 * it + nch)
                pe.wait_ge(s_ex, 8 * it + 4 * nch)
                for hh in range(GLA_HEADS):
                    for vh in range(2):
                        ins = pe.matmul(bank[0][0:nq, hh:hh + 1], sq[:, hh, vh, 0:nq], ones[:, 0:1], start=vh == 0, stop=vh == 1)
                ins.then_inc(s_rm, 1)
                pe.wait_ge(s_gdg, it + 1)
                ins = pe.matmul(bank[1][:, :].rearrange("p (a q) -> p a q", a=GLA_HEADS)[:, :, 0:nq], ones[0:nq, :], gdiag[0:nq, :, 0:nq],
                                start=True, stop=True).then_inc(s_rb, 1)

            attend(0, kts=(1,))
            with pe.Fori(1, N_IT - 1) as it:
                attend(it)
            attend(N_IT - 1, DEC, nch=1)

            pe.wait_ge(s_t1, N_IT)
            pe.wait_ge(s_su, 8 * (N_IT - 1) + 4)
            pe.wait_ge(s_oev, 2 * (N_IT - 1) + 1)
            def branch(m, first=False):
                tile = m + W_BRANCH
                for h in range(2):
                    pe.wait_ge(s_wlo, 2 * tile + h + 1)
                    for g in range(3):
                        if first:
                            pe.wait_ge(s_ulo, NB + 4 * (3 * h + g) + 4)
                        else:
                            pe.wait_ge((s_ya, s_yg)[h], 3 * (m - 1) + g + 1)
                        products(bank[3 * h + g], h, bh, bl, g, True, True)

            branch(0, True)
            with pe.Fori(1, N_OUT) as m:
                branch(m)

            pe.wait_ge(s_yg, 3 * N_OUT)
            for g in range(3):
                base = W_OUT + g * KT

                def pair(i, first=False):
                    for r in range(2):
                        m = 2 * i + r
                        tile = base + m
                        if not (first and g == 0):
                            pe.wait_ge(s_oev2, g * KT + m - 1)
                        for h in range(2):
                            pe.wait_ge(s_wlo, 2 * tile + h + 1)
                            if first and r == 0:
                                pe.wait_ge(s_ulo, 2 * NB + 8 * g + 4 * h + 4)
                            products(bank[r], h, mh, ml, g, h == 0, h == 1)

                pair(0, True)
                with pe.Fori(1, KT // 2) as i:
                    pair(i)
                w = GRP[g][1]
                pe.wait_ge(s_sqo, 2 * (g + 1) * KT)
                token_sums(3 + g, w, bank[2], ssqo)
                spread(3 + g, w, bank[2], diag_m)


def tiles(u):
    tt, half, pr = u // 4, (u // 2) % 2, u % 2
    return 4 * tt + 2 * pr, half


def head0(u):
    tile, half = tiles(u)
    return GROUP * (2 * (tile // 4) + half) + tile % 4


def constants():
    import numpy as np
    ident = np.eye(P, dtype=np.float32)
    q, k = np.arange(P)[:, None], np.arange(2 * P)[None, :]
    seen = (k // CHUNK - q // CHUNK >= 0) & (k // CHUNK - q // CHUNK <= WINDOW // CHUNK)
    dist = np.where(seen, np.abs(q + WINDOW - k), -MASKED).astype(np.float32)
    s, t = np.arange(CHUNK)[:, None], np.arange(CHUNK)[None, :]
    decay = [(s <= t)]
    mask = []
    for w in (32, 16, 8, 4, 2, 1):
        ref = t // (2 * w) * 2 * w + w - 1
        right = t // w % 2 == 1
        decay.append(np.where(right, (s > ref) & (s <= t), (s > t) & (s <= ref)))
        mask.append((s // (2 * w) == t // (2 * w)) & (s // w % 2 == 0) & right)
    decay.append(s > t)
    mask.append(s == t)
    decay = np.concatenate(decay, 1).astype(np.float32)
    mask = np.concatenate(mask, 1).astype(np.float32)
    return ident, dist, np.concatenate([decay, decay], 0), np.concatenate([mask, mask], 0)


def kernel(x_prompt, x_sample, cache_k, cache_v, state_gla, norm_pre, norm_post, w_in, b_gate,
           attn_sinks, w_forget_up, b_forget, gla_norm, w_branch_attn, w_branch_gla, w_out):
    import numpy as np
    import concourse.bacc as bacc
    from concourse.bass_utils import run_bass_kernel_spmd

    asc = np.ascontiguousarray
    x = np.concatenate([np.asarray(x_prompt)[0], np.asarray(x_sample)[0]], 0)
    w = np.asarray(w_in)[0]
    cut = np.cumsum([0, 1024, 256, 256, 1024, 512, 512, 1024, 1024, 16, 2048, 2048])
    part = {n: w[:, cut[i]:cut[i + 1]] for i, n in enumerate(("q", "k", "v", "za", "gq", "gk", "gv", "zg", "lr", "ga", "gg"))}
    order = np.arange(HEADS * HEAD_DIM).reshape(2, 2, GROUP, HEAD_DIM).transpose(0, 2, 1, 3).reshape(-1)
    cols = np.concatenate([part["q"][:, order], part["v"], part["za"][:, order], part["k"], part["gq"], part["gk"],
                           part["gv"], part["zg"], part["ga"], part["gg"]], 1)
    branch = np.concatenate([np.asarray(w_branch_attn)[0][order], np.asarray(w_branch_gla)[0]], 0)

    def tiled(a):
        return a.reshape(KT, P, -1, P).transpose(2, 1, 0, 3).reshape(-1, P, KT * P)

    w_tiles = np.concatenate([tiled(cols), tiled(branch), tiled(np.asarray(w_out)[0])], 0)
    up = np.asarray(w_forget_up)[0]
    ident, dist, decay, mask = constants()

    def per_partition(a):
        return asc(a.reshape(-1, P).T)

    ins = {
        "xT": asc(x.T),
        "w_tiles": w_tiles,
        "w_lr": asc(part["lr"].reshape(KT, P, RANK).transpose(1, 0, 2)),
        "w_up": asc(np.concatenate([up, up, np.asarray(b_forget)[0][None]], 0)),
        "norms": asc(np.stack([per_partition(np.asarray(norm_pre)[0]), per_partition(np.asarray(norm_post)[0])], 1)),
        "bgate": per_partition(np.asarray(b_gate)[0]),
        "sinks": asc(np.broadcast_to(np.asarray(attn_sinks)[0], (P, HEADS))),
        "gnorm": per_partition(np.asarray(gla_norm)[0]),
        "kT_cache": asc(np.asarray(cache_k)[0, 0].reshape(WINDOW, 2, P).transpose(1, 2, 0)),
        "v_cache": asc(np.asarray(cache_v)[0, 0].reshape(WINDOW, 2 * P)),
        "state_in": asc(np.asarray(state_gla)[0, 0]),
        "ident_c": ident, "dist_c": dist, "decay_c": decay, "mask_c": mask,
    }
    outs = {
        "yT": [D_MODEL, TOKENS], "k_prompt": [2, P, WINDOW], "v_prompt": [2, P, WINDOW],
        "state_prompt": [GLA_HEADS, GLA_DK, GLA_DV], "k_sample": [2, P, WINDOW],
        "v_old": [WINDOW - DEC, 2 * P], "v_new": [2, P, DEC], "state_sample": [GLA_HEADS, GLA_DK, GLA_DV],
    }
    nc = bacc.Bacc("TRN2", target_bir_lowering=False, num_devices=1)
    aps = {n: nc.dram_tensor("in_" + n, a.shape, mybir.dt.from_np(a.dtype), kind="ExternalInput").ap() for n, a in ins.items()}
    aps |= {n: nc.dram_tensor("out_" + n, shape, mybir.dt.float32, kind="ExternalOutput").ap() for n, shape in outs.items()}
    build_trunk(nc, **aps)
    r = run_bass_kernel_spmd(nc, [{"in_" + n: a for n, a in ins.items()}], core_ids=[0])
    got = {n: np.asarray(r.results[0]["out_" + n]) for n in outs}

    def rows(a):
        return asc(a.transpose(2, 0, 1).reshape(1, 1, a.shape[2], KV_HEADS, HEAD_DIM))

    y = got["yT"].T
    v_sample = np.concatenate([got["v_old"].reshape(1, 1, WINDOW - DEC, KV_HEADS, HEAD_DIM), rows(got["v_new"])], 2)
    return (asc(y[None, :SEQ]), asc(y[None, SEQ:]), rows(got["k_prompt"]), rows(got["v_prompt"]),
            got["state_prompt"][None, None], rows(got["k_sample"]), v_sample, got["state_sample"][None, None])
```

```python
import concourse.bass as bass
from concourse import mybir
from contextlib import ExitStack

D_MODEL, SEQ, DEC, WINDOW = 2048, 1024, 64, 128
TOKENS = SEQ + DEC
HEADS, KV_HEADS, HEAD_DIM = 16, 4, 64
GROUP = HEADS // KV_HEADS
GLA_HEADS, GLA_DK, GLA_DV, RANK = 4, 128, 256, 16
TAU, EPS = 16.0, 1e-6
CHUNK = 64
P = 128
KT = D_MODEL // P
HK = KT // 2
GA, GAW = 4, TOKENS // 4
GRP = [(0, 364), (364, 362), (726, 362)]
GW = 364
T_Q, T_V, T_ZA, T_K, T_GQ, T_GK, T_GV, T_ZG = 0, 8, 10, 18, 20, 24, 28, 36
X_SLOTS = 6
FORGET = [(0, 4), (4, 8), (8, 9)]
N_P = 44
N_GATE = 32
N_OUT = D_MODEL // P
ROW_GATE, ROW_BRANCH, ROW_OUT = N_P, N_P + N_GATE, N_P + N_GATE + N_OUT
PASS_GATE = N_P
PASS_BRANCH = PASS_GATE + GA * N_GATE
PASS_OUT = PASS_BRANCH + N_OUT
N_IT = SEQ // P + 1
BLOCKS = 8
LEVELS = BLOCKS - 2
N_T = 15
STEPS = 26
MASKED = -1e30
LATE = (18, 19, 20, 21, 25)


def alibi_slope(h):
    return 2.0 ** (-8.0 * (h + 1) / HEADS)


def weave(halves):
    return [([s for s in range(STEPS) if s * halves // STEPS == j], j) for j in range(halves)]


def build_trunk(nc, xT, w_tiles, w_lr, w_up, norms, bgate, sinks, gnorm, kT_cache, v_cache, state_in,
                ident_c, dist_c, decay_c, mask_c,
                yT, k_prompt, v_prompt, state_prompt, k_sample, v_old, v_new, state_sample):
    f32, f32r = mybir.dt.float32, mybir.dt.float32r
    ALU = mybir.AluOpType
    ACT = mybir.ActivationFunctionType
    AX = mybir.AxisListType

    p_dram = nc.dram_tensor("p_scratch", [N_P, P, TOKENS], f32).ap()
    g_dram = nc.dram_tensor("gate_scratch", [N_GATE, P, TOKENS], f32).ap()
    o_dram = nc.dram_tensor("o_scratch", [KT, P, TOKENS], f32).ap()
    m_dram = nc.dram_tensor("m_scratch", [KT, P, TOKENS], f32).ap()
    la_dram = nc.dram_tensor("la_scratch", [N_IT, P, GLA_HEADS * GLA_DK], f32).ap()

    with ExitStack() as ctx:
        def sb(name, shape, dt=f32, to=None):
            return (to or ctx).enter_context(nc.sbuf_tensor(name, shape, dt))

        def sem(name):
            return ctx.enter_context(nc.semaphore(name))

        w_raw = sb("w_raw", [P, 2, HK, P])
        w_hi = sb("w_hi", [P, 2, HK, P], f32r)
        w_lo = sb("w_lo", [P, 2, HK, P], f32r)
        stage = sb("stage", [P, TOKENS])
        stage2 = sb("stage2", [P, TOKENS])
        ring = sb("ring", [P, 2, 2, GW])
        rows = sb("rows", [P, 3 * GW])
        norm_sb = sb("norm_sb", [P, 2, KT])
        bg_sb = sb("bg_sb", [P, N_GATE])
        bg_half = sb("bg_half", [P, N_GATE])
        gn_sb = sb("gn_sb", [P, 2])
        gn_half = sb("gn_half", [P, 2])
        sink_sb = sb("sink_sb", [P, HEADS])
        nsink_sb = sb("nsink_sb", [P, HEADS])
        ident = sb("ident", [P, P])
        ones = sb("ones", [P, P])
        minus_half = sb("minus_half", [P, 1])
        mean = sb("mean", [P, N_IT])
        root = sb("root", [P, N_IT])

        with ExitStack() as ph:
            uh, ul = [], []
            for g in range(GA):
                uh.append(sb(f"uh{g}", [P, KT, GAW], f32r, ph))
                ul.append(sb(f"ul{g}", [P, KT, GAW], f32r, ph))
            sqx = sb("sqx", [P, 2, 2, GAW], f32, ph)
            ssq = sb("ssq", [P, GA, GAW], f32, ph)
            wlr = sb("wlr", [P, KT, P], f32r, ph)
            wlr_raw = sb("wlr_raw", [P, KT, RANK], f32, ph)
            lr = sb("lr", [P, TOKENS], f32, ph)
            wup = sb("wup", [P, GLA_HEADS * GLA_DK], f32, ph)
        with ExitStack() as ph:
            for g in range(GA):
                sb(f"uh_under{g}", [P, KT, GAW], f32r, ph)
                sb(f"ul_under{g}", [P, KT, GAW], f32r, ph)
            fmin = sb("fmin", [P, 4, GLA_HEADS * GLA_DK], f32, ph)
            sb("forget_gap", [P, 4 * GAW * 2 - 4 * GLA_HEADS * GLA_DK], f32, ph)
            fexp = sb("fexp", [P, 4, GLA_HEADS * GLA_DK], f32, ph)
        with ExitStack() as ph:
            sb("uh_kept", [P, KT, GAW], f32r, ph)
            sb("ul_kept", [P, KT, GAW], f32r, ph)
            bias = sb("bias", [P, HEADS, 2 * P], f32, ph)
            mask = sb("mask", [P, 7, CHUNK], f32, ph)
            decay = sb("decay", [P, 2, BLOCKS * CHUNK], f32r, ph)
            lac = sb("lac", [P, 512], f32, ph)
            lac_hi = sb("lac_hi", [P, 512], f32r, ph)
            lac_lo = sb("lac_lo", [P, 512], f32r, ph)
            th = sb("th", [P, 8, P], f32, ph)
            zs = sb("zs", [P, 8, P], f32, ph)
            v_prev = sb("v_prev", [P, KV_HEADS * HEAD_DIM], f32, ph)
            v_cur = sb("v_cur", [P, KV_HEADS * HEAD_DIM], f32, ph)
            s8 = sb("s8", [P, 2, 2, 2 * P], f32, ph)
            pb = sb("pb", [P, 2, 2, 2 * P], f32, ph)
            m8 = sb("m8", [P, 2, 2], f32, ph)
            nm = sb("nm", [P, 2, 2], f32, ph)
            snm = sb("snm", [P, 2, 2], f32, ph)
            rsum = sb("rsum", [P, 2, 2], f32, ph)
            esink = sb("esink", [P, 2, 2], f32, ph)
            den = sb("den", [P, 2, 2], f32, ph)
            rden = sb("rden", [P, 2, 2], f32, ph)
            pT = sb("pT", [P, 2, 2, GROUP, P], f32, ph)
            ob = sb("ob", [P, 8, P], f32, ph)
            vg = sb("vg", [P, GLA_HEADS * GLA_DV], f32, ph)
            ex = sb("ex", [P, 2, 2, BLOCKS, CHUNK], f32, ph)
            ebend = sb("ebend", [P, GLA_HEADS, 2], f32, ph)
            qb = sb("qb", [P, GLA_HEADS, 2, CHUNK], f32, ph)
            qe = sb("qe", [P, 2, 2, LEVELS, CHUNK], f32, ph)
            ke = sb("ke", [P, 2, 2, LEVELS, CHUNK], f32, ph)
            kend = sb("kend", [P, 2, 2, CHUNK], f32, ph)
            tm = sb("tm", [P, 7, CHUNK], f32, ph)
            gsc = sb("gsc", [P, GLA_HEADS, 2, CHUNK], f32, ph)
            kt_tok = sb("kt_tok", [P, 2, GLA_HEADS, GLA_DK], f32, ph)
            st = sb("st", [P, 2, GLA_HEADS, GLA_DV], f32, ph)
            gmean = sb("gmean", [P, GLA_HEADS], f32, ph)
            groot = sb("groot", [P, GLA_HEADS], f32, ph)
            gdiag = sb("gdiag", [P, GLA_HEADS, P], f32, ph)
            kw = sb("kw", [P, 2, 2, 2 * P], f32, ph)
            qa = sb("qa", [P, 18, P], f32, ph)
            gl = sb("gl", [P, 24, P], f32, ph)
        os_ = s8[:].rearrange("p u i k -> p (u i k)").rearrange("p (a b q) -> p a b q", a=GLA_HEADS, b=2)
        sq = pb[:].rearrange("p u i k -> p (u i k)").rearrange("p (a b q) -> p a b q", a=GLA_HEADS, b=2)
        ex_flat = ex[:].rearrange("p a b l t -> p (a b l t)")
        dist, decay_raw = ex_flat[:, 0:2 * P], ex_flat[:, 512:1536].rearrange("p (c n) -> p c n", c=2)
        with ExitStack() as ph:
            bh = [sb(f"bh{g}", [P, KT, GW], f32r, ph) for g in range(3)]
            bl = [sb(f"bl{g}", [P, KT, GW], f32r, ph) for g in range(3)]
            gate = sb("gate", [P, 2, TOKENS], f32, ph)
            ya = sb("ya", [P, TOKENS], f32, ph)
        with ExitStack() as ph:
            mh = [sb(f"mh{g}", [P, KT, GW], f32r, ph) for g in range(3)]
            ml = [sb(f"ml{g}", [P, KT, GW], f32r, ph) for g in range(3)]
            out_sb = [sb("out0", [P, KT, GW], f32, ph)]
        with ExitStack() as ph:
            out_sb.append(sb("out1", [P, KT, GW], f32, ph))
            out_sb.append(sb("out2", [P, KT, GW], f32, ph))
        rstd = rows[:, 0:TOKENS]
        rso, ssqo, sqo = (rows[:, i * GW:(i + 1) * GW] for i in range(3))
        diag = ring[:].rearrange("p a b t -> p (a b t)")[:, 0:N_IT * P].rearrange("p (n q) -> p n q", n=N_IT)
        x_slot = [ring[:, i, :, 0:GAW] for i in range(2)]
        for buf in (stage, stage2):
            x_slot += [buf[:, i * 2 * GAW:(i + 1) * 2 * GAW].rearrange("p (q t) -> p q t", q=2) for i in range(2)]

        def blocks(w):
            return [(n, n * P, min(P, w - n * P)) for n in range(-(-w // P))]

        bank = [ctx.enter_context(nc.psum_tensor(f"bank{i}", [P, 512], f32)) for i in range(8)]
        quarter = [(g, g * GAW) for g in range(GA)]

        s_const = sem("consts_loaded")
        s_cset = sem("consts_set")
        s_w = [sem("w_half0_loaded"), sem("w_half1_loaded")]
        s_whi = sem("w_hi_done")
        s_wlo = sem("w_lo_done")
        s_mp = sem("projection_products_done")
        s_mg = sem("gate_products_done")
        s_mb = sem("branch_products_done")
        s_mo = sem("output_products_done")
        s_x = [sem(f"x_slot{i}_loaded") for i in range(X_SLOTS)]
        s_xa = [sem("x_again_slot0_loaded"), sem("x_again_slot1_loaded")]
        s_norm = sem("norms_loaded")
        s_wlr = sem("lr_weights_loaded")
        s_uhi = sem("x_hi_done")
        s_ulo = sem("x_lo_done")
        s_y = [sem("branch_slot0_loaded"), sem("branch_slot1_loaded")]
        s_bhi = sem("branch_hi_done")
        s_blo = sem("branch_lo_done")
        s_z = [sem("merged_slot0_loaded"), sem("merged_slot1_loaded")]
        s_mhi = sem("merged_hi_done")
        s_mlo = sem("merged_lo_done")
        s_sqx = sem("x_squared")
        s_ssq = sem("square_sums_done")
        s_ones = sem("token_sums_done")
        s_rst = sem("mean_squares_ready")
        s_rsp = sem("roots_ready")
        s_dg = sem("root_diagonals_ready")
        s_spread = sem("roots_spread")
        s_rstd = sem("rstd_ready")
        s_pset = sem("gpsimd_constants_set")
        s_lrhi = sem("lr_weights_hi_done")
        s_lrlo = sem("lr_weights_lo_done")
        s_lrp = sem("lr_product_done")
        s_lrc = sem("lr_copied")
        s_lr = sem("lr_scaled")
        s_ev = sem("tile_chunks_evacuated")
        s_st = sem("tiles_stored")
        s_gz = sem("gate_units_scaled")
        s_th = sem("gate_units_tanh_done")
        s_gst = [sem("gate_slot0_stored"), sem("gate_slot1_stored")]
        s_pass = {e.engine: sem(f"{n}_waits_passed") for n, e in (("sync", nc.sync), ("scalar", nc.scalar), ("vector", nc.vector))}

        s_wup = sem("forget_weights_loaded")
        s_lap = sem("forget_product_done")
        s_lmin = sem("forget_min_done")
        s_labs = sem("forget_abs_done")
        s_lexp = sem("forget_exp_done")
        s_lln = sem("forget_log_done")
        s_la = sem("forget_logs_ready")
        s_last = sem("forget_logs_stored")
        s_bc = sem("attention_consts_loaded")
        s_bias = sem("alibi_tables_ready")
        s_dcy = sem("decay_matrix_ready")
        s_clr = sem("attention_buffers_cleared")
        s_kv = sem("cache_outputs_stored")

        s_qa = sem("attention_inputs_loaded")
        s_kw = sem("key_window_loaded")
        s_gl = sem("gla_inputs_loaded")
        s_lac = sem("forget_block_loaded")
        s_lch = sem("forget_block_hi_done")
        s_lcl = sem("forget_block_lo_done")
        s_vp = sem("cached_values_loaded")
        s_pt = sem("transposes_done")
        s_tev = sem("transposes_evacuated")
        s_sc = sem("scores_done")
        s_a = sem("scores_biased")
        s_nm = sem("negated_maxima_ready")
        s_snm = sem("sink_minus_max_ready")
        s_ep = sem("exponentials_done")
        s_den = sem("denominators_ready")
        s_rden = sem("reciprocals_ready")
        s_pr = sem("probabilities_ready")
        s_pv = sem("weighted_values_done")
        s_tz = sem("attention_gate_tanh")
        s_zs = sem("attention_gate_silu")
        s_oa = sem("attention_output_ready")
        s_oast = sem("attention_output_stored")
        s_e = sem("decay_sums_done")
        s_ex = sem("decay_exps_done")
        s_qk = sem("decayed_qk_ready")
        s_gs = sem("gla_scores_done")
        s_gm = sem("gla_scores_masked")
        s_gr = sem("gla_scores_ready")
        s_o = sem("gla_output_products_done")
        s_oev = sem("gla_output_evacuated")
        s_ds = sem("state_product_done")
        s_su = sem("state_updated")
        s_rm = sem("gla_square_sums_done")
        s_var = sem("gla_mean_squares_ready")
        s_gpw = sem("gla_roots_ready")
        s_gdg = sem("gla_root_diagonals_ready")
        s_rb = sem("gla_roots_spread")
        s_t1 = sem("gla_output_scaled")
        s_z2 = sem("gla_gate_silu")
        s_tg = sem("gla_gate_tanh")
        s_og = sem("gla_output_ready")
        s_ogst = sem("gla_output_stored")
        s_vsh = sem("values_shifted")
        s_sst = sem("state_stored")
        s_sld = sem("state_loaded")

        s_g = [sem("gate_a_loaded"), sem("gate_b_loaded")]
        s_ya = sem("attention_branch_weighted")
        s_y2 = sem("gla_branch_weighted")
        s_yg = sem("branches_merged")
        s_mst = sem("merged_stored")
        s_oev2 = sem("output_tiles_evacuated")
        s_ssz = sem("square_sums_cleared")
        s_sqo = sem("output_squares_summed")
        s_xo = sem("residual_loaded")
        s_fin = sem("output_steps")
        s_yst = sem("output_stored")

        def ge(eng, s, value):
            if not isinstance(value, int) or value > 0:
                eng.wait_ge(s, value)

        def settle(eng):
            eng.sem_inc(s_pass[eng.engine], 1)

        X_ORDER = [(h, g, j) for h in range(2) for g in range(GA) for j in range(HK // 2)]
        B_ORDER = [(h, g, j) for h in range(2) for g in range(3) for j in range(HK // 2)]
        NX, NB = len(X_ORDER), len(B_ORDER)
        X_AGAIN = KT // 2

        def w_src(row, h):
            return w_tiles[row, :, h * HK * P:(h + 1) * HK * P].rearrange("p (k c) -> p k c", c=P)

        def row_of(p):
            if p < PASS_GATE:
                return p
            if p < PASS_BRANCH:
                return ROW_GATE + (p - PASS_GATE) % N_GATE
            if p < PASS_OUT:
                return ROW_BRANCH + p - PASS_BRANCH
            return ROW_OUT + (p - PASS_OUT) % N_OUT

        def sequence(eng, attend):
            half = N_GATE // 2
            attend(0, 0, 0, half)
            attend(1, 0, half, half, again=1)
            with eng.Fori(1, GA - 1) as p:
                attend(2 * p, p, 0, half, fresh=True)
                attend(2 * p + 1, p, half, half, again=p + 1)
            attend(N_IT - 3, GA - 1, 0, 12, fresh=True)
            attend(N_IT - 2, GA - 1, 12, 12)
            attend(N_IT - 1, GA - 1, 24, 8, nxt=False)

        block = ctx.enter_context(nc.Block())

        @block.sync
        def _(sp):
            def load_w(p, h, row):
                ge(sp, s_wlo, 2 * (p - 1) + h + 1)
                if not isinstance(p, int):
                    settle(sp)
                sp.dma_start(w_raw[:, h], w_src(row, h)).then_inc(s_w[h], 16)

            def load_piece(view, k, a, w, n, sems, split):
                slot = k // 2 % 2
                ge(sp, split, n - 1)
                settle(sp)
                sp.dma_start(ring[:, slot, :, 0:w], view[:, k:k + 2, a]).then_inc(sems[slot], 16)

            x_view = xT.rearrange("(k p) t -> p k t", p=P)

            def columns(a, w):
                return slice(a, a + w) if isinstance(a, int) else bass.ds(a, w)

            sp.dma_start(norm_sb[:], norms).then_inc(s_norm, 16)
            sp.dma_start(wlr_raw[:], w_lr).then_inc(s_wlr, 16)
            for n, (h, g, j) in enumerate(X_ORDER):
                k = h * HK + 2 * j
                ge(sp, s_ulo, n + 1 - X_SLOTS)
                ge(sp, s_sqx, n + 1 - X_SLOTS)
                sp.dma_start(x_slot[n % X_SLOTS], x_view[:, k:k + 2, g * GAW:(g + 1) * GAW]).then_inc(s_x[n % X_SLOTS], 16)
                if n == 0:
                    load_w(0, 0, 0)
                if n == X_SLOTS:
                    load_w(0, 1, 0)
                    for dst, src in ((bg_sb, bgate), (gn_sb, gnorm), (sink_sb, sinks), (ident, ident_c)):
                        sp.dma_start(dst[:], src).then_inc(s_const, 16)
            load_w(1, 0, 1)
            sp.dma_start(wup[:], w_up).then_inc(s_wup, 16)

            def store_p(tile):
                sp.wait_ge(s_ev, GA * tile + GA)
                sp.dma_start(p_dram[tile], stage[:]).then_inc(s_st, 16)

            def store_forget(n):
                a, b = FORGET[n]
                nq = P if b < N_IT else DEC
                sp.wait_ge(s_la, n + 1)
                sp.dma_start(la_dram[a:b, 0:nq].rearrange("i p n -> p i n"), fmin[0:nq, 0:b - a]).then_inc(s_last, 16)

            load_w(1, 1, 1)
            load_w(2, 0, 2)
            store_p(0)
            for t in range(1, 1 + len(FORGET)):
                load_w(t + 1, 1, t + 1)
                store_forget(t - 1)
                load_w(t + 2, 0, t + 2)
                store_p(t)
            with sp.Fori(1 + len(FORGET), N_P) as t:
                load_w(t + 1, 1, t + 1)
                load_w(t + 2, 0, t + 2)
                store_p(t)

            def tokens(it, n):
                return slice(it * P, it * P + n) if isinstance(it, int) else bass.ds(it * P, n)

            def load_attention(it, nq=P):
                ge(sp, s_sc, 8 * it)
                ge(sp, s_zs, it)
                settle(sp)
                sp.dma_start(qa[:, :, 0:nq], p_dram[T_Q:T_K, :, tokens(it, nq)].rearrange("t p n -> p t n")).then_inc(s_qa, 16)
                keys = p_dram[T_K:T_GQ].rearrange("t p n -> p t n")
                cached = kT_cache.rearrange("t p n -> p t n")
                for half in range(2):
                    r = slice(half * HEAD_DIM, (half + 1) * HEAD_DIM)
                    if isinstance(it, int) and it == 0:
                        sp.wait_ge(s_clr, 1)
                        sp.dma_start(kw[r, half, :, P:2 * P], keys[r, :, 0:P]).then_inc(s_kw, 16)
                    elif isinstance(it, int) and it == N_IT - 1:
                        sp.dma_start(kw[r, half, :, 0:P], cached[r]).then_inc(s_kw, 16)
                        sp.dma_start(kw[r, half, :, P:P + nq], keys[r, :, tokens(it, nq)]).then_inc(s_kw, 16)
                    else:
                        sp.dma_start(kw[r, half], keys[r, :, bass.ds((it - 1) * P, 2 * P)]).then_inc(s_kw, 16)

            def load_gla(it, nq=P):
                ge(sp, s_og, 2 * it)
                settle(sp)
                sp.dma_start(gl[:, :, 0:nq], p_dram[T_GQ:N_P, :, tokens(it, nq)].rearrange("t p n -> p t n")).then_inc(s_gl, 16)
                sp.dma_start(lac[0:nq], la_dram[it, 0:nq]).then_inc(s_lac, 16)

            def store_attention(it, nq=P):
                sp.wait_ge(s_oa, 2 * it + 2)
                settle(sp)
                sp.dma_start(o_dram[0:HK, :, tokens(it, nq)].rearrange("t p n -> p t n"), ob[:, :, 0:nq]).then_inc(s_oast, 16)

            def store_gla(it, nq=P):
                sp.wait_ge(s_og, 2 * it + 2)
                settle(sp)
                sp.dma_start(o_dram[HK:KT, :, tokens(it, nq)].rearrange("t p n -> p t n"), ob[:, :, 0:nq]).then_inc(s_ogst, 16)

            sp.wait_ge(s_st, 16 * T_GQ)
            sp.wait_ge(s_lr, 1)
            sp.wait_ge(s_last, 16 * len(FORGET))
            load_attention(0)
            sp.wait_ge(s_mp, 2 * GA * N_P)
            for dst, src in ((dist, dist_c), (decay_raw, decay_c.rearrange("p (c n) -> p c n", c=2)), (mask[:], mask_c.rearrange("p (l t) -> p l t", l=7))):
                sp.dma_start(dst, src).then_inc(s_bc, 16)
            sp.wait_ge(s_st, 16 * N_P)
            load_gla(0)
            recent = SEQ - WINDOW
            for dst, src in ((k_prompt, p_dram[T_K:T_K + 2, :, recent:SEQ]), (v_prompt, p_dram[T_V:T_V + 2, :, recent:SEQ]),
                             (k_sample[:, :, 0:WINDOW - DEC], kT_cache[:, :, DEC:WINDOW]),
                             (k_sample[:, :, WINDOW - DEC:WINDOW], p_dram[T_K:T_K + 2, :, SEQ:TOKENS]),
                             (v_old, v_cache[DEC:WINDOW, :]), (v_new, p_dram[T_V:T_V + 2, :, SEQ:TOKENS])):
                sp.dma_start(dst, src).then_inc(s_kv, 16)

            def store_gate(p, m):
                ge(sp, s_th, N_GATE * p + m + 1)
                settle(sp)
                slot = m % 2
                sp.dma_start(g_dram[m, :, columns(p * GAW, GAW)], stage2[:, slot * GAW:(slot + 1) * GAW]).then_inc(s_gst[slot], 16)

            def remake(p, pieces):
                for j in pieces:
                    load_piece(x_view, 2 * j, columns(p * GAW, GAW), GAW, NX + X_AGAIN * (p - 1) + j, s_xa, s_ulo)

            def attend(it, p, m0, count, nxt=True, again=None, fresh=False):
                nq = DEC if isinstance(it, int) and it == N_IT - 1 else P
                for steps, j in weave(2 * count):
                    m, h = m0 + j // 2, j % 2
                    unit = N_GATE * p + m
                    if fresh and j == 0:
                        remake(p, range(4, 8))
                    if again is not None and j == 2 * count - 3:
                        remake(again, range(0, 2))
                    ahead = m + 1 + h
                    if isinstance(unit, int):
                        row = row_of(PASS_GATE + unit + 1 + h)
                    else:
                        row = ROW_GATE + ahead % N_GATE
                    load_w(PASS_GATE + unit + 1 + h, 1 - h, row)
                    if again is not None and j == 2 * count - 1:
                        remake(again, range(2, 4))
                    if h == 1 and not (isinstance(unit, int) and unit == 0):
                        if m > 0:
                            store_gate(p, m - 1)
                        else:
                            store_gate(p - 1, N_GATE - 1)
                    for s in steps:
                        if s == 2 and not (isinstance(it, int) and it == 0):
                            store_gla(it - 1)
                            load_gla(it, nq)
                        if s == 3 and isinstance(it, int) and it == N_IT - 1:
                            sp.wait_ge(s_su, 8 * it)
                            sp.dma_start(state_prompt.rearrange("h d v -> d h v"), st[:, 0]).then_inc(s_sst, 16)
                            sp.wait_ge(s_sst, 16)
                            sp.dma_start(st[:, 0], state_in.rearrange("h d v -> d h v")).then_inc(s_sld, 16)
                        if s == 12 and nxt:
                            load_attention(it + 1, DEC if isinstance(it, int) and it == N_IT - 2 else P)
                        if s == 12 and isinstance(it, int) and it == N_IT - 2:
                            sp.wait_ge(s_pv, 4 * it + 4)
                            sp.dma_start(v_prev[:], v_cache).then_inc(s_vp, 16)
                        if s == 13:
                            store_attention(it, nq)

            sequence(sp, attend)
            store_gate(GA - 1, N_GATE - 1)
            store_gla(N_IT - 1, DEC)
            sp.wait_ge(s_su, 8 * (N_IT - 1) + 4)
            sp.dma_start(state_sample.rearrange("h d v -> d h v"), st[:, 1]).then_inc(s_sst, 16)

            sp.wait_ge(s_oast, 16 * N_IT)
            sp.wait_ge(s_ogst, 16 * N_IT)
            sp.wait_ge(s_mg, 2 * GA * N_GATE)
            for n, (h, g, j) in enumerate(B_ORDER):
                load_piece(o_dram.rearrange("k p t -> p k t"), h * HK + 2 * j, columns(*GRP[g]), GRP[g][1], n, s_y, s_blo)
            for slot in range(2):
                sp.wait_ge(s_gst[slot], 8 * GA * N_GATE)
            sp.wait_ge(s_sst, 32)

            def load_gate(m, i):
                ge(sp, (s_ya, s_yg)[i], 3 * m)
                settle(sp)
                sp.dma_start(gate[:, i], g_dram[m + i * N_OUT]).then_inc(s_g[i], 16)

            def store_merged(m):
                sp.wait_ge(s_yg, 3 * m + 3)
                settle(sp)
                sp.dma_start(m_dram[m], stage[:]).then_inc(s_mst, 16)

            def load_merged(h):
                for n, (hh, g, j) in enumerate(B_ORDER):
                    if hh == h:
                        load_piece(m_dram.rearrange("k p t -> p k t"), h * HK + 2 * j, columns(*GRP[g]), GRP[g][1], n, s_z, s_mlo)

            load_gate(0, 0)
            load_gate(0, 1)
            with sp.Fori(0, N_OUT - 2) as m:
                load_w(m + PASS_BRANCH + 1, 1, m + ROW_BRANCH + 1)
                load_gate(m + 1, 0)
                load_w(m + PASS_BRANCH + 2, 0, m + ROW_BRANCH + 2)
                store_merged(m)
                load_gate(m + 1, 1)
            for m in range(N_OUT - 2, N_OUT):
                load_w(m + PASS_BRANCH + 1, 1, m + ROW_BRANCH + 1)
                if m + 1 < N_OUT:
                    load_gate(m + 1, 0)
                load_w(m + PASS_BRANCH + 2, 0, m + ROW_BRANCH + 2)
                if m + 1 < N_OUT:
                    store_merged(m)
                    load_gate(m + 1, 1)
            sp.wait_ge(s_mst, 16 * (N_OUT - 1))
            load_merged(0)
            store_merged(N_OUT - 1)
            sp.wait_ge(s_mst, 16 * N_OUT)
            load_merged(1)

            def load_x(g, n, k):
                a, w = GRP[g]
                ge(sp, s_fin, 2 * n)
                settle(sp)
                sp.dma_start(stage[:, 0:w], xT.rearrange("(k p) t -> k p t", p=P)[k, :, a:a + w]).then_inc(s_xo, 16)

            def store_y(g, n, k):
                a, w = GRP[g]
                sp.wait_ge(s_fin, 2 * n + 2)
                settle(sp)
                sp.dma_start(yT.rearrange("(k p) t -> k p t", p=P)[k, :, a:a + w], stage2[:, 0:w]).then_inc(s_yst, 16)

            for g in range(3):
                base = PASS_OUT + g * KT

                def pair(i):
                    for r in range(2):
                        m = 2 * i + r
                        if g > 0:
                            load_x(g - 1, (g - 1) * KT + m, m)
                        for d in range(2):
                            p = base + m + 1 + d
                            if isinstance(p, int):
                                if p < PASS_OUT + 3 * KT:
                                    load_w(p, 1 - d, row_of(p))
                            else:
                                load_w(p, 1 - d, ROW_OUT + m + 1 + d)
                        if g > 0:
                            store_y(g - 1, (g - 1) * KT + m, m)

                pair(0)
                with sp.Fori(1, KT // 2 - 1) as i:
                    pair(i)
                pair(KT // 2 - 1)
            with sp.Fori(0, KT) as m:
                load_x(2, 2 * KT + m, m)
                store_y(2, 2 * KT + m, m)
            sp.wait_ge(s_kv, 16 * 6)
            sp.wait_ge(s_yst, 16 * 3 * KT)

        @block.scalar
        def _(act):
            def hi_w(p, h, *freed):
                act.wait_ge(s_w[h], 16 * p + 16)
                if freed:
                    act.wait_ge(*freed)
                act.activation(w_hi[:, h], w_raw[:, h], ACT.Copy).then_inc(s_whi, 1)

            def hi_piece(n, sems, done, out, k, w, scale):
                slot = k // 2 % 2
                act.wait_ge(sems[slot], 8 * (n - slot) + 16)
                for q in range(2):
                    i = act.activation(out[:, k + q, 0:w], ring[:, slot, q, 0:w], ACT.Copy, scale=scale(k + q))
                i.then_inc(done, 1)

            act.wait_ge(s_wlr, 16)
            act.wait_ge(s_cset, 2)
            act.activation(wlr[:, :, 0:RANK], wlr_raw[:], ACT.Copy).then_inc(s_lrhi, 1)
            act.wait_ge(s_norm, 16)
            pre = lambda k: norm_sb[:, 0, k:k + 1]
            for n, (h, g, j) in enumerate(X_ORDER):
                slot, k = n % X_SLOTS, h * HK + 2 * j
                act.wait_ge(s_x[slot], 16 * (n // X_SLOTS) + 16)
                for q in range(2):
                    i = act.activation(uh[g][:, k + q, :], x_slot[slot][:, q], ACT.Copy, scale=pre(k + q))
                i.then_inc(s_uhi, 1)
                ge(act, s_ssq, 2 * n - 1)
                act.activation(sqx[:, n % 2], x_slot[slot], ACT.Square).then_inc(s_sqx, 1)
                if n == 0:
                    hi_w(0, 0)
                if n == NX // 2 - 3:
                    hi_w(0, 1)
            hi_w(1, 0, s_mp, GA)
            for t in range(1, 1 + len(FORGET)):
                hi_w(t, 1, s_mp, 2 * GA * t)
                a, b = FORGET[t - 1]
                nq = P if b < N_IT else DEC
                for i in range(b - a):
                    if i == 0 and t == 1:
                        act.wait_ge(s_lrp, 2 * GA)
                    act.wait_ge(s_lmin, a + i + 1)
                    ins = act.activation(fexp[0:nq, i], bank[4 + i][0:nq, :], ACT.Abs)
                ins.then_inc(s_labs, 1)
                act.wait_ge(s_labs, t)
                act.activation(fexp[0:nq, 0:b - a], fexp[0:nq, 0:b - a], ACT.Exp, scale=-1.0).then_inc(s_lexp, 1)
                act.wait_ge(s_lexp, t)
                act.activation(fexp[0:nq, 0:b - a], fexp[0:nq, 0:b - a], ACT.Ln, bias=1.0).then_inc(s_lln, 1)
                hi_w(t + 1, 0, s_mp, 2 * GA * t + GA)
                act.wait_ge(s_la, t)
            with act.Fori(1 + len(FORGET), N_P) as t:
                hi_w(t, 1, s_mp, 2 * GA * t)
                hi_w(t + 1, 0, s_mp, 2 * GA * t + GA)

            act.wait_ge(s_mp, 2 * GA * N_P)
            act.wait_ge(s_bc, 48)
            act.activation(decay[:], decay_raw, ACT.Copy).then_inc(s_dcy, 1)
            act.wait_ge(s_clr, 4)

            def step(s, it, nq, kts, nch):
                lo, hi = kts[0] * P, P + nq
                nk = (P, nq)
                first = isinstance(it, int) and it == 0
                final = isinstance(it, int) and it == N_IT - 1

                if s == 0:
                    ge(act, s_pv, 4 * it)
                    if not first and not final:
                        act.activation(v_prev[:], v_cur[:], ACT.Copy).then_inc(s_vsh, 1)
                        act.wait_ge(s_vsh, it)
                    act.wait_ge(s_pt, N_T * it + 1)
                    act.activation(v_cur[0:nq], bank[2][0:nq, 0:256], ACT.Copy).then_inc(s_tev, 1)
                if 2 <= s < 10:
                    u = s - 2
                    act.wait_ge(s_pt, N_T * it + 2 + u)
                    gi = u // 2
                    if gi >= 2:
                        act.wait_ge(s_pv, 4 * it + gi - 1)
                    for kt in kts:
                        i = act.activation(pT[0:nk[kt], gi % 2, kt, 2 * (u % 2):2 * (u % 2) + 2, 0:nq],
                                           bank[2][0:nk[kt], :].rearrange("p (k i q) -> p k i q", k=2, i=2)[:, kt, :, 0:nq],
                                           ACT.Copy)
                    i.then_inc(s_tev, 1)
                if s < 8:
                    u = s
                    act.wait_ge(s_snm, 8 * it + u + 1)
                    ge(act, s_pt, N_T * it + u if u >= 2 else N_T * it)
                    for i in range(2):
                        act.activation(pb[0:nq, u % 2, i, lo:hi], s8[0:nq, u % 2, i, lo:hi], ACT.Exp,
                                       bias=nm[0:nq, u % 2, i:i + 1], scale=HEAD_DIM ** -0.5,
                                       accum_out=rsum[0:nq, u % 2, i:i + 1])
                    act.activation(esink[0:nq, u % 2], snm[0:nq, u % 2], ACT.Exp).then_inc(s_ep, 1)
                if s == 3:
                    act.wait_ge(s_qa, 16 * it + 16)
                    ge(act, s_z2, it)
                    act.activation(th[:, :, 0:nq], qa[:, 10:18, 0:nq], ACT.Tanh, scale=0.5).then_inc(s_tz, 1)
                if s == 8:
                    act.wait_ge(s_lac, 16 * it + 16)
                    act.activation(lac_hi[0:nq], lac[0:nq], ACT.Copy).then_inc(s_lch, 1)
                if s in (9, 11, 13, 15):
                    hh = (s - 9) // 2
                    ge(act, s_qk, 4 * it + hh - 1)
                    for c in range(nch):
                        act.wait_ge(s_e, 8 * it + nch * hh + c + 1)
                        act.activation(ex[:, hh % 2, c], bank[c][:, :].rearrange("p (b t) -> p b t", t=CHUNK),
                                       ACT.Exp).then_inc(s_ex, 1)
                if s in (10, 12):
                    half = (s - 10) // 2
                    act.wait_ge(s_pt, N_T * it + (10, 12)[half])
                    act.activation(vg[0:nq, half * 512:half * 512 + 512], bank[2][0:nq, :], ACT.Copy).then_inc(s_tev, 1)
                if s in (11, 13, 15, 17):
                    hh = (s - 11) // 2
                    act.wait_ge(s_pt, N_T * it + (11, 13, 14, 15)[hh])
                    for c in range(nch):
                        r = slice(c * CHUNK, (c + 1) * CHUNK)
                        i = act.activation(kt_tok[r, c, hh], bank[2][r, 0:GLA_DK], ACT.Copy)
                    i.then_inc(s_tev, 1)
                if s in (17, 21):
                    pair = (s - 17) // 4
                    act.wait_ge(s_o, 4 * it + nch * (pair + 1))
                    ps = bank[(3, 0)[pair]][:, :].rearrange("p (a b t) -> p a b t", a=2, b=2)[:, :, :, 0:nq]
                    a = slice(2 * pair, 2 * pair + 2)
                    act.activation(os_[:, a, :, 0:nq], ps, ACT.Copy, scale=GLA_DK ** -0.5)
                    act.activation(sq[:, a, :, 0:nq], ps, ACT.Square, scale=GLA_DK ** -0.5).then_inc(s_oev, 1)
                if s == 19:
                    act.wait_ge(s_gl, 16 * it + 16)
                    act.wait_ge(s_zs, it + 1)
                    act.activation(th[:, :, 0:nq], gl[:, 16:24, 0:nq], ACT.Tanh, scale=0.5).then_inc(s_tg, 1)

            def remake(p, pieces, unit):
                for j in pieces:
                    act.wait_ge(s_mg, 2 * unit + 1 + j // 4)
                    hi_piece(X_AGAIN * (p - 1) + j, s_xa, s_uhi, uh[0], 2 * j, GAW, pre)

            def gate_tanh(unit, m):
                act.wait_ge(s_gz, unit + 1)
                slot = m % 2
                ge(act, s_gst[slot], 8 * (unit - slot))
                act.activation(stage2[:, slot * GAW:(slot + 1) * GAW], stage[:, slot * GAW:(slot + 1) * GAW], ACT.Tanh,
                               bias=bg_half[:, m:m + 1], scale=0.5).then_inc(s_th, 1)

            def attend(it, p, m0, count, nxt=True, again=None, fresh=False):
                kts, nch, nq = shape_of(it)
                for steps, j in weave(2 * count):
                    m, h = m0 + j // 2, j % 2
                    unit = N_GATE * p + m
                    if h == 0:
                        if isinstance(unit, int) and unit == 0:
                            hi_w(PASS_GATE, 1, s_mp, 2 * GA * N_P)
                        else:
                            hi_w(PASS_GATE + unit, 1, s_mg, 2 * unit)
                    else:
                        hi_w(PASS_GATE + unit + 1, 0, s_mg, 2 * unit + 1)
                    for s in steps:
                        step(s, it, nq, kts, nch)
                    if h == 0 and not (isinstance(unit, int) and unit == 0):
                        gate_tanh(unit - 1, (m - 1) % N_GATE)
                    if fresh and j == 0:
                        remake(p, range(4, 8), unit - 1)
                    if again is not None and j == 2 * count - 1:
                        remake(again, range(0, 4), unit)

            sequence(act, attend)
            gate_tanh(GA * N_GATE - 1, N_GATE - 1)

            act.wait_ge(s_mg, 2 * GA * N_GATE)
            for n, (h, g, j) in enumerate(B_ORDER):
                hi_piece(n, s_y, s_bhi, bh[g], h * HK + 2 * j, GRP[g][1], lambda k: 1.0)
                if n == NB // 2:
                    hi_w(PASS_BRANCH, 1, s_mg, 2 * GA * N_GATE)
            hi_w(PASS_BRANCH + 1, 0, s_mb, 3)
            with act.Fori(1, N_OUT) as m:
                hi_w(PASS_BRANCH + m, 1, s_mb, 6 * m)
                hi_w(PASS_BRANCH + m + 1, 0, s_mb, 6 * m + 3)

            for n, (h, g, j) in enumerate(B_ORDER):
                if n == NB // 2:
                    act.wait_ge(s_mb, 6 * N_OUT)
                hi_piece(n, s_z, s_mhi, mh[g], h * HK + 2 * j, GRP[g][1], lambda k: 0.5)
                if n == NB // 2 + 3:
                    hi_w(PASS_OUT, 1, s_mb, 6 * N_OUT)
            for g in range(3):
                base = PASS_OUT + g * KT

                def pair(i):
                    for r in range(2):
                        m = 2 * i + r
                        n = g * KT + m
                        if not isinstance(n, int) or n > 0:
                            hi_w(PASS_OUT + n, 1, s_mo, 2 * n)
                        if not isinstance(n, int) or n < 3 * KT - 1:
                            hi_w(PASS_OUT + n + 1, 0, s_mo, 2 * n + 1)
                        act.wait_ge(s_mo, 2 * n + 2)
                        settle(act)
                        act.activation(out_sb[g][:, bass.ds(m, 1), 0:GRP[g][1]], bank[r][:, 0:GRP[g][1]].unsqueeze(1),
                                       ACT.Copy).then_inc(s_oev2, 1)

                pair(0)
                with act.Fori(1, KT // 2 - 1) as i:
                    pair(i)
                pair(KT // 2 - 1)

        @block.gpsimd
        def _(pool):
            pool.memset(ssq[:], 0.0).then_inc(s_ssq, 1)
            pool.memset(minus_half[:], -0.5).then_inc(s_pset, 1)
            pool.memset(mean[:], 1.0).then_inc(s_pset, 1)
            pool.wait_ge(s_pset, 2)
            pool.wait_ge(s_ssq, 1)
            for n, (h, g, j) in enumerate(X_ORDER):
                pool.wait_ge(s_sqx, n + 1)
                for q in range(2):
                    pool.tensor_tensor(ssq[:, g], ssq[:, g], sqx[:, n % 2, q], ALU.add).then_inc(s_ssq, 1)
                    pool.wait_ge(s_ssq, 2 * n + q + 2)

            def roots(n, count):
                pool.wait_ge(s_rst, 2 * n + 2)
                pool.tensor_tensor(root[:, 0:count], mean[:, 0:count], minus_half[:].to_broadcast([P, count]), ALU.pow).then_inc(s_rsp, 1)

            def gla_roots(it, nq=P):
                pool.wait_ge(s_var, it + 1)
                ge(pool, s_gdg, it)
                pool.tensor_tensor(groot[0:nq], gmean[0:nq], minus_half[0:nq].to_broadcast([nq, GLA_HEADS]), ALU.pow).then_inc(s_gpw, 1)

            roots(0, N_IT)
            pool.wait_ge(s_last, 16 * len(FORGET))
            pool.memset(kw[:], 0.0).then_inc(s_clr, 1)
            pool.wait_ge(s_mp, 2 * GA * N_P)
            pool.memset(st[:, 0], 0.0).then_inc(s_clr, 1)
            pool.memset(kt_tok[:], 0.0).then_inc(s_clr, 1)
            pool.memset(gsc[:], 0.0).then_inc(s_clr, 1)
            gla_roots(0)
            with pool.Fori(1, N_IT - 1) as it:
                gla_roots(it)
            gla_roots(N_IT - 1, DEC)
            for n in range(3):
                roots(n + 1, 3)

        @block.vector
        def _(dve):
            def lo_w(p, h):
                dve.wait_ge(s_whi, 2 * p + h + 1)
                dve.tensor_tensor(w_lo[:, h], w_raw[:, h], w_hi[:, h].bitcast(f32), ALU.subtract).then_inc(s_wlo, 1)

            def lo_piece(n, hi_done, done, hi_t, out, k, w, scale):
                dve.wait_ge(hi_done, n + 1)
                slot = k // 2 % 2
                for q in range(2):
                    i = dve.scalar_tensor_tensor(out=out[:, k + q, 0:w], in0=ring[:, slot, q, 0:w], scalar=scale(k + q),
                                                 in1=hi_t[:, k + q, 0:w].bitcast(f32), op0=ALU.mult, op1=ALU.subtract)
                i.then_inc(done, 1)

            dve.memset(ones[:], 1.0).then_inc(s_cset, 1)
            dve.memset(wlr[:].bitcast(f32), 0.0).then_inc(s_cset, 1)
            dve.memset(lr[:], 0.0).then_inc(s_cset, 1)
            dve.wait_ge(s_cset, 3)
            dve.memset(lr[2 * RANK:2 * RANK + 1, :], 1.0).then_inc(s_cset, 1)
            dve.wait_ge(s_lrhi, 1)
            dve.tensor_tensor(wlr[:, :, RANK:2 * RANK], wlr_raw[:], wlr[:, :, 0:RANK].bitcast(f32), ALU.subtract).then_inc(s_lrlo, 1)
            pre = lambda k: norm_sb[:, 0, k:k + 1]
            dve.wait_ge(s_norm, 16)
            for n, (h, g, j) in enumerate(X_ORDER):
                k = h * HK + 2 * j
                dve.wait_ge(s_uhi, n + 1)
                for q in range(2):
                    i = dve.scalar_tensor_tensor(out=ul[g][:, k + q, :], in0=x_slot[n % X_SLOTS][:, q], scalar=pre(k + q),
                                                 in1=uh[g][:, k + q, :].bitcast(f32), op0=ALU.mult, op1=ALU.subtract)
                i.then_inc(s_ulo, 1)
                if n == 0:
                    lo_w(0, 0)
                if n == NX // 2 - 3:
                    lo_w(0, 1)
            dve.wait_ge(s_const, 16 * 4)
            dve.tensor_scalar(bg_half[:], bg_sb[:], 0.5, None, ALU.mult).then_inc(s_cset, 1)
            dve.tensor_scalar(gn_half[:], gn_sb[:], 0.5, None, ALU.mult).then_inc(s_cset, 1)
            dve.tensor_scalar(nsink_sb[:], sink_sb[:], -1.0, None, ALU.mult).then_inc(s_cset, 1)

            def token_rstd(n, w, ps, out):
                if n == 0:
                    dve.wait_ge(s_pset, 2)
                full, rest = w // P, w % P
                dve.wait_ge(s_ones, n + 1)
                dve.tensor_scalar(mean[:, 0:full], ps[0][:, 0:full], 1.0 / D_MODEL, EPS, ALU.mult, ALU.add).then_inc(s_rst, 1)
                dve.tensor_scalar(mean[0:rest, full:full + 1], ps[0][0:rest, full:full + 1], 1.0 / D_MODEL, EPS, ALU.mult, ALU.add).then_inc(s_rst, 1)
                dve.wait_ge(s_rsp, n + 1)
                for i, t, size in blocks(w):
                    ins = dve.tensor_scalar(diag[0:size, i], ident[0:size], root[0:size, i:i + 1], None, ALU.mult)
                ins.then_inc(s_dg, 1)
                dve.wait_ge(s_spread, n + 1)
                for b in range(-(-w // 512)):
                    t, size = b * 512, min(512, w - b * 512)
                    dve.tensor_copy(out[:, t:t + size], ps[b][:, 0:size]).then_inc(s_rstd, 1)

            for g, a in quarter:
                dve.wait_ge(s_lrp, GA + g + 1)
                dve.tensor_copy(lr[0:2 * RANK, a:a + GAW], bank[4 + g][0:2 * RANK, 0:GAW]).then_inc(s_lrc, 1)
            lo_w(1, 0)
            token_rstd(0, TOKENS, bank[4:7], rstd)

            def evacuate(tile):
                ge(dve, s_st, 16 * tile)
                for g, a in quarter:
                    dve.wait_ge(s_mp, 2 * GA * tile + GA + g + 1)
                    dve.tensor_tensor(stage[:, a:a + GAW], bank[g][:, 0:GAW], rstd[:, a:a + GAW], ALU.mult).then_inc(s_ev, 1)

            dve.wait_ge(s_rstd, 3)
            evacuate(0)
            dve.wait_ge(s_lrc, GA)
            dve.tensor_tensor(lr[0:2 * RANK], lr[0:2 * RANK], rstd[0:2 * RANK], ALU.mult).then_inc(s_lr, 1)
            for t in range(1, 1 + len(FORGET)):
                lo_w(t, 1)
                a, b = FORGET[t - 1]
                nq = P if b < N_IT else DEC
                for i in range(b - a):
                    dve.wait_ge(s_lap, a + i + 1)
                    ge(dve, s_last, 16 * (t - 1))
                    dve.tensor_scalar(fmin[0:nq, i], bank[4 + i][0:nq, :], 0.0, 1.0 / TAU, ALU.min, ALU.mult).then_inc(s_lmin, 1)
                dve.wait_ge(s_lmin, b)
                dve.wait_ge(s_lln, t)
                dve.scalar_tensor_tensor(out=fmin[0:nq, 0:b - a], in0=fexp[0:nq, 0:b - a], scalar=-1.0 / TAU, in1=fmin[0:nq, 0:b - a],
                                         op0=ALU.mult, op1=ALU.add).then_inc(s_la, 1)
                lo_w(t + 1, 0)
                evacuate(t)
            with dve.Fori(1 + len(FORGET), N_P) as t:
                lo_w(t, 1)
                lo_w(t + 1, 0)
                evacuate(t)

            dve.wait_ge(s_mp, 2 * GA * N_P)
            dve.wait_ge(s_bc, 48)
            for h in range(HEADS):
                dve.tensor_scalar(bias[:, h], dist, -alibi_slope(h) * HEAD_DIM ** 0.5, None, ALU.mult).then_inc(s_bias, 1)
            dve.wait_ge(s_bias, HEADS)

            def step(s, it, nq, kts, nch):
                lo, hi = kts[0] * P, P + nq
                first = isinstance(it, int) and it == 0
                final = isinstance(it, int) and it == N_IT - 1

                def silu_twice(s_tanh, src, done):
                    dve.wait_ge(s_tanh, it + 1)
                    dve.scalar_tensor_tensor(out=zs[:, :, 0:nq], in0=th[:, :, 0:nq], scalar=1.0, in1=src,
                                             op0=ALU.add, op1=ALU.mult).then_inc(done, 1)

                if 1 <= s < 9:
                    u = s - 1
                    dve.wait_ge(s_ep, 8 * it + u + 1)
                    dve.tensor_tensor(den[0:nq, u % 2], rsum[0:nq, u % 2], esink[0:nq, u % 2], ALU.add).then_inc(s_den, 1)
                    dve.wait_ge(s_den, 8 * it + u + 1)
                    dve.reciprocal(rden[0:nq, u % 2], den[0:nq, u % 2]).then_inc(s_rden, 1)
                    dve.wait_ge(s_rden, 8 * it + u + 1)
                    for i in range(2):
                        ins = dve.tensor_scalar(pb[0:nq, u % 2, i, lo:hi], pb[0:nq, u % 2, i, lo:hi],
                                                rden[0:nq, u % 2, i:i + 1], None, ALU.mult)
                    ins.then_inc(s_pr, 1)
                if s < 8:
                    u = s
                    h0 = head0(u)
                    dve.wait_ge(s_sc, 8 * it + u + 1)
                    ge(dve, s_ep, 8 * it + u - 1)
                    if u < 2:
                        ge(dve, s_og, 2 * it)
                    settle(dve)
                    for i in range(2):
                        ins = dve.tensor_tensor_reduce(
                            out=s8[0:nq, u % 2, i, lo:hi], in0=bank[u % 2][0:nq, :].rearrange("p (i k) -> p i k", i=2)[:, i, lo:hi],
                            in1=bias[0:nq, h0 + i, lo:hi], scale=1.0, scalar=-3e38, op0=ALU.add, op1=ALU.max,
                            accum_out=m8[0:nq, u % 2, i:i + 1])
                    ins.then_inc(s_a, 1)
                    dve.wait_ge(s_a, 8 * it + u + 1)
                    dve.scalar_tensor_tensor(out=nm[0:nq, u % 2], in0=m8[0:nq, u % 2], scalar=-HEAD_DIM ** -0.5,
                                             in1=nsink_sb[0:nq, h0:h0 + 2], op0=ALU.mult, op1=ALU.min).then_inc(s_nm, 1)
                    dve.wait_ge(s_nm, 8 * it + u + 1)
                    dve.tensor_tensor(snm[0:nq, u % 2], nm[0:nq, u % 2], sink_sb[0:nq, h0:h0 + 2], ALU.add).then_inc(s_snm, 1)
                if s == 5:
                    silu_twice(s_tz, qa[:, 10:18, 0:nq], s_zs)
                if s in (7, 11):
                    tt = (s - 7) // 4
                    dve.wait_ge(s_pv, 4 * it + 2 * tt + 2)
                    dve.wait_ge(s_zs, it + 1)
                    ge(dve, s_ogst, 16 * it)
                    dve.scalar_tensor_tensor(out=ob[:, 4 * tt:4 * tt + 4, 0:nq],
                                             in0=bank[3][:, :].rearrange("p (j q) -> p j q", j=GROUP)[:, :, 0:nq],
                                             scalar=0.5, in1=zs[:, 4 * tt:4 * tt + 4, 0:nq],
                                             op0=ALU.mult, op1=ALU.mult).then_inc(s_oa, 1)
                if s == 8:
                    dve.wait_ge(s_lch, it + 1)
                    dve.tensor_tensor(lac_lo[0:nq], lac[0:nq], lac_hi[0:nq].bitcast(f32), ALU.subtract).then_inc(s_lcl, 1)
                if s in (10, 12, 14, 16):
                    hh = (s - 10) // 2
                    dve.wait_ge(s_ex, 8 * it + nch * (hh + 1))
                    ge(dve, s_pt, N_T * it + ((0, 0, 11, 13)[hh]))
                    ge(dve, s_o, 4 * it)
                    if hh == 0:
                        dve.wait_ge(s_gl, 16 * it + 16)
                    e = ex[:, hh % 2, 0:nch]
                    q, k = (gl[:, t + hh, 0:nq].rearrange("p (c t) -> p c t", t=CHUNK) for t in (0, 4))
                    wide = [P, nch, LEVELS, CHUNK]
                    dve.tensor_copy(ebend[:, hh, 0:nch].unsqueeze(2), e[:, :, 0, CHUNK - 1:CHUNK])
                    dve.tensor_tensor(qb[:, hh, 0:nch], e[:, :, 0], q, ALU.mult)
                    dve.tensor_tensor(kend[:, hh % 2, 0:nch], e[:, :, 7], k, ALU.mult)
                    dve.tensor_tensor(qe[:, hh % 2, 0:nch], e[:, :, 1:7], q.unsqueeze(2).to_broadcast(wide), ALU.mult)
                    dve.tensor_tensor(ke[:, hh % 2, 0:nch], e[:, :, 1:7], k.unsqueeze(2).to_broadcast(wide), ALU.mult).then_inc(s_qk, 1)
                if s in (11, 13, 15, 17):
                    hh = (s - 11) // 2
                    dve.wait_ge(s_gs, 4 * it + hh + 1)
                    ge(dve, s_gr, 4 * it + hh)
                    if first and hh == 0:
                        dve.wait_ge(s_clr, 4)
                    dve.tensor_tensor(tm[0:nq], bank[4][0:nq, 0:7 * CHUNK].rearrange("p (l t) -> p l t", l=7),
                                      mask[0:nq], ALU.mult).then_inc(s_gm, 1)
                    dve.wait_ge(s_gm, 4 * it + hh + 1)
                    for c in range(nch):
                        r = slice(c * CHUNK, (c + 1) * CHUNK)
                        ins = dve.tensor_reduce(gsc[r, hh, c], tm[r].rearrange("p l t -> p t l"), AX.X, ALU.add)
                    ins.then_inc(s_gr, 1)
                if s in ((14, 16, 18, 20) if nch == 2 else (14, 18)):
                    pair, c = (s - 14) // 4, (s - 14) // 2 % 2
                    n = nch * pair + c
                    if final and pair == 0:
                        dve.wait_ge(s_sld, 16)
                    dve.wait_ge(s_ds, 4 * it + n + 1)
                    ge(dve, s_o, 4 * it + (n if c else 0))
                    ge(dve, s_su, 8 * it + 2 * n)
                    if first and n == 0:
                        dve.wait_ge(s_clr, 4)
                    for i in range(2):
                        hh = 2 * pair + i
                        dve.scalar_tensor_tensor(
                            out=st[:, 1 - c, hh], in0=st[:, c, hh], scalar=ebend[:, hh, c:c + 1],
                            in1=bank[5][:, :].rearrange("p (i v) -> p i v", i=2)[:, i],
                            op0=ALU.mult, op1=ALU.add).then_inc(s_su, 1)
                if s == 19:
                    silu_twice(s_tg, gl[:, 16:24, 0:nq], s_z2)
                if s == 22:
                    dve.wait_ge(s_rm, it + 1)
                    ge(dve, s_gpw, it)
                    dve.tensor_scalar(gmean[0:nq], bank[5][0:nq, 0:GLA_HEADS], 1.0 / GLA_DV, EPS, ALU.mult, ALU.add).then_inc(s_var, 1)
                if s == 23:
                    dve.wait_ge(s_gpw, it + 1)
                    ge(dve, s_rb, it)
                    for hh in range(GLA_HEADS):
                        ins = dve.tensor_scalar(gdiag[0:nq, hh], ident[0:nq], groot[0:nq, hh:hh + 1], None, ALU.mult)
                    ins.then_inc(s_gdg, 1)
                if s == 24:
                    dve.wait_ge(s_rb, it + 1)
                    ps = bank[1][:, :].rearrange("p (a q) -> p a q", a=GLA_HEADS)[:, :, 0:nq]
                    dve.tensor_tensor(os_[:, :, :, 0:nq], os_[:, :, :, 0:nq],
                                      ps.unsqueeze(2).to_broadcast([P, GLA_HEADS, 2, nq]), ALU.mult).then_inc(s_t1, 1)
                if s == 25:
                    dve.wait_ge(s_t1, it + 1)
                    dve.wait_ge(s_z2, it + 1)
                    dve.wait_ge(s_oast, 16 * it + 16)
                    for vh in range(2):
                        dve.scalar_tensor_tensor(out=ob[:, :, 0:nq].rearrange("p (a b) q -> p a b q", b=2)[:, :, vh],
                                                 in0=zs[:, :, 0:nq].rearrange("p (a b) q -> p a b q", b=2)[:, :, vh],
                                                 scalar=gn_half[:, vh:vh + 1], in1=os_[:, :, vh, 0:nq],
                                                 op0=ALU.mult, op1=ALU.mult).then_inc(s_og, 1)

            def remake(p, pieces):
                for j in pieces:
                    lo_piece(NX + X_AGAIN * (p - 1) + j, s_uhi, s_ulo, uh[0], ul[0], 2 * j, GAW, pre)

            def scale_gate(unit, p, m):
                dve.wait_ge(s_mg, 2 * unit + 2)
                ge(dve, s_th, unit - 1)
                if isinstance(unit, int) and unit < 2:
                    dve.wait_ge(s_st, 16 * N_P)
                if not isinstance(unit, int):
                    settle(dve)
                slot = m % 2
                dve.tensor_tensor(stage[:, slot * GAW:(slot + 1) * GAW], bank[6 + slot][:, 0:GAW],
                                  rows[:, p * GAW:(p + 1) * GAW] if isinstance(p, int) else rows[:, bass.ds(p * GAW, GAW)],
                                  ALU.mult).then_inc(s_gz, 1)

            def attend(it, p, m0, count, nxt=True, again=None, fresh=False):
                kts, nch, nq = shape_of(it)
                for steps, j in weave(2 * count):
                    m, h = m0 + j // 2, j % 2
                    unit = N_GATE * p + m
                    early = 0
                    while early < len(steps) and steps[early] not in LATE:
                        step(steps[early], it, nq, kts, nch)
                        early += 1
                    if h == 0:
                        lo_w(PASS_GATE + unit, 1)
                        if not (isinstance(unit, int) and unit == 0):
                            if m > 0:
                                scale_gate(unit - 1, p, m - 1)
                            else:
                                scale_gate(unit - 1, p - 1, N_GATE - 1)
                    else:
                        lo_w(PASS_GATE + unit + 1, 0)
                    for s in steps[early:]:
                        step(s, it, nq, kts, nch)
                    if fresh and j == 0:
                        remake(p, range(4, 8))
                    if again is not None and j == 2 * count - 1:
                        remake(again, range(0, 4))

            sequence(dve, attend)
            scale_gate(GA * N_GATE - 1, GA - 1, N_GATE - 1)

            for n, (h, g, j) in enumerate(B_ORDER):
                lo_piece(n, s_bhi, s_blo, bh[g], bl[g], h * HK + 2 * j, GRP[g][1], lambda k: 1.0)
                if n == NB // 2:
                    lo_w(PASS_BRANCH, 1)

            def merge(m):
                p = m + PASS_BRANCH
                dve.wait_ge(s_g[0], 16 * m + 16)
                for c, (a, w) in enumerate(GRP):
                    dve.wait_ge(s_mb, 6 * m + 1 + c)
                    ge(dve, s_yg, 3 * m)
                    dve.scalar_tensor_tensor(out=ya[:, a:a + w], in0=gate[:, 0, a:a + w], scalar=1.0, in1=bank[c][:, 0:w],
                                             op0=ALU.add, op1=ALU.mult).then_inc(s_ya, 1)
                lo_w(p + 1, 0)
                if isinstance(m, int) and m == N_OUT - 1:
                    for n, (h, g, j) in enumerate(B_ORDER[:NB // 2]):
                        lo_piece(n, s_mhi, s_mlo, mh[g], ml[g], 2 * j, GRP[g][1], lambda k: 0.5)
                dve.wait_ge(s_g[1], 16 * m + 16)
                ge(dve, s_mst, 16 * m)
                for c, (a, w) in enumerate(GRP):
                    dve.wait_ge(s_mb, 6 * m + 4 + c)
                    dve.scalar_tensor_tensor(out=stage2[:, a:a + w], in0=gate[:, 1, a:a + w], scalar=1.0,
                                             in1=bank[3 + c][:, 0:w], op0=ALU.add, op1=ALU.mult).then_inc(s_y2, 1)
                    dve.wait_ge(s_y2, 3 * m + c + 1)
                    dve.wait_ge(s_ya, 3 * m + c + 1)
                    dve.tensor_tensor(stage[:, a:a + w], ya[:, a:a + w], stage2[:, a:a + w], ALU.add).then_inc(s_yg, 1)

            merge(0)
            lo_w(PASS_BRANCH + 1, 1)
            with dve.Fori(1, N_OUT - 1) as m:
                merge(m)
                lo_w(m + PASS_BRANCH + 1, 1)
            merge(N_OUT - 1)

            for n, (h, g, j) in enumerate(B_ORDER):
                if h == 1:
                    lo_piece(n, s_mhi, s_mlo, mh[g], ml[g], HK + 2 * j, GRP[g][1], lambda k: 0.5)
                if n == NB // 2 + 3:
                    lo_w(PASS_OUT, 1)

            def finish(g, k, n):
                w = GRP[g][1]
                ge(dve, s_yst, 16 * n)
                settle(dve)
                dve.scalar_tensor_tensor(out=stage2[:, 0:w].unsqueeze(1), in0=out_sb[g][:, bass.ds(k, 1), 0:w],
                                         scalar=norm_sb[:, 1, bass.ds(k, 1)], in1=rso[:, 0:w].unsqueeze(1),
                                         op0=ALU.mult, op1=ALU.mult).then_inc(s_fin, 1)
                dve.wait_ge(s_fin, 2 * n + 1)
                dve.wait_ge(s_xo, 16 * n + 16)
                dve.tensor_tensor(stage2[:, 0:w], stage2[:, 0:w], stage[:, 0:w], ALU.add).then_inc(s_fin, 1)

            for g in range(3):
                w = GRP[g][1]
                if g:
                    dve.wait_ge(s_ones, g + 1)
                dve.memset(ssqo, 0.0).then_inc(s_ssz, 1)
                dve.wait_ge(s_ssz, g + 1)

                def pair(i):
                    for r in range(2):
                        m = 2 * i + r
                        n = g * KT + m
                        if not isinstance(n, int) or n > 0:
                            lo_w(PASS_OUT + n, 1)
                        if not isinstance(n, int) or n < 3 * KT - 1:
                            lo_w(PASS_OUT + n + 1, 0)
                        if g > 0:
                            finish(g - 1, m, (g - 1) * KT + m)
                        dve.wait_ge(s_oev2, n + 1)
                        settle(dve)
                        src = out_sb[g][:, bass.ds(m, 1), 0:w]
                        dve.tensor_tensor(sqo[:, 0:w].unsqueeze(1), src, src, ALU.mult).then_inc(s_sqo, 1)
                        dve.wait_ge(s_sqo, 2 * n + 1)
                        dve.tensor_tensor(ssqo[:, 0:w], ssqo[:, 0:w], sqo[:, 0:w], ALU.add).then_inc(s_sqo, 1)
                        dve.wait_ge(s_sqo, 2 * n + 2)

                pair(0)
                with dve.Fori(1, KT // 2 - 1) as i:
                    pair(i)
                pair(KT // 2 - 1)
                token_rstd(g + 1, w, bank[6:7], rso)
                dve.wait_ge(s_rstd, 3 + g + 1)
            with dve.Fori(0, KT) as k:
                finish(2, k, 2 * KT + k)

        @block.tensor
        def _(pe):
            def products(out, h, hi_t, lo_t, w, done, start, stop):
                for k in range(HK):
                    for j, (wt, ut) in enumerate(((w_hi, hi_t), (w_hi, lo_t), (w_lo, hi_t))):
                        ins = pe.matmul(out[:, 0:w], wt[:, h, k, :], ut[:, h * HK + k, 0:w],
                                        start=start and k == 0 and j == 0, stop=stop and k == HK - 1 and j == 2)
                ins.then_inc(done, 1)

            pe.wait_ge(s_lrlo, 1)
            for h in range(2):
                pe.wait_ge(s_wlo, h + 1)
                for g in range(GA):
                    pe.wait_ge(s_ulo, 4 * (GA * h + g) + 4)
                    for k in range(HK):
                        for j, ut in enumerate((uh, ul)):
                            ins = pe.matmul(bank[4 + g][:, 0:GAW], wlr[:, h * HK + k, :], ut[g][:, h * HK + k, 0:GAW],
                                            start=h == 0 and k == 0 and j == 0, stop=h == 1 and k == HK - 1 and j == 1)
                    ins.then_inc(s_lrp, 1)
                    products(bank[g], h, uh[g], ul[g], GAW, s_mp, h == 0, h == 1)

            def token_rstd(n, w, ps, sums):
                for i, t, size in blocks(w):
                    ins = pe.matmul(ps[0][0:size, i:i + 1], sums[:, t:t + size], ones[:, 0:1], start=True, stop=True)
                ins.then_inc(s_ones, 1)
                pe.wait_ge(s_dg, n + 1)
                for i, t, size in blocks(w):
                    ins = pe.matmul(ps[t // 512][:, t % 512:t % 512 + size], ones[0:size, :], diag[0:size, i, 0:size], start=True, stop=True)
                ins.then_inc(s_spread, 1)

            pe.wait_ge(s_cset, 4)
            pe.wait_ge(s_ssq, 2 * NX + 1)
            pe.wait_ge(s_lrc, GA)
            token_rstd(0, TOKENS, bank[4:7], ssq[:].rearrange("p g t -> p (g t)"))

            def project(tile):
                for h in range(2):
                    pe.wait_ge(s_wlo, 2 * tile + h + 1)
                    for g in range(GA):
                        if h == 0:
                            pe.wait_ge(s_ev, GA * (tile - 1) + g + 1)
                        products(bank[g], h, uh[g], ul[g], GAW, s_mp, h == 0, h == 1)

            def forget_products(n):
                a, b = FORGET[n]
                nq = P if b < N_IT else DEC
                ge(pe, s_labs, n)
                for i in range(b - a):
                    t = (a + i) * P
                    pe.matmul(bank[4 + i][0:nq, :], lr[:, t:t + nq], wup[:], start=True, stop=True).then_inc(s_lap, 1)

            pe.wait_ge(s_wup, 16)
            pe.wait_ge(s_lr, 1)
            pe.wait_ge(s_rstd, 3)
            for t in range(1, 1 + len(FORGET)):
                forget_products(t - 1)
                project(t)
            with pe.Fori(1 + len(FORGET), N_P) as t:
                project(t)

            pe.wait_ge(s_labs, len(FORGET))
            pe.wait_ge(s_ev, GA * N_P)

            def step(s, it, nq, kts, nch):
                nk = (P, nq)
                first = isinstance(it, int) and it == 0
                final = isinstance(it, int) and it == N_IT - 1

                if s == 0:
                    pe.wait_ge(s_qa, 16 * it + 16)
                    ge(pe, s_tev, N_T * it)
                    for i in range(2):
                        ins = pe.transpose(bank[2][0:nq, i * P:(i + 1) * P], qa[:, T_V + i, 0:nq], ident[:])
                    ins.then_inc(s_pt, 1)
                    pe.wait_ge(s_kw, 32 * it + (64 if final else 32))
                if 2 <= s < 10:
                    u = s - 2
                    pe.wait_ge(s_pr, 8 * it + u + 1)
                    pe.wait_ge(s_tev, N_T * it + 1 + u)
                    dst = bank[2][:, :].rearrange("p (k i q) -> p k i q", k=2, i=2)
                    for kt in kts:
                        for i in range(2):
                            ins = pe.transpose(dst[0:nk[kt], kt, i, 0:nq], pb[0:nq, u % 2, i, kt * P:kt * P + nk[kt]], ident[0:nq, 0:nq])
                    ins.then_inc(s_pt, 1)
                if s < 8:
                    u = s
                    tile, half = tiles(u)
                    if u >= 2:
                        pe.wait_ge(s_a, 8 * it + u - 1)
                    elif u == 0:
                        ge(pe, s_oev, 2 * it)
                    else:
                        ge(pe, s_t1, it)
                    c0 = kts[0] * P
                    for i in range(2):
                        ins = pe.matmul(bank[u % 2][0:nq, :].rearrange("p (i k) -> p i k", i=2)[:, i, c0:P + nq],
                                        qa[:, tile + i, 0:nq], kw[:, half, tile // 4, c0:P + nq], start=True, stop=True)
                    ins.then_inc(s_sc, 1)
                if s in (4, 6, 8, 10):
                    gi = (s - 4) // 2
                    half, tt = gi % 2, gi // 2
                    g = 2 * tt + half
                    pe.wait_ge(s_tev, N_T * it + 3 + 2 * gi)
                    if gi == 0:
                        ge(pe, s_oev, 2 * it)
                        if final:
                            pe.wait_ge(s_vp, 16)
                    if gi == 2:
                        pe.wait_ge(s_oa, 2 * it + 1)
                    for kt in kts:
                        v = (v_prev, v_cur)[kt]
                        ins = pe.matmul(bank[3][half * HEAD_DIM:(half + 1) * HEAD_DIM, :].rearrange("p (j q) -> p j q", j=GROUP)[:, :, 0:nq],
                                        v[0:nk[kt], g * HEAD_DIM:(g + 1) * HEAD_DIM], pT[0:nk[kt], gi % 2, kt, :, 0:nq],
                                        start=kt == kts[0], stop=kt == kts[-1])
                    ins.then_inc(s_pv, 1)
                if s in (9, 11, 13, 15):
                    hh = (s - 9) // 2
                    if hh == 0:
                        pe.wait_ge(s_lcl, it + 1)
                        if first:
                            pe.wait_ge(s_dcy, 1)
                    d = slice(hh * GLA_DK, (hh + 1) * GLA_DK)
                    for c in range(nch):
                        if hh == 0:
                            pe.wait_ge(s_a, 8 * it + 7 + c)
                        else:
                            pe.wait_ge(s_ex, 8 * it + nch * (hh - 1) + c + 1)
                        pe.matmul(bank[c][:, :], lac_hi[0:nq, d], decay[0:nq, c], start=True, stop=False)
                        pe.matmul(bank[c][:, :], lac_lo[0:nq, d], decay[0:nq, c], start=False, stop=True).then_inc(s_e, 1)
                if s in (10, 12):
                    half = (s - 10) // 2
                    pe.wait_ge(s_gl, 16 * it + 16)
                    pe.wait_ge(s_tev, N_T * it + (9, 11)[half])
                    for i in range(4):
                        ins = pe.transpose(bank[2][0:nq, i * P:(i + 1) * P], gl[:, 8 + 4 * half + i, 0:nq], ident[:])
                    ins.then_inc(s_pt, 1)
                if s in (11, 13, 15, 17):
                    hh = (s - 11) // 2
                    pe.wait_ge(s_qk, 4 * it + hh + 1)
                    ge(pe, s_gm, 4 * it + hh)
                    for c in range(nch):
                        r = slice(c * CHUNK, (c + 1) * CHUNK)
                        for l in range(LEVELS):
                            pe.matmul(bank[4][r, l * CHUNK:(l + 1) * CHUNK], ke[:, hh % 2, c, l], qe[:, hh % 2, c, l], start=True, stop=True)
                        ins = pe.matmul(bank[4][r, 6 * CHUNK:7 * CHUNK], gl[:, 4 + hh, r], gl[:, hh, r], start=True, stop=True)
                    ins.then_inc(s_gs, 1)
                    pe.wait_ge(s_tev, N_T * it + (10, 12, 13, 14)[hh])
                    pe.transpose(bank[2][0:nq, 0:GLA_DK], kend[:, hh % 2, 0:nch].rearrange("p c t -> p (c t)"), ident[:]).then_inc(s_pt, 1)
                if s in ((14, 16, 18, 20) if nch == 2 else (14, 18)):
                    pair, c = (s - 14) // 4, (s - 14) // 2 % 2
                    n = nch * pair + c
                    b = (3, 0)[pair]
                    dst = bank[b][:, :].rearrange("p (a b t) -> p a b t", a=2, b=2)
                    if c == 0:
                        pe.wait_ge(s_gr, 4 * it + 2 * pair + 2)
                        pe.wait_ge(s_tev, N_T * it + (13, 15)[pair])
                        if pair == 0:
                            pe.wait_ge(s_oa, 2 * it + 2)
                            if final:
                                pe.wait_ge(s_sld, 16)
                            elif first:
                                pe.wait_ge(s_clr, 4)
                            else:
                                ge(pe, s_su, 8 * it)
                        else:
                            pe.wait_ge(s_ex, 8 * it + 4 * nch)
                        for i in range(2):
                            hh = 2 * pair + i
                            for vh in range(2):
                                v0 = hh * GLA_DV + vh * P
                                pe.matmul(dst[:, i, vh, 0:nq], vg[0:nq, v0:v0 + P],
                                          gsc[0:nq, hh, 0:nch].rearrange("p c t -> p (c t)"),
                                          start=i == 0 and vh == 0, stop=False, skip_group_check=True)
                    else:
                        pe.wait_ge(s_su, 8 * it + 2 * n)
                    for i in range(2):
                        hh = 2 * pair + i
                        for vh in range(2):
                            ins = pe.matmul(dst[:, i, vh, c * CHUNK:(c + 1) * CHUNK], st[:, c, hh, vh * P:(vh + 1) * P], qb[:, hh, c],
                                            start=False, stop=True, skip_group_check=True)
                    ins.then_inc(s_o, 1)
                    if n == 0:
                        ge(pe, s_var, it)
                    else:
                        pe.wait_ge(s_su, 8 * it + 2 * n)
                    for i in range(2):
                        hh = 2 * pair + i
                        ins = pe.matmul(bank[5][:, i * GLA_DV:(i + 1) * GLA_DV], kt_tok[0:nq, c, hh],
                                        vg[0:nq, hh * GLA_DV:(hh + 1) * GLA_DV], start=True, stop=True)
                    ins.then_inc(s_ds, 1)
                if s == 22:
                    pe.wait_ge(s_oev, 2 * it + 2)
                    pe.wait_ge(s_su, 8 * it + 4 * nch)
                    for hh in range(GLA_HEADS):
                        for vh in range(2):
                            ins = pe.matmul(bank[5][0:nq, hh:hh + 1], sq[:, hh, vh, 0:nq], ones[:, 0:1], start=vh == 0, stop=vh == 1)
                    ins.then_inc(s_rm, 1)
                if s == 24:
                    pe.wait_ge(s_gdg, it + 1)
                    pe.matmul(bank[1][:, :].rearrange("p (a q) -> p a q", a=GLA_HEADS)[:, :, 0:nq], ones[0:nq, :], gdiag[0:nq, :, 0:nq],
                              start=True, stop=True).then_inc(s_rb, 1)

            def attend(it, p, m0, count, nxt=True, again=None, fresh=False):
                kts, nch, nq = shape_of(it)
                for steps, j in weave(2 * count):
                    for s in steps:
                        step(s, it, nq, kts, nch)
                    m, h = m0 + j // 2, j % 2
                    unit = N_GATE * p + m
                    pe.wait_ge(s_wlo, 2 * (PASS_GATE + unit) + h + 1)
                    if fresh and j < 2:
                        pe.wait_ge(s_ulo, NX + X_AGAIN * (p - 1) + 4 * j + 4)
                    if h == 0:
                        ge(pe, s_gz, unit - 1)
                    products(bank[6 + m % 2], h, uh[0], ul[0], GAW, s_mg, h == 0, h == 1)

            sequence(pe, attend)

            pe.wait_ge(s_t1, N_IT)
            pe.wait_ge(s_su, 8 * (N_IT - 1) + 4)

            def branch(m):
                for h in range(2):
                    pe.wait_ge(s_wlo, 2 * (m + PASS_BRANCH) + h + 1)
                    for g in range(3):
                        if isinstance(m, int):
                            pe.wait_ge(s_blo, 4 * (3 * h + g) + 4)
                        else:
                            pe.wait_ge((s_ya, s_yg)[h], 3 * (m - 1) + g + 1)
                        products(bank[3 * h + g], h, bh[g], bl[g], GRP[g][1], s_mb, True, True)

            branch(0)
            with pe.Fori(1, N_OUT) as m:
                branch(m)

            pe.wait_ge(s_ya, 3 * N_OUT)
            for g in range(3):
                def pair(i):
                    for r in range(2):
                        m = 2 * i + r
                        n = g * KT + m
                        ge(pe, s_oev2, n - 1)
                        for h in range(2):
                            pe.wait_ge(s_wlo, 2 * (PASS_OUT + n) + h + 1)
                            if isinstance(m, int) and m == 0:
                                pe.wait_ge(s_mlo, 4 * (3 * h + g) + 4)
                            products(bank[r], h, mh[g], ml[g], GRP[g][1], s_mo, h == 0, h == 1)

                pair(0)
                with pe.Fori(1, KT // 2) as i:
                    pair(i)
                if g == 0:
                    pe.wait_ge(s_ya, 3 * N_OUT)
                pe.wait_ge(s_sqo, 2 * (g + 1) * KT)
                token_rstd(g + 1, GRP[g][1], bank[6:7], ssqo)


def shape_of(it):
    if isinstance(it, int) and it == 0:
        return (1,), 2, P
    if isinstance(it, int) and it == N_IT - 1:
        return (0, 1), 1, DEC
    return (0, 1), 2, P


def tiles(u):
    tt, half, pr = u // 4, (u // 2) % 2, u % 2
    return 4 * tt + 2 * pr, half


def head0(u):
    tile, half = tiles(u)
    return GROUP * (2 * (tile // 4) + half) + tile % 4


def constants():
    import numpy as np
    ident = np.eye(P, dtype=np.float32)
    q, k = np.arange(P)[:, None], np.arange(2 * P)[None, :]
    seen = (k // CHUNK - q // CHUNK >= 0) & (k // CHUNK - q // CHUNK <= WINDOW // CHUNK)
    dist = np.where(seen, np.abs(q + WINDOW - k), -MASKED).astype(np.float32)
    s, t = np.arange(CHUNK)[:, None], np.arange(CHUNK)[None, :]
    decay = [(s <= t)]
    mask = []
    for w in (32, 16, 8, 4, 2, 1):
        ref = t // (2 * w) * 2 * w + w - 1
        right = t // w % 2 == 1
        decay.append(np.where(right, (s > ref) & (s <= t), (s > t) & (s <= ref)))
        mask.append((s // (2 * w) == t // (2 * w)) & (s // w % 2 == 0) & right)
    decay.append(s > t)
    mask.append(s == t)
    decay = np.concatenate(decay, 1).astype(np.float32)
    mask = np.concatenate(mask, 1).astype(np.float32)
    none = np.zeros_like(decay)
    decay = np.block([[decay, none], [none, decay]])
    return ident, dist, decay, np.concatenate([mask, mask], 0)


def kernel(x_prompt, x_sample, cache_k, cache_v, state_gla, norm_pre, norm_post, w_in, b_gate,
           attn_sinks, w_forget_up, b_forget, gla_norm, w_branch_attn, w_branch_gla, w_out):
    import numpy as np
    import concourse.bacc as bacc
    from concourse.bass_utils import run_bass_kernel_spmd

    asc = np.ascontiguousarray
    x = np.concatenate([np.asarray(x_prompt)[0], np.asarray(x_sample)[0]], 0)
    w = np.asarray(w_in)[0]
    cut = np.cumsum([0, 1024, 256, 256, 1024, 512, 512, 1024, 1024, 16, 2048, 2048])
    part = {n: w[:, cut[i]:cut[i + 1]] for i, n in enumerate(("q", "k", "v", "za", "gq", "gk", "gv", "zg", "lr", "ga", "gg"))}
    order = np.arange(HEADS * HEAD_DIM).reshape(2, 2, GROUP, HEAD_DIM).transpose(0, 2, 1, 3).reshape(-1)
    cols = np.concatenate([part["q"][:, order], part["v"], part["za"][:, order], part["k"], part["gq"], part["gk"],
                           part["gv"], part["zg"], part["ga"], part["gg"]], 1)
    branch = np.concatenate([np.asarray(w_branch_attn)[0][order], np.asarray(w_branch_gla)[0]], 0)

    def tiled(a):
        return a.reshape(KT, P, -1, P).transpose(2, 1, 0, 3).reshape(-1, P, KT * P)

    w_tiles = np.concatenate([tiled(cols), tiled(branch), tiled(np.asarray(w_out)[0])], 0)
    up = np.asarray(w_forget_up)[0]
    ident, dist, decay, mask = constants()

    def per_partition(a):
        return asc(a.reshape(-1, P).T)

    ins = {
        "xT": asc(x.T),
        "w_tiles": w_tiles,
        "w_lr": asc(part["lr"].reshape(KT, P, RANK).transpose(1, 0, 2)),
        "w_up": np.concatenate([up, up, np.asarray(b_forget)[0][None], np.zeros((P - 2 * RANK - 1, up.shape[1]), up.dtype)], 0),
        "norms": asc(np.stack([per_partition(np.asarray(norm_pre)[0]), per_partition(np.asarray(norm_post)[0])], 1)),
        "bgate": per_partition(np.asarray(b_gate)[0]),
        "sinks": asc(np.broadcast_to(np.asarray(attn_sinks)[0], (P, HEADS))),
        "gnorm": per_partition(np.asarray(gla_norm)[0]),
        "kT_cache": asc(np.asarray(cache_k)[0, 0].reshape(WINDOW, 2, P).transpose(1, 2, 0)),
        "v_cache": asc(np.asarray(cache_v)[0, 0].reshape(WINDOW, 2 * P)),
        "state_in": asc(np.asarray(state_gla)[0, 0]),
        "ident_c": ident, "dist_c": dist, "decay_c": decay, "mask_c": mask,
    }
    outs = {
        "yT": [D_MODEL, TOKENS], "k_prompt": [2, P, WINDOW], "v_prompt": [2, P, WINDOW],
        "state_prompt": [GLA_HEADS, GLA_DK, GLA_DV], "k_sample": [2, P, WINDOW],
        "v_old": [WINDOW - DEC, 2 * P], "v_new": [2, P, DEC], "state_sample": [GLA_HEADS, GLA_DK, GLA_DV],
    }
    nc = bacc.Bacc("TRN2", target_bir_lowering=False, num_devices=1)
    aps = {n: nc.dram_tensor("in_" + n, a.shape, mybir.dt.from_np(a.dtype), kind="ExternalInput").ap() for n, a in ins.items()}
    aps |= {n: nc.dram_tensor("out_" + n, shape, mybir.dt.float32, kind="ExternalOutput").ap() for n, shape in outs.items()}
    build_trunk(nc, **aps)
    r = run_bass_kernel_spmd(nc, [{"in_" + n: a for n, a in ins.items()}], core_ids=[0])
    got = {n: np.asarray(r.results[0]["out_" + n]) for n in outs}

    def rows(a):
        return asc(a.transpose(2, 0, 1).reshape(1, 1, a.shape[2], KV_HEADS, HEAD_DIM))

    y = got["yT"].T
    v_sample = np.concatenate([got["v_old"].reshape(1, 1, WINDOW - DEC, KV_HEADS, HEAD_DIM), rows(got["v_new"])], 2)
    return (asc(y[None, :SEQ]), asc(y[None, SEQ:]), rows(got["k_prompt"]), rows(got["v_prompt"]),
            got["state_prompt"][None, None], rows(got["k_sample"]), v_sample, got["state_sample"][None, None])
```

```python
import concourse.bass as bass
from concourse import mybir
from contextlib import ExitStack

D_MODEL, SEQ, DEC, WINDOW = 2048, 1024, 64, 128
TOKENS = SEQ + DEC
HEADS, KV_HEADS, HEAD_DIM = 16, 4, 64
GROUP = HEADS // KV_HEADS
GLA_HEADS, GLA_DK, GLA_DV, RANK = 4, 128, 256, 16
TAU, EPS = 16.0, 1e-6
CHUNK = 64
P = 128
KT = D_MODEL // P
HK = KT // 2
GA, GAW = 4, TOKENS // 4
GRP = [(0, 364), (364, 362), (726, 362)]
GW = 364
T_Q, T_V, T_ZA, T_K, T_GQ, T_GK, T_GV, T_ZG = 0, 8, 10, 18, 20, 24, 28, 36
X_SLOTS, XA_SLOTS = 6, 4
FORGET = [(0, 4), (4, 8), (8, 9)]
N_P = 44
N_GATE = 32
N_OUT = D_MODEL // P
ROW_GATE, ROW_BRANCH, ROW_OUT = N_P, N_P + N_GATE, N_P + N_GATE + N_OUT
PASS_GATE = N_P
PASS_BRANCH = PASS_GATE + GA * N_GATE
PASS_OUT = PASS_BRANCH + N_OUT
N_IT = SEQ // P + 1
BLOCKS = 8
LEVELS = BLOCKS - 2
N_T = 15
STEPS = 26
MASKED = -1e30
ALONE = 3
WITH_LAST = (11, 10, 8)
JOINED = (19, 21, 25, 23)
LATE = (18, 19, 20, 21, 25)


def alibi_slope(h):
    return 2.0 ** (-8.0 * (h + 1) / HEADS)


def weave(halves, it):
    if it is None:
        return [([], j) for j in range(halves)]
    joined = JOINED[:max(0, STEPS - halves)]
    groups = []
    for s in range(STEPS):
        if s in joined:
            groups[-1].append(s)
        else:
            groups.append([s])
    return [(sum((g for i, g in enumerate(groups) if i * halves // len(groups) == j), []), j) for j in range(halves)]


def build_trunk(nc, xT, w_tiles, w_lr, w_up, norms, bgate, sinks, gnorm, kT_cache, v_cache, state_in,
                ident_c, dist_c, decay_c, mask_c,
                yT, k_prompt, v_prompt, state_prompt, k_sample, v_old, v_new, state_sample):
    f32, f32r = mybir.dt.float32, mybir.dt.float32r
    ALU = mybir.AluOpType
    ACT = mybir.ActivationFunctionType
    AX = mybir.AxisListType

    p_dram = nc.dram_tensor("p_scratch", [N_P, P, TOKENS], f32).ap()
    g_dram = nc.dram_tensor("gate_scratch", [N_GATE, P, TOKENS], f32).ap()
    o_dram = nc.dram_tensor("o_scratch", [KT, P, TOKENS], f32).ap()
    m_dram = nc.dram_tensor("m_scratch", [KT, P, TOKENS], f32).ap()
    la_dram = nc.dram_tensor("la_scratch", [N_IT, P, GLA_HEADS * GLA_DK], f32).ap()

    with ExitStack() as ctx:
        def sb(name, shape, dt=f32, to=None):
            return (to or ctx).enter_context(nc.sbuf_tensor(name, shape, dt))

        def sem(name):
            return ctx.enter_context(nc.semaphore(name))

        w_raw = sb("w_raw", [P, 2, HK, P])
        w_hi = sb("w_hi", [P, 2, HK, P], f32r)
        w_lo = sb("w_lo", [P, 2, HK, P], f32r)
        stage = sb("stage", [P, TOKENS])
        stage2 = sb("stage2", [P, TOKENS])
        ring = sb("ring", [P, 2, 2, GW])
        rows = sb("rows", [P, 3 * GW])
        norm_sb = sb("norm_sb", [P, 2, KT])
        bg_sb = sb("bg_sb", [P, N_GATE])
        bg_half = sb("bg_half", [P, N_GATE])
        gn_sb = sb("gn_sb", [P, 2])
        gn_half = sb("gn_half", [P, 2])
        sink_sb = sb("sink_sb", [P, HEADS])
        nsink_sb = sb("nsink_sb", [P, HEADS])
        ident = sb("ident", [P, P])
        ones = sb("ones", [P, P])
        minus_half = sb("minus_half", [P, 1])
        mean = sb("mean", [P, N_IT])
        root = sb("root", [P, N_IT])

        with ExitStack() as ph:
            uh, ul = [], []
            for g in range(GA):
                uh.append(sb(f"uh{g}", [P, KT, GAW], f32r, ph))
                ul.append(sb(f"ul{g}", [P, KT, GAW], f32r, ph))
            sqx = sb("sqx", [P, 2, 2, GAW], f32, ph)
            ssq = sb("ssq", [P, GA, GAW], f32, ph)
            wlr = sb("wlr", [P, KT, P], f32r, ph)
            wlr_raw = sb("wlr_raw", [P, KT, RANK], f32, ph)
            lr = sb("lr", [P, TOKENS], f32, ph)
            wup = sb("wup", [P, GLA_HEADS * GLA_DK], f32, ph)
        with ExitStack() as ph:
            for g in range(GA):
                sb(f"uh_under{g}", [P, KT, GAW], f32r, ph)
                sb(f"ul_under{g}", [P, KT, GAW], f32r, ph)
            fmin = sb("fmin", [P, 4, GLA_HEADS * GLA_DK], f32, ph)
            sb("forget_gap", [P, 4 * GAW * 2 - 4 * GLA_HEADS * GLA_DK], f32, ph)
            fexp = sb("fexp", [P, 4, GLA_HEADS * GLA_DK], f32, ph)
        with ExitStack() as ph:
            sb("uh_kept", [P, KT, GAW], f32r, ph)
            sb("ul_kept", [P, KT, GAW], f32r, ph)
            bias = sb("bias", [P, HEADS, 2 * P], f32, ph)
            mask = sb("mask", [P, 7, CHUNK], f32, ph)
            decay = sb("decay", [P, 2, BLOCKS * CHUNK], f32r, ph)
            lac = sb("lac", [P, 512], f32, ph)
            lac_hi = sb("lac_hi", [P, 512], f32r, ph)
            lac_lo = sb("lac_lo", [P, 512], f32r, ph)
            th = sb("th", [P, 8, P], f32, ph)
            zs = sb("zs", [P, 8, P], f32, ph)
            v_prev = sb("v_prev", [P, KV_HEADS * HEAD_DIM], f32, ph)
            v_cur = sb("v_cur", [P, KV_HEADS * HEAD_DIM], f32, ph)
            s8 = sb("s8", [P, 2, 2, 2 * P], f32, ph)
            pb = sb("pb", [P, 2, 2, 2 * P], f32, ph)
            m8 = sb("m8", [P, 2, 2], f32, ph)
            nm = sb("nm", [P, 2, 2], f32, ph)
            snm = sb("snm", [P, 2, 2], f32, ph)
            rsum = sb("rsum", [P, 2, 2], f32, ph)
            esink = sb("esink", [P, 2, 2], f32, ph)
            den = sb("den", [P, 2, 2], f32, ph)
            rden = sb("rden", [P, 2, 2], f32, ph)
            pT = sb("pT", [P, 2, 2, GROUP, P], f32, ph)
            ob = sb("ob", [P, 8, P], f32, ph)
            vg = sb("vg", [P, GLA_HEADS * GLA_DV], f32, ph)
            ex = sb("ex", [P, 2, 2, BLOCKS, CHUNK], f32, ph)
            ebend = sb("ebend", [P, GLA_HEADS, 2], f32, ph)
            qb = sb("qb", [P, GLA_HEADS, 2, CHUNK], f32, ph)
            qe = sb("qe", [P, 2, 2, LEVELS, CHUNK], f32, ph)
            ke = sb("ke", [P, 2, 2, LEVELS, CHUNK], f32, ph)
            kend = sb("kend", [P, 2, 2, CHUNK], f32, ph)
            tm = sb("tm", [P, 7, CHUNK], f32, ph)
            gsc = sb("gsc", [P, GLA_HEADS, 2, CHUNK], f32, ph)
            kt_tok = sb("kt_tok", [P, 2, GLA_HEADS, GLA_DK], f32, ph)
            st = sb("st", [P, 2, GLA_HEADS, GLA_DV], f32, ph)
            gmean = sb("gmean", [P, GLA_HEADS], f32, ph)
            groot = sb("groot", [P, GLA_HEADS], f32, ph)
            gdiag = sb("gdiag", [P, GLA_HEADS, P], f32, ph)
            kw = sb("kw", [P, 2, 2, 2 * P], f32, ph)
            qa = sb("qa", [P, 18, P], f32, ph)
            gl = sb("gl", [P, 24, P], f32, ph)
        os_ = s8[:].rearrange("p u i k -> p (u i k)").rearrange("p (a b q) -> p a b q", a=GLA_HEADS, b=2)
        sq = pb[:].rearrange("p u i k -> p (u i k)").rearrange("p (a b q) -> p a b q", a=GLA_HEADS, b=2)
        ex_flat = ex[:].rearrange("p a b l t -> p (a b l t)")
        dist, decay_raw = ex_flat[:, 0:2 * P], ex_flat[:, 512:1536].rearrange("p (c n) -> p c n", c=2)
        with ExitStack() as ph:
            bh, bl = [None] * 3, [None] * 3
            for g in (2, 0, 1):
                bh[g] = sb(f"bh{g}", [P, KT, GW], f32r, ph)
                bl[g] = sb(f"bl{g}", [P, KT, GW], f32r, ph)
            gate = sb("gate", [P, 2, TOKENS], f32, ph)
            ya = sb("ya", [P, TOKENS], f32, ph)
        with ExitStack() as ph:
            mh, ml = [None] * 3, [None] * 3
            for g in (2, 0, 1):
                mh[g] = sb(f"mh{g}", [P, KT, GW], f32r, ph)
                ml[g] = sb(f"ml{g}", [P, KT, GW], f32r, ph)
            out_sb = [sb("out0", [P, KT, GW], f32, ph)]
        with ExitStack() as ph:
            for n in ("mh2_under", "ml2_under"):
                sb(n, [P, KT, GW], f32r, ph)
            out_sb.append(sb("out1", [P, KT, GW], f32, ph))
            x_last = sb("x_last", [P, KT, GW], f32, ph)
            out_sb.append(sb("out2", [P, KT, GW], f32, ph))
        rstd = rows[:, 0:TOKENS]
        rso, ssqo, sqo = (rows[:, i * GW:(i + 1) * GW] for i in range(3))
        diag = ring[:].rearrange("p a b t -> p (a b t)")[:, 0:N_IT * P].rearrange("p (n q) -> p n q", n=N_IT)
        x_slot = [ring[:, i, :, 0:GAW] for i in range(2)]
        for buf in (stage, stage2):
            x_slot += [buf[:, i * 2 * GAW:(i + 1) * 2 * GAW].rearrange("p (q t) -> p q t", q=2) for i in range(2)]
        xa_slot = [x_slot[i] for i in (0, 1, 3, 5)]
        b_slot = [ring[:, i] for i in range(2)] + [t[:, 0:2 * GW].rearrange("p (q t) -> p q t", q=2) for t in (ya, gate[:, 1])]

        def blocks(w):
            return [(n, n * P, min(P, w - n * P)) for n in range(-(-w // P))]

        bank = [ctx.enter_context(nc.psum_tensor(f"bank{i}", [P, 512], f32)) for i in range(8)]
        quarter = [(g, g * GAW) for g in range(GA)]

        s_const = sem("consts_loaded")
        s_cset = sem("consts_set")
        s_w = [sem("w_half0_loaded"), sem("w_half1_loaded")]
        s_whi = sem("w_hi_done")
        s_wlo = sem("w_lo_done")
        s_mp = sem("projection_products_done")
        s_mg = sem("gate_products_done")
        s_mb = sem("branch_products_done")
        s_mo = sem("output_products_done")
        s_x = [sem(f"x_slot{i}_loaded") for i in range(X_SLOTS)]
        s_xa = [sem(f"x_again_slot{i}_loaded") for i in range(XA_SLOTS)]
        s_norm = sem("norms_loaded")
        s_wlr = sem("lr_weights_loaded")
        s_uhi = sem("x_hi_done")
        s_ulo = sem("x_lo_done")
        s_y = [sem(f"branch_slot{i}_loaded") for i in range(4)]
        s_bhi = sem("branch_hi_done")
        s_blo = sem("branch_lo_done")
        s_z = [sem("merged_slot0_loaded"), sem("merged_slot1_loaded")]
        s_mhi = sem("merged_hi_done")
        s_mlo = sem("merged_lo_done")
        s_sqx = sem("x_squared")
        s_ssq = sem("square_sums_done")
        s_ones = sem("token_sums_done")
        s_rst = sem("mean_squares_ready")
        s_rsp = sem("roots_ready")
        s_dg = sem("root_diagonals_ready")
        s_spread = sem("roots_spread")
        s_rstd = sem("rstd_ready")
        s_pset = sem("gpsimd_constants_set")
        s_lrhi = sem("lr_weights_hi_done")
        s_lrlo = sem("lr_weights_lo_done")
        s_lrp = sem("lr_product_done")
        s_lrc = sem("lr_copied")
        s_lr = sem("lr_scaled")
        s_ev = sem("tile_chunks_evacuated")
        s_st = sem("tiles_stored")
        s_gz = sem("gate_units_scaled")
        s_th = sem("gate_units_tanh_done")
        s_gst = [sem("gate_slot0_stored"), sem("gate_slot1_stored")]
        s_pass = {e.engine: sem(f"{n}_waits_passed") for n, e in (("sync", nc.sync), ("scalar", nc.scalar), ("vector", nc.vector))}

        s_wup = sem("forget_weights_loaded")
        s_lap = sem("forget_product_done")
        s_lmin = sem("forget_min_done")
        s_labs = sem("forget_abs_done")
        s_lexp = sem("forget_exp_done")
        s_lln = sem("forget_log_done")
        s_la = sem("forget_logs_ready")
        s_last = sem("forget_logs_stored")
        s_bc = sem("attention_consts_loaded")
        s_bias = sem("alibi_tables_ready")
        s_dcy = sem("decay_matrix_ready")
        s_clr = sem("attention_buffers_cleared")
        s_kv = sem("cache_outputs_stored")

        s_qa = sem("attention_inputs_loaded")
        s_kw = sem("key_window_loaded")
        s_gl = sem("gla_inputs_loaded")
        s_lac = sem("forget_block_loaded")
        s_lch = sem("forget_block_hi_done")
        s_lcl = sem("forget_block_lo_done")
        s_vp = sem("cached_values_loaded")
        s_pt = sem("transposes_done")
        s_tev = sem("transposes_evacuated")
        s_sc = sem("scores_done")
        s_a = sem("scores_biased")
        s_nm = sem("negated_maxima_ready")
        s_snm = sem("sink_minus_max_ready")
        s_ep = sem("exponentials_done")
        s_den = sem("denominators_ready")
        s_rden = sem("reciprocals_ready")
        s_pr = sem("probabilities_ready")
        s_pv = sem("weighted_values_done")
        s_tz = sem("attention_gate_tanh")
        s_zs = sem("attention_gate_silu")
        s_oa = sem("attention_output_ready")
        s_oast = sem("attention_output_stored")
        s_e = sem("decay_sums_done")
        s_ex = sem("decay_exps_done")
        s_qk = sem("decayed_qk_ready")
        s_gs = sem("gla_scores_done")
        s_gm = sem("gla_scores_masked")
        s_gr = sem("gla_scores_ready")
        s_o = sem("gla_output_products_done")
        s_oev = sem("gla_output_evacuated")
        s_ds = sem("state_product_done")
        s_su = sem("state_updated")
        s_rm = sem("gla_square_sums_done")
        s_var = sem("gla_mean_squares_ready")
        s_gpw = sem("gla_roots_ready")
        s_gdg = sem("gla_root_diagonals_ready")
        s_rb = sem("gla_roots_spread")
        s_t1 = sem("gla_output_scaled")
        s_z2 = sem("gla_gate_silu")
        s_tg = sem("gla_gate_tanh")
        s_og = sem("gla_output_ready")
        s_ogst = sem("gla_output_stored")
        s_vsh = sem("values_shifted")
        s_sst = sem("state_stored")
        s_sld = sem("state_loaded")

        s_g = [sem("gate_a_loaded"), sem("gate_b_loaded")]
        s_ya = sem("attention_branch_weighted")
        s_y2 = sem("gla_branch_weighted")
        s_yg = sem("branches_merged")
        s_mst = sem("merged_stored")
        s_mlast = [sem(f"last_merged_group{g}_stored") for g in range(3)]
        s_xl = sem("last_residual_loaded")
        s_yl = sem("last_output_stored")
        s_sc2 = sem("last_output_scaled")
        s_add = [sem("last_even_tiles_added"), sem("last_odd_tiles_added")]
        s_oev2 = sem("output_tiles_evacuated")
        s_ssz = sem("square_sums_cleared")
        s_sqo = sem("output_squares_summed")
        s_xo = [sem("residual_slot0_loaded"), sem("residual_slot1_loaded")]
        s_fin = sem("output_steps")
        s_yst = [sem("output_slot0_stored"), sem("output_slot1_stored")]

        def ge(eng, s, value):
            if not isinstance(value, int) or value > 0:
                eng.wait_ge(s, value)

        def settle(eng):
            eng.sem_inc(s_pass[eng.engine], 1)

        X_ORDER = [(h, g, j) for h in range(2) for g in range(GA) for j in range(HK // 2)]
        B_ORDER = [(h, g, j) for h in range(2) for g in range(3) for j in range(HK // 2)]
        M_ORDER = [(h, g, j) for g in range(3) for h in range(2) for j in range(HK // 2)]
        NX, NB = len(X_ORDER), len(B_ORDER)
        B_LOADS = [0] + [min(2 * j, max(4, j + 1)) for j in range(1, 2 * ALONE)]
        B_SPLITS = [max(0, j - 3) for j in range(2 * ALONE + 1)]
        B_EARLY = B_SPLITS[-1]
        NG = NB // 3
        X_AGAIN = KT // 2

        def w_src(row, h):
            return w_tiles[row, :, h * HK * P:(h + 1) * HK * P].rearrange("p (k c) -> p k c", c=P)

        def row_of(p):
            if p < PASS_GATE:
                return p
            if p < PASS_BRANCH:
                return ROW_GATE + (p - PASS_GATE) % N_GATE
            if p < PASS_OUT:
                return ROW_BRANCH + p - PASS_BRANCH
            return ROW_OUT + (p - PASS_OUT) % N_OUT

        def sequence(eng, attend):
            half = N_GATE // 2
            attend(0, 0, 0, half)
            attend(1, 0, half, half, again=1)
            with eng.Fori(1, GA - 1) as p:
                attend(2 * p, p, 0, half, fresh=True)
                attend(2 * p + 1, p, half, half, again=p + 1)
            attend(N_IT - 3, GA - 1, 0, WITH_LAST[0], fresh=True)
            attend(N_IT - 2, GA - 1, WITH_LAST[0], WITH_LAST[1])
            attend(N_IT - 1, GA - 1, WITH_LAST[0] + WITH_LAST[1], WITH_LAST[2], nxt=False)
            attend(None, GA - 1, N_GATE - ALONE, ALONE, nxt=False)

        block = ctx.enter_context(nc.Block())

        @block.sync
        def _(sp):
            def load_w(p, h, row):
                ge(sp, s_wlo, 2 * (p - 1) + h + 1)
                if not isinstance(p, int):
                    settle(sp)
                sp.dma_start(w_raw[:, h], w_src(row, h)).then_inc(s_w[h], 16)

            def load_piece(view, k, a, w, n, sems, split):
                slot = k // 2 % 2
                ge(sp, split, n - 1)
                settle(sp)
                sp.dma_start(ring[:, slot, :, 0:w], view[:, k:k + 2, a]).then_inc(sems[slot], 16)

            x_view = xT.rearrange("(k p) t -> p k t", p=P)

            def columns(a, w):
                return slice(a, a + w) if isinstance(a, int) else bass.ds(a, w)

            sp.dma_start(norm_sb[:], norms).then_inc(s_norm, 16)
            sp.dma_start(wlr_raw[:], w_lr).then_inc(s_wlr, 16)
            for n, (h, g, j) in enumerate(X_ORDER):
                k = h * HK + 2 * j
                ge(sp, s_ulo, n + 1 - X_SLOTS)
                ge(sp, s_sqx, n + 1 - X_SLOTS)
                sp.dma_start(x_slot[n % X_SLOTS], x_view[:, k:k + 2, g * GAW:(g + 1) * GAW]).then_inc(s_x[n % X_SLOTS], 16)
                if n == 0:
                    load_w(0, 0, 0)
                if n == X_SLOTS:
                    load_w(0, 1, 0)
                    for dst, src in ((bg_sb, bgate), (gn_sb, gnorm), (sink_sb, sinks), (ident, ident_c)):
                        sp.dma_start(dst[:], src).then_inc(s_const, 16)
            load_w(1, 0, 1)
            sp.dma_start(wup[:], w_up).then_inc(s_wup, 16)

            def store_p(tile):
                sp.wait_ge(s_ev, GA * tile + GA)
                sp.dma_start(p_dram[tile], stage[:]).then_inc(s_st, 16)

            def store_forget(n):
                a, b = FORGET[n]
                nq = P if b < N_IT else DEC
                sp.wait_ge(s_la, n + 1)
                sp.dma_start(la_dram[a:b, 0:nq].rearrange("i p n -> p i n"), fmin[0:nq, 0:b - a]).then_inc(s_last, 16)

            load_w(1, 1, 1)
            load_w(2, 0, 2)
            store_p(0)
            load_w(2, 1, 2)
            load_w(3, 0, 3)
            store_p(1)
            for t in range(2, 2 + len(FORGET)):
                load_w(t + 1, 1, t + 1)
                store_forget(t - 2)
                load_w(t + 2, 0, t + 2)
                store_p(t)
            with sp.Fori(2 + len(FORGET), N_P - 1) as t:
                load_w(t + 1, 1, t + 1)
                load_w(t + 2, 0, t + 2)
                store_p(t)

            def tokens(it, n):
                return slice(it * P, it * P + n) if isinstance(it, int) else bass.ds(it * P, n)

            def load_attention(it, nq=P):
                ge(sp, s_sc, 8 * it)
                ge(sp, s_zs, it)
                settle(sp)
                sp.dma_start(qa[:, :, 0:nq], p_dram[T_Q:T_K, :, tokens(it, nq)].rearrange("t p n -> p t n")).then_inc(s_qa, 16)
                keys = p_dram[T_K:T_GQ].rearrange("t p n -> p t n")
                cached = kT_cache.rearrange("t p n -> p t n")
                for half in range(2):
                    r = slice(half * HEAD_DIM, (half + 1) * HEAD_DIM)
                    if isinstance(it, int) and it == 0:
                        sp.wait_ge(s_clr, 1)
                        sp.dma_start(kw[r, half, :, P:2 * P], keys[r, :, 0:P]).then_inc(s_kw, 16)
                    elif isinstance(it, int) and it == N_IT - 1:
                        sp.dma_start(kw[r, half, :, 0:P], cached[r]).then_inc(s_kw, 16)
                        sp.dma_start(kw[r, half, :, P:P + nq], keys[r, :, tokens(it, nq)]).then_inc(s_kw, 16)
                    else:
                        sp.dma_start(kw[r, half], keys[r, :, bass.ds((it - 1) * P, 2 * P)]).then_inc(s_kw, 16)

            def load_gla(it, nq=P):
                ge(sp, s_og, 2 * it)
                settle(sp)
                sp.dma_start(gl[:, :, 0:nq], p_dram[T_GQ:N_P, :, tokens(it, nq)].rearrange("t p n -> p t n")).then_inc(s_gl, 16)
                sp.dma_start(lac[0:nq], la_dram[it, 0:nq]).then_inc(s_lac, 16)

            def store_attention(it, nq=P):
                sp.wait_ge(s_oa, 2 * it + 2)
                settle(sp)
                sp.dma_start(o_dram[0:HK, :, tokens(it, nq)].rearrange("t p n -> p t n"), ob[:, :, 0:nq]).then_inc(s_oast, 16)

            def store_gla(it, nq=P):
                sp.wait_ge(s_og, 2 * it + 2)
                settle(sp)
                sp.dma_start(o_dram[HK:KT, :, tokens(it, nq)].rearrange("t p n -> p t n"), ob[:, :, 0:nq]).then_inc(s_ogst, 16)

            sp.wait_ge(s_st, 16 * T_GQ)
            sp.wait_ge(s_lr, 1)
            sp.wait_ge(s_last, 16 * len(FORGET))
            load_attention(0)
            load_w(N_P, 1, N_P)
            load_w(N_P + 1, 0, N_P + 1)
            store_p(N_P - 1)
            sp.wait_ge(s_mp, 2 * GA * N_P)
            for dst, src in ((dist, dist_c), (decay_raw, decay_c.rearrange("p (c n) -> p c n", c=2)), (mask[:], mask_c.rearrange("p (l t) -> p l t", l=7))):
                sp.dma_start(dst, src).then_inc(s_bc, 16)
            sp.wait_ge(s_st, 16 * N_P)
            load_gla(0)
            recent = SEQ - WINDOW
            for dst, src in ((k_prompt, p_dram[T_K:T_K + 2, :, recent:SEQ]), (v_prompt, p_dram[T_V:T_V + 2, :, recent:SEQ]),
                             (k_sample[:, :, 0:WINDOW - DEC], kT_cache[:, :, DEC:WINDOW]),
                             (k_sample[:, :, WINDOW - DEC:WINDOW], p_dram[T_K:T_K + 2, :, SEQ:TOKENS]),
                             (v_old, v_cache[DEC:WINDOW, :]), (v_new, p_dram[T_V:T_V + 2, :, SEQ:TOKENS])):
                sp.dma_start(dst, src).then_inc(s_kv, 16)

            def store_gate(p, m):
                ge(sp, s_th, N_GATE * p + m + 1)
                settle(sp)
                slot = m % 2
                sp.dma_start(g_dram[m, :, columns(p * GAW, GAW)], stage2[:, slot * GAW:(slot + 1) * GAW]).then_inc(s_gst[slot], 16)

            def remake(p, pieces):
                for j in pieces:
                    slot = j % XA_SLOTS
                    ge(sp, s_ulo, NX + X_AGAIN * (p - 1) + j + 1 - XA_SLOTS)
                    settle(sp)
                    sp.dma_start(xa_slot[slot], x_view[:, 2 * j:2 * j + 2, columns(p * GAW, GAW)]).then_inc(s_xa[slot], 16)

            def load_branch(n):
                h, g, j = B_ORDER[n]
                k, (a, w) = h * HK + 2 * j, GRP[g]
                ge(sp, s_blo, n - 3)
                sp.dma_start(b_slot[n % 4][:, :, 0:w], o_dram.rearrange("k p t -> p k t")[:, k:k + 2, a:a + w]).then_inc(s_y[n % 4], 16)

            def attend(it, p, m0, count, nxt=True, again=None, fresh=False):
                nq = DEC if isinstance(it, int) and it == N_IT - 1 else P
                if it is None:
                    store_gla(N_IT - 1, DEC)
                    sp.dma_start(state_sample.rearrange("h d v -> d h v"), st[:, 1]).then_inc(s_sst, 16)
                for steps, j in weave(2 * count, it):
                    m, h = m0 + j // 2, j % 2
                    unit = N_GATE * p + m
                    if fresh and j == 0:
                        remake(p, range(4, 8))
                    if again is not None and j == 2 * count - 5:
                        remake(again, range(0, XA_SLOTS))
                    ahead = m + 1 + h
                    if isinstance(unit, int):
                        row = row_of(PASS_GATE + unit + 1 + h)
                    else:
                        row = ROW_GATE + ahead % N_GATE
                    load_w(PASS_GATE + unit + 1 + h, 1 - h, row)
                    if h == 1 and not (isinstance(unit, int) and unit == 0):
                        if m > 0:
                            store_gate(p, m - 1)
                        else:
                            store_gate(p - 1, N_GATE - 1)
                    for s in steps:
                        if s == 2 and not (isinstance(it, int) and it == 0):
                            store_gla(it - 1)
                            load_gla(it, nq)
                        if s == 3 and isinstance(it, int) and it == N_IT - 1:
                            sp.wait_ge(s_su, 8 * it)
                            sp.dma_start(state_prompt.rearrange("h d v -> d h v"), st[:, 0]).then_inc(s_sst, 16)
                            sp.wait_ge(s_sst, 16)
                            sp.dma_start(st[:, 0], state_in.rearrange("h d v -> d h v")).then_inc(s_sld, 16)
                        if s == 12 and nxt:
                            load_attention(it + 1, DEC if isinstance(it, int) and it == N_IT - 2 else P)
                        if s == 12 and isinstance(it, int) and it == N_IT - 2:
                            sp.wait_ge(s_pv, 4 * it + 4)
                            sp.dma_start(v_prev[:], v_cache).then_inc(s_vp, 16)
                        if s == 13:
                            store_attention(it, nq)
                    if it is None and j == 1:
                        sp.wait_ge(s_sst, 32)
                        sp.wait_ge(s_oast, 16 * N_IT)
                        sp.wait_ge(s_ogst, 16 * N_IT)
                    if it is None and j > 0:
                        for n in range(B_LOADS[j - 1], B_LOADS[j]):
                            load_branch(n)

            sequence(sp, attend)
            for n in range(B_LOADS[-1], NB):
                load_branch(n)
                if n == B_LOADS[-1]:
                    store_gate(GA - 1, N_GATE - 1)

            def load_gate(m, i):
                ge(sp, (s_ya, s_yg)[i], 3 * m)
                settle(sp)
                sp.dma_start(gate[:, i], g_dram[m + i * N_OUT]).then_inc(s_g[i], 16)

            def store_merged(m):
                sp.wait_ge(s_yg, 3 * m + 3)
                settle(sp)
                sp.dma_start(m_dram[m], stage[:]).then_inc(s_mst, 16)

            m_view = m_dram.rearrange("k p t -> p k t")

            def load_merged(*pieces):
                for n in pieces:
                    h, g, j = M_ORDER[n]
                    if (h, j) == (1, HK // 2 - 1):
                        sp.wait_ge(s_mlast[g], 16)
                    load_piece(m_view, h * HK + 2 * j, columns(*GRP[g]), GRP[g][1], n, s_z, s_mlo)

            def store_last_merged(g):
                a, w = GRP[g]
                sp.wait_ge(s_yg, 3 * (N_OUT - 1) + g + 1)
                sp.dma_start(m_dram[N_OUT - 1, :, a:a + w], stage[:, a:a + w]).then_inc(s_mlast[g], 16)

            for slot in range(2):
                sp.wait_ge(s_gst[slot], 8 * GA * N_GATE)
            load_gate(0, 0)
            sp.wait_ge(s_blo, NB)
            load_gate(0, 1)
            with sp.Fori(0, N_OUT - 2) as m:
                load_w(m + PASS_BRANCH + 1, 1, m + ROW_BRANCH + 1)
                load_gate(m + 1, 0)
                load_w(m + PASS_BRANCH + 2, 0, m + ROW_BRANCH + 2)
                store_merged(m)
                load_gate(m + 1, 1)
            m = N_OUT - 2
            load_w(m + PASS_BRANCH + 1, 1, m + ROW_BRANCH + 1)
            load_gate(m + 1, 0)
            load_w(m + PASS_BRANCH + 2, 0, m + ROW_BRANCH + 2)
            sp.wait_ge(s_mst, 16 * (N_OUT - 2))
            load_merged(0, 1)
            store_merged(m)
            load_gate(m + 1, 1)
            load_w(PASS_OUT, 1, ROW_OUT)
            load_merged(2, 3)
            sp.wait_ge(s_mst, 16 * (N_OUT - 1))
            load_merged(4, 5)
            load_w(PASS_OUT + 1, 0, ROW_OUT + 1)
            store_last_merged(0)
            load_merged(6, 7)
            store_last_merged(1)
            store_last_merged(2)

            def load_x(g, n, k, slot):
                a, w = GRP[g]
                ge(sp, s_fin, 2 * (n - 1))
                settle(sp)
                sp.dma_start(stage[:, slot * GW:slot * GW + w], xT.rearrange("(k p) t -> k p t", p=P)[k, :, a:a + w]).then_inc(s_xo[slot], 16)

            def store_y(g, n, k, slot):
                a, w = GRP[g]
                sp.wait_ge(s_fin, 2 * n + 2)
                settle(sp)
                sp.dma_start(yT.rearrange("(k p) t -> k p t", p=P)[k, :, a:a + w], stage2[:, slot * GW:slot * GW + w]).then_inc(s_yst[slot], 16)

            def next_w(p, m):
                for d in range(2):
                    if not isinstance(p, int) or p + 1 + d < PASS_OUT + 3 * KT:
                        load_w(p + 1 + d, 1 - d, ROW_OUT + ((m + 1 + d) % KT if isinstance(m, int) else m + 1 + d))

            for m in range(KT):
                if m > 0:
                    load_merged(*merged_pieces(m))
                next_w(PASS_OUT + m, m)
            load_x(0, 0, 0, 0)
            for g in (1, 2):
                def pair(i):
                    for r in range(2):
                        m = 2 * i + r
                        n = (g - 1) * KT + m
                        if not isinstance(n, int) or n + 1 < 2 * KT:
                            if isinstance(m, int) and m == KT - 1:
                                load_x(g, n + 1, 0, 1 - r)
                            else:
                                load_x(g - 1, n + 1, m + 1, 1 - r)
                        next_w(PASS_OUT + g * KT + m, m)
                        store_y(g - 1, n, m, r)

                def load_last(k):
                    a, w = GRP[2]
                    sp.dma_start(x_last[:, k:k + 4, 0:w], x_view[:, k:k + 4, a:a + w]).then_inc(s_xl, 16)

                pair(0)
                if g == 1:
                    sp.wait_ge(s_mo, 2 * KT)
                load_last(8 * (g - 1))
                with sp.Fori(1, KT // 2 - 1) as i:
                    pair(i)
                load_last(8 * (g - 1) + 4)
                pair(KT // 2 - 1)
            a, w = GRP[2]
            for i in range(KT // 2):
                for r in range(2):
                    sp.wait_ge(s_add[r], i + 1)
                sp.dma_start(yT.rearrange("(k p) t -> p k t", p=P)[:, 2 * i:2 * i + 2, a:a + w], out_sb[2][:, 2 * i:2 * i + 2, 0:w]).then_inc(s_yl, 16)
            sp.wait_ge(s_yl, 16 * KT // 2)
            sp.wait_ge(s_kv, 16 * 6)
            for slot in range(2):
                sp.wait_ge(s_yst[slot], 16 * KT)

        @block.scalar
        def _(act):
            def hi_w(p, h, *freed):
                act.wait_ge(s_w[h], 16 * p + 16)
                if freed:
                    act.wait_ge(*freed)
                act.activation(w_hi[:, h], w_raw[:, h], ACT.Copy).then_inc(s_whi, 1)

            def hi_piece(n, sems, done, out, k, w, scale):
                slot = k // 2 % 2
                act.wait_ge(sems[slot], 8 * (n - slot) + 16)
                for q in range(2):
                    i = act.activation(out[:, k + q, 0:w], ring[:, slot, q, 0:w], ACT.Copy, scale=scale(k + q))
                i.then_inc(done, 1)

            act.wait_ge(s_wlr, 16)
            act.wait_ge(s_cset, 2)
            act.activation(wlr[:, :, 0:RANK], wlr_raw[:], ACT.Copy).then_inc(s_lrhi, 1)
            act.wait_ge(s_norm, 16)
            pre = lambda k: norm_sb[:, 0, k:k + 1]
            for n, (h, g, j) in enumerate(X_ORDER):
                slot, k = n % X_SLOTS, h * HK + 2 * j
                act.wait_ge(s_x[slot], 16 * (n // X_SLOTS) + 16)
                for q in range(2):
                    i = act.activation(uh[g][:, k + q, :], x_slot[slot][:, q], ACT.Copy, scale=pre(k + q))
                i.then_inc(s_uhi, 1)
                if n == 0:
                    hi_w(0, 0)
                if n == NX // 2 - 3:
                    hi_w(0, 1)
            hi_w(1, 0, s_mp, GA)
            hi_w(1, 1, s_mp, 2 * GA)
            hi_w(2, 0, s_mp, 3 * GA)
            for n, t in enumerate(range(2, 2 + len(FORGET))):
                hi_w(t, 1, s_mp, 2 * GA * t)
                a, b = FORGET[n]
                nq = P if b < N_IT else DEC
                for i in range(b - a):
                    if i == 0 and n == 0:
                        act.wait_ge(s_lrp, 2 * GA)
                    act.wait_ge(s_lmin, a + i + 1)
                    ins = act.activation(fexp[0:nq, i], bank[4 + i][0:nq, :], ACT.Abs)
                ins.then_inc(s_labs, 1)
                act.wait_ge(s_labs, n + 1)
                act.activation(fexp[0:nq, 0:b - a], fexp[0:nq, 0:b - a], ACT.Exp, scale=-1.0).then_inc(s_lexp, 1)
                act.wait_ge(s_lexp, n + 1)
                act.activation(fexp[0:nq, 0:b - a], fexp[0:nq, 0:b - a], ACT.Ln, bias=1.0).then_inc(s_lln, 1)
                hi_w(t + 1, 0, s_mp, 2 * GA * t + GA)
                act.wait_ge(s_la, n + 1)
            with act.Fori(2 + len(FORGET), N_P) as t:
                hi_w(t, 1, s_mp, 2 * GA * t)
                hi_w(t + 1, 0, s_mp, 2 * GA * t + GA)

            hi_w(PASS_GATE, 1, s_mp, 2 * GA * N_P)
            act.wait_ge(s_mp, 2 * GA * N_P)
            act.wait_ge(s_bc, 48)
            act.activation(decay[:], decay_raw, ACT.Copy).then_inc(s_dcy, 1)
            act.wait_ge(s_clr, 4)

            def step(s, it, nq, kts, nch):
                lo, hi = kts[0] * P, P + nq
                nk = (P, nq)
                first = isinstance(it, int) and it == 0
                final = isinstance(it, int) and it == N_IT - 1

                if s == 0:
                    ge(act, s_pv, 4 * it)
                    if not first and not final:
                        act.activation(v_prev[:], v_cur[:], ACT.Copy).then_inc(s_vsh, 1)
                        act.wait_ge(s_vsh, it)
                    act.wait_ge(s_pt, N_T * it + 1)
                    act.activation(v_cur[0:nq], bank[2][0:nq, 0:256], ACT.Copy).then_inc(s_tev, 1)
                if 2 <= s < 10:
                    u = s - 2
                    act.wait_ge(s_pt, N_T * it + 2 + u)
                    gi = u // 2
                    if gi >= 2:
                        act.wait_ge(s_pv, 4 * it + gi - 1)
                    for kt in kts:
                        i = act.activation(pT[0:nk[kt], gi % 2, kt, 2 * (u % 2):2 * (u % 2) + 2, 0:nq],
                                           bank[2][0:nk[kt], :].rearrange("p (k i q) -> p k i q", k=2, i=2)[:, kt, :, 0:nq],
                                           ACT.Copy)
                    i.then_inc(s_tev, 1)
                if s < 8:
                    u = s
                    act.wait_ge(s_snm, 8 * it + u + 1)
                    ge(act, s_pt, N_T * it + u if u >= 2 else N_T * it)
                    for i in range(2):
                        act.activation(pb[0:nq, u % 2, i, lo:hi], s8[0:nq, u % 2, i, lo:hi], ACT.Exp,
                                       bias=nm[0:nq, u % 2, i:i + 1], scale=HEAD_DIM ** -0.5,
                                       accum_out=rsum[0:nq, u % 2, i:i + 1])
                    act.activation(esink[0:nq, u % 2], snm[0:nq, u % 2], ACT.Exp).then_inc(s_ep, 1)
                if s == 3:
                    act.wait_ge(s_qa, 16 * it + 16)
                    ge(act, s_z2, it)
                    act.activation(th[:, :, 0:nq], qa[:, 10:18, 0:nq], ACT.Tanh, scale=0.5).then_inc(s_tz, 1)
                if s == 8:
                    act.wait_ge(s_lac, 16 * it + 16)
                    act.activation(lac_hi[0:nq], lac[0:nq], ACT.Copy).then_inc(s_lch, 1)
                if s in (9, 11, 13, 15):
                    hh = (s - 9) // 2
                    ge(act, s_qk, 4 * it + hh - 1)
                    for c in range(nch):
                        act.wait_ge(s_e, 8 * it + nch * hh + c + 1)
                        act.activation(ex[:, hh % 2, c], bank[c][:, :].rearrange("p (b t) -> p b t", t=CHUNK),
                                       ACT.Exp).then_inc(s_ex, 1)
                if s in (10, 12):
                    half = (s - 10) // 2
                    act.wait_ge(s_pt, N_T * it + (10, 12)[half])
                    act.activation(vg[0:nq, half * 512:half * 512 + 512], bank[2][0:nq, :], ACT.Copy).then_inc(s_tev, 1)
                if s in (11, 13, 15, 17):
                    hh = (s - 11) // 2
                    act.wait_ge(s_pt, N_T * it + (11, 13, 14, 15)[hh])
                    for c in range(nch):
                        r = slice(c * CHUNK, (c + 1) * CHUNK)
                        i = act.activation(kt_tok[r, c, hh], bank[2][r, 0:GLA_DK], ACT.Copy)
                    i.then_inc(s_tev, 1)
                if s in (17, 21):
                    pair = (s - 17) // 4
                    act.wait_ge(s_o, 4 * it + nch * (pair + 1))
                    ps = bank[(3, 0)[pair]][:, :].rearrange("p (a b t) -> p a b t", a=2, b=2)[:, :, :, 0:nq]
                    a = slice(2 * pair, 2 * pair + 2)
                    act.activation(os_[:, a, :, 0:nq], ps, ACT.Copy, scale=GLA_DK ** -0.5)
                    act.activation(sq[:, a, :, 0:nq], ps, ACT.Square, scale=GLA_DK ** -0.5).then_inc(s_oev, 1)
                if s == 19:
                    act.wait_ge(s_gl, 16 * it + 16)
                    act.wait_ge(s_zs, it + 1)
                    act.activation(th[:, :, 0:nq], gl[:, 16:24, 0:nq], ACT.Tanh, scale=0.5).then_inc(s_tg, 1)

            def remake(p, pieces, unit):
                for j in pieces:
                    slot = j % XA_SLOTS
                    act.wait_ge(s_mg, 2 * unit + 1 + j // 4)
                    n = X_AGAIN * (p - 1) + j
                    act.wait_ge(s_xa[slot], 16 // XA_SLOTS * (n - slot) + 16)
                    for q in range(2):
                        i = act.activation(uh[0][:, 2 * j + q, :], xa_slot[slot][:, q], ACT.Copy, scale=pre(2 * j + q))
                    i.then_inc(s_uhi, 1)

            def gate_tanh(unit, m):
                act.wait_ge(s_gz, unit + 1)
                slot = m % 2
                ge(act, s_gst[slot], 8 * (unit - slot))
                act.activation(stage2[:, slot * GAW:(slot + 1) * GAW], stage[:, slot * GAW:(slot + 1) * GAW], ACT.Tanh,
                               bias=bg_half[:, m:m + 1], scale=0.5).then_inc(s_th, 1)

            def hi_branch(n):
                h, g, j = B_ORDER[n]
                k, w = h * HK + 2 * j, GRP[g][1]
                act.wait_ge(s_y[n % 4], 16 * (n // 4) + 16)
                for q in range(2):
                    i = act.activation(bh[g][:, k + q, 0:w], b_slot[n % 4][:, q, 0:w], ACT.Copy)
                i.then_inc(s_bhi, 1)

            def attend(it, p, m0, count, nxt=True, again=None, fresh=False):
                kts, nch, nq = shape_of(it)
                for steps, j in weave(2 * count, it):
                    m, h = m0 + j // 2, j % 2
                    unit = N_GATE * p + m
                    if h == 0:
                        if not (isinstance(unit, int) and unit == 0):
                            hi_w(PASS_GATE + unit, 1, s_mg, 2 * unit)
                    else:
                        hi_w(PASS_GATE + unit + 1, 0, s_mg, 2 * unit + 1)
                    for s in steps:
                        step(s, it, nq, kts, nch)
                    if fresh and j == 0:
                        remake(p, range(4, 8), unit - 1)
                    if h == 0 and not (isinstance(unit, int) and unit == 0):
                        gate_tanh(unit - 1, (m - 1) % N_GATE)
                    if again is not None and j == 2 * count - 1:
                        remake(again, range(0, 4), unit)
                    if it is None:
                        for n in range(B_SPLITS[j], B_SPLITS[j + 1]):
                            hi_branch(n)

            sequence(act, attend)
            gate_tanh(GA * N_GATE - 1, N_GATE - 1)

            hi_w(PASS_BRANCH, 1, s_mg, 2 * GA * N_GATE)
            for n in range(B_EARLY, NB):
                hi_branch(n)
            hi_w(PASS_BRANCH + 1, 0, s_mb, 3)
            with act.Fori(1, N_OUT - 1) as m:
                hi_w(PASS_BRANCH + m, 1, s_mb, 6 * m)
                hi_w(PASS_BRANCH + m + 1, 0, s_mb, 6 * m + 3)

            def hi_merged(*pieces):
                for n in pieces:
                    h, g, j = M_ORDER[n]
                    if n < NG:
                        act.wait_ge(s_mb, 6 * (N_OUT - 1) + 3 * h + 1)
                    hi_piece(n, s_z, s_mhi, mh[g], h * HK + 2 * j, GRP[g][1], lambda k: 0.5)

            hi_w(PASS_OUT - 1, 1, s_mb, 6 * (N_OUT - 1))
            hi_merged(0, 1, 2, 3)
            hi_w(PASS_OUT, 0, s_mb, 6 * (N_OUT - 1) + 3)
            hi_merged(4, 5)
            hi_w(PASS_OUT, 1, s_mb, 6 * N_OUT)
            hi_merged(6, 7)

            def tile(g, m, r):
                n = g * KT + m
                if not isinstance(n, int) or n < 3 * KT - 1:
                    hi_w(PASS_OUT + n + 1, 0, s_mo, 2 * n + 1)
                if g == 0 and m > 0:
                    hi_merged(*merged_pieces(m))
                if not isinstance(n, int) or n < 3 * KT - 1:
                    hi_w(PASS_OUT + n + 1, 1, s_mo, 2 * n + 2)
                act.wait_ge(s_mo, 2 * n + 2)
                settle(act)
                act.activation(out_sb[g][:, bass.ds(m, 1), 0:GRP[g][1]], bank[r][:, 0:GRP[g][1]].unsqueeze(1),
                               ACT.Copy).then_inc(s_oev2, 1)

            for m in range(KT):
                tile(0, m, m % 2)
            for g in (1, 2):
                def pair(i):
                    for r in range(2):
                        tile(g, 2 * i + r, r)

                pair(0)
                with act.Fori(1, KT // 2 - 1) as i:
                    pair(i)
                pair(KT // 2 - 1)

        @block.gpsimd
        def _(pool):
            pool.memset(ssq[:], 0.0).then_inc(s_ssq, 1)
            pool.memset(minus_half[:], -0.5).then_inc(s_pset, 1)
            pool.memset(mean[:], 1.0).then_inc(s_pset, 1)
            pool.wait_ge(s_pset, 2)
            pool.wait_ge(s_ssq, 1)
            for n, (h, g, j) in enumerate(X_ORDER):
                pool.wait_ge(s_sqx, n + 1)
                for q in range(2):
                    pool.tensor_tensor(ssq[:, g], ssq[:, g], sqx[:, n % 2, q], ALU.add).then_inc(s_ssq, 1)
                    pool.wait_ge(s_ssq, 2 * n + q + 2)

            def roots(n, count):
                pool.wait_ge(s_rst, 2 * n + 2)
                pool.tensor_tensor(root[:, 0:count], mean[:, 0:count], minus_half[:].to_broadcast([P, count]), ALU.pow).then_inc(s_rsp, 1)

            def gla_roots(it, nq=P):
                pool.wait_ge(s_var, it + 1)
                ge(pool, s_gdg, it)
                pool.tensor_tensor(groot[0:nq], gmean[0:nq], minus_half[0:nq].to_broadcast([nq, GLA_HEADS]), ALU.pow).then_inc(s_gpw, 1)

            roots(0, N_IT)
            pool.wait_ge(s_last, 16 * len(FORGET))
            pool.memset(kw[:], 0.0).then_inc(s_clr, 1)
            pool.wait_ge(s_mp, 2 * GA * N_P)
            pool.memset(st[:, 0], 0.0).then_inc(s_clr, 1)
            pool.memset(kt_tok[:], 0.0).then_inc(s_clr, 1)
            pool.memset(gsc[:], 0.0).then_inc(s_clr, 1)
            gla_roots(0)
            with pool.Fori(1, N_IT - 1) as it:
                gla_roots(it)
            gla_roots(N_IT - 1, DEC)
            for n in range(3):
                roots(n + 1, 3)
            w = GRP[2][1]
            for k in range(1, KT, 2):
                pool.wait_ge(s_sc2, k + 1)
                if k == 1:
                    pool.wait_ge(s_xl, 16 * KT // 4)
                pool.tensor_tensor(out_sb[2][:, k, 0:w], out_sb[2][:, k, 0:w], x_last[:, k, 0:w], ALU.add).then_inc(s_add[1], 1)

        @block.vector
        def _(dve):
            def lo_w(p, h):
                dve.wait_ge(s_whi, 2 * p + h + 1)
                dve.tensor_tensor(w_lo[:, h], w_raw[:, h], w_hi[:, h].bitcast(f32), ALU.subtract).then_inc(s_wlo, 1)

            def lo_piece(n, hi_done, done, hi_t, out, k, w, scale):
                dve.wait_ge(hi_done, n + 1)
                slot = k // 2 % 2
                for q in range(2):
                    i = dve.scalar_tensor_tensor(out=out[:, k + q, 0:w], in0=ring[:, slot, q, 0:w], scalar=scale(k + q),
                                                 in1=hi_t[:, k + q, 0:w].bitcast(f32), op0=ALU.mult, op1=ALU.subtract)
                i.then_inc(done, 1)

            dve.memset(ones[:], 1.0).then_inc(s_cset, 1)
            dve.memset(wlr[:].bitcast(f32), 0.0).then_inc(s_cset, 1)
            dve.memset(lr[:], 0.0).then_inc(s_cset, 1)
            dve.wait_ge(s_cset, 3)
            dve.memset(lr[2 * RANK:2 * RANK + 1, :], 1.0).then_inc(s_cset, 1)
            dve.wait_ge(s_lrhi, 1)
            dve.tensor_tensor(wlr[:, :, RANK:2 * RANK], wlr_raw[:], wlr[:, :, 0:RANK].bitcast(f32), ALU.subtract).then_inc(s_lrlo, 1)
            pre = lambda k: norm_sb[:, 0, k:k + 1]
            dve.wait_ge(s_norm, 16)
            for n, (h, g, j) in enumerate(X_ORDER):
                slot, k = n % X_SLOTS, h * HK + 2 * j
                dve.wait_ge(s_x[slot], 16 * (n // X_SLOTS) + 16)
                ge(dve, s_ssq, 2 * n - 1)
                dve.tensor_tensor(sqx[:, n % 2], x_slot[slot], x_slot[slot], ALU.mult).then_inc(s_sqx, 1)
                dve.wait_ge(s_uhi, n + 1)
                for q in range(2):
                    i = dve.scalar_tensor_tensor(out=ul[g][:, k + q, :], in0=x_slot[slot][:, q], scalar=pre(k + q),
                                                 in1=uh[g][:, k + q, :].bitcast(f32), op0=ALU.mult, op1=ALU.subtract)
                i.then_inc(s_ulo, 1)
                if n == 0:
                    lo_w(0, 0)
                if n == NX // 2 - 3:
                    lo_w(0, 1)
            dve.wait_ge(s_const, 16 * 4)
            dve.tensor_scalar(bg_half[:], bg_sb[:], 0.5, None, ALU.mult).then_inc(s_cset, 1)
            dve.tensor_scalar(gn_half[:], gn_sb[:], 0.5, None, ALU.mult).then_inc(s_cset, 1)
            dve.tensor_scalar(nsink_sb[:], sink_sb[:], -1.0, None, ALU.mult).then_inc(s_cset, 1)

            def roots(n, w, ps):
                if n == 0:
                    dve.wait_ge(s_pset, 2)
                full, rest = w // P, w % P
                dve.wait_ge(s_ones, n + 1)
                dve.tensor_scalar(mean[:, 0:full], ps[:, 0:full], 1.0 / D_MODEL, EPS, ALU.mult, ALU.add).then_inc(s_rst, 1)
                dve.tensor_scalar(mean[0:rest, full:full + 1], ps[0:rest, full:full + 1], 1.0 / D_MODEL, EPS, ALU.mult, ALU.add).then_inc(s_rst, 1)
                dve.wait_ge(s_rsp, n + 1)
                for i, t, size in blocks(w):
                    ins = dve.tensor_scalar(diag[0:size, i], ident[0:size], root[0:size, i:i + 1], None, ALU.mult)
                ins.then_inc(s_dg, 1)

            def spread(n, w, ps, out):
                dve.wait_ge(s_spread, n + 1)
                for b in range(-(-w // 512)):
                    t, size = b * 512, min(512, w - b * 512)
                    dve.tensor_copy(out[:, t:t + size], ps[b][:, 0:size]).then_inc(s_rstd, 1)

            for g, a in quarter:
                dve.wait_ge(s_lrp, GA + g + 1)
                dve.tensor_copy(lr[0:2 * RANK, a:a + GAW], bank[4 + g][0:2 * RANK, 0:GAW]).then_inc(s_lrc, 1)
            lo_w(1, 0)
            roots(0, TOKENS, bank[4])
            spread(0, TOKENS, bank[4:7], rstd)

            def evacuate(tile):
                ge(dve, s_st, 16 * tile)
                for g, a in quarter:
                    dve.wait_ge(s_mp, 2 * GA * tile + GA + g + 1)
                    dve.tensor_tensor(stage[:, a:a + GAW], bank[g][:, 0:GAW], rstd[:, a:a + GAW], ALU.mult).then_inc(s_ev, 1)

            dve.wait_ge(s_rstd, 3)
            evacuate(0)
            dve.wait_ge(s_lrc, GA)
            dve.tensor_tensor(lr[0:2 * RANK], lr[0:2 * RANK], rstd[0:2 * RANK], ALU.mult).then_inc(s_lr, 1)
            lo_w(1, 1)
            lo_w(2, 0)
            evacuate(1)
            for n, t in enumerate(range(2, 2 + len(FORGET))):
                lo_w(t, 1)
                a, b = FORGET[n]
                nq = P if b < N_IT else DEC
                for i in range(b - a):
                    dve.wait_ge(s_lap, a + i + 1)
                    ge(dve, s_last, 16 * n)
                    dve.tensor_scalar(fmin[0:nq, i], bank[4 + i][0:nq, :], 0.0, 1.0 / TAU, ALU.min, ALU.mult).then_inc(s_lmin, 1)
                dve.wait_ge(s_lmin, b)
                dve.wait_ge(s_lln, n + 1)
                dve.scalar_tensor_tensor(out=fmin[0:nq, 0:b - a], in0=fexp[0:nq, 0:b - a], scalar=-1.0 / TAU, in1=fmin[0:nq, 0:b - a],
                                         op0=ALU.mult, op1=ALU.add).then_inc(s_la, 1)
                lo_w(t + 1, 0)
                evacuate(t)
            with dve.Fori(2 + len(FORGET), N_P) as t:
                lo_w(t, 1)
                lo_w(t + 1, 0)
                evacuate(t)

            lo_w(PASS_GATE, 1)
            dve.wait_ge(s_mp, 2 * GA * N_P)
            dve.wait_ge(s_bc, 48)
            for h in range(HEADS):
                dve.tensor_scalar(bias[:, h], dist, -alibi_slope(h) * HEAD_DIM ** 0.5, None, ALU.mult).then_inc(s_bias, 1)
            dve.wait_ge(s_bias, HEADS)

            def step(s, it, nq, kts, nch):
                lo, hi = kts[0] * P, P + nq
                first = isinstance(it, int) and it == 0
                final = isinstance(it, int) and it == N_IT - 1

                def silu_twice(s_tanh, src, done):
                    dve.wait_ge(s_tanh, it + 1)
                    dve.scalar_tensor_tensor(out=zs[:, :, 0:nq], in0=th[:, :, 0:nq], scalar=1.0, in1=src,
                                             op0=ALU.add, op1=ALU.mult).then_inc(done, 1)

                if 1 <= s < 9:
                    u = s - 1
                    dve.wait_ge(s_ep, 8 * it + u + 1)
                    dve.tensor_tensor(den[0:nq, u % 2], rsum[0:nq, u % 2], esink[0:nq, u % 2], ALU.add).then_inc(s_den, 1)
                    dve.wait_ge(s_den, 8 * it + u + 1)
                    dve.reciprocal(rden[0:nq, u % 2], den[0:nq, u % 2]).then_inc(s_rden, 1)
                    dve.wait_ge(s_rden, 8 * it + u + 1)
                    for i in range(2):
                        ins = dve.tensor_scalar(pb[0:nq, u % 2, i, lo:hi], pb[0:nq, u % 2, i, lo:hi],
                                                rden[0:nq, u % 2, i:i + 1], None, ALU.mult)
                    ins.then_inc(s_pr, 1)
                if s < 8:
                    u = s
                    h0 = head0(u)
                    dve.wait_ge(s_sc, 8 * it + u + 1)
                    ge(dve, s_ep, 8 * it + u - 1)
                    if u < 2:
                        ge(dve, s_og, 2 * it)
                    settle(dve)
                    for i in range(2):
                        ins = dve.tensor_tensor_reduce(
                            out=s8[0:nq, u % 2, i, lo:hi], in0=bank[u % 2][0:nq, :].rearrange("p (i k) -> p i k", i=2)[:, i, lo:hi],
                            in1=bias[0:nq, h0 + i, lo:hi], scale=1.0, scalar=-3e38, op0=ALU.add, op1=ALU.max,
                            accum_out=m8[0:nq, u % 2, i:i + 1])
                    ins.then_inc(s_a, 1)
                    dve.wait_ge(s_a, 8 * it + u + 1)
                    dve.scalar_tensor_tensor(out=nm[0:nq, u % 2], in0=m8[0:nq, u % 2], scalar=-HEAD_DIM ** -0.5,
                                             in1=nsink_sb[0:nq, h0:h0 + 2], op0=ALU.mult, op1=ALU.min).then_inc(s_nm, 1)
                    dve.wait_ge(s_nm, 8 * it + u + 1)
                    dve.tensor_tensor(snm[0:nq, u % 2], nm[0:nq, u % 2], sink_sb[0:nq, h0:h0 + 2], ALU.add).then_inc(s_snm, 1)
                if s == 5:
                    silu_twice(s_tz, qa[:, 10:18, 0:nq], s_zs)
                if s in (7, 11):
                    tt = (s - 7) // 4
                    dve.wait_ge(s_pv, 4 * it + 2 * tt + 2)
                    dve.wait_ge(s_zs, it + 1)
                    ge(dve, s_ogst, 16 * it)
                    dve.scalar_tensor_tensor(out=ob[:, 4 * tt:4 * tt + 4, 0:nq],
                                             in0=bank[3][:, :].rearrange("p (j q) -> p j q", j=GROUP)[:, :, 0:nq],
                                             scalar=0.5, in1=zs[:, 4 * tt:4 * tt + 4, 0:nq],
                                             op0=ALU.mult, op1=ALU.mult).then_inc(s_oa, 1)
                if s == 8:
                    dve.wait_ge(s_lch, it + 1)
                    dve.tensor_tensor(lac_lo[0:nq], lac[0:nq], lac_hi[0:nq].bitcast(f32), ALU.subtract).then_inc(s_lcl, 1)
                if s in (10, 12, 14, 16):
                    hh = (s - 10) // 2
                    dve.wait_ge(s_ex, 8 * it + nch * (hh + 1))
                    ge(dve, s_pt, N_T * it + ((0, 0, 11, 13)[hh]))
                    ge(dve, s_o, 4 * it)
                    if hh == 0:
                        dve.wait_ge(s_gl, 16 * it + 16)
                    e = ex[:, hh % 2, 0:nch]
                    q, k = (gl[:, t + hh, 0:nq].rearrange("p (c t) -> p c t", t=CHUNK) for t in (0, 4))
                    wide = [P, nch, LEVELS, CHUNK]
                    dve.tensor_copy(ebend[:, hh, 0:nch].unsqueeze(2), e[:, :, 0, CHUNK - 1:CHUNK])
                    dve.tensor_tensor(qb[:, hh, 0:nch], e[:, :, 0], q, ALU.mult)
                    dve.tensor_tensor(kend[:, hh % 2, 0:nch], e[:, :, 7], k, ALU.mult)
                    dve.tensor_tensor(qe[:, hh % 2, 0:nch], e[:, :, 1:7], q.unsqueeze(2).to_broadcast(wide), ALU.mult)
                    dve.tensor_tensor(ke[:, hh % 2, 0:nch], e[:, :, 1:7], k.unsqueeze(2).to_broadcast(wide), ALU.mult).then_inc(s_qk, 1)
                if s in (11, 13, 15, 17):
                    hh = (s - 11) // 2
                    dve.wait_ge(s_gs, 4 * it + hh + 1)
                    ge(dve, s_gr, 4 * it + hh)
                    if first and hh == 0:
                        dve.wait_ge(s_clr, 4)
                    dve.tensor_tensor(tm[0:nq], bank[4][0:nq, 0:7 * CHUNK].rearrange("p (l t) -> p l t", l=7),
                                      mask[0:nq], ALU.mult).then_inc(s_gm, 1)
                    dve.wait_ge(s_gm, 4 * it + hh + 1)
                    for c in range(nch):
                        r = slice(c * CHUNK, (c + 1) * CHUNK)
                        ins = dve.tensor_reduce(gsc[r, hh, c], tm[r].rearrange("p l t -> p t l"), AX.X, ALU.add)
                    ins.then_inc(s_gr, 1)
                if s in ((14, 16, 18, 20) if nch == 2 else (14, 18)):
                    pair, c = (s - 14) // 4, (s - 14) // 2 % 2
                    n = nch * pair + c
                    if final and pair == 0:
                        dve.wait_ge(s_sld, 16)
                    dve.wait_ge(s_ds, 4 * it + n + 1)
                    ge(dve, s_o, 4 * it + (n if c else 0))
                    ge(dve, s_su, 8 * it + 2 * n)
                    if first and n == 0:
                        dve.wait_ge(s_clr, 4)
                    for i in range(2):
                        hh = 2 * pair + i
                        dve.scalar_tensor_tensor(
                            out=st[:, 1 - c, hh], in0=st[:, c, hh], scalar=ebend[:, hh, c:c + 1],
                            in1=bank[5][:, :].rearrange("p (i v) -> p i v", i=2)[:, i],
                            op0=ALU.mult, op1=ALU.add).then_inc(s_su, 1)
                if s == 19:
                    silu_twice(s_tg, gl[:, 16:24, 0:nq], s_z2)
                if s == 22:
                    dve.wait_ge(s_rm, it + 1)
                    ge(dve, s_gpw, it)
                    dve.tensor_scalar(gmean[0:nq], bank[5][0:nq, 0:GLA_HEADS], 1.0 / GLA_DV, EPS, ALU.mult, ALU.add).then_inc(s_var, 1)
                if s == 23:
                    dve.wait_ge(s_gpw, it + 1)
                    ge(dve, s_rb, it)
                    for hh in range(GLA_HEADS):
                        ins = dve.tensor_scalar(gdiag[0:nq, hh], ident[0:nq], groot[0:nq, hh:hh + 1], None, ALU.mult)
                    ins.then_inc(s_gdg, 1)
                if s == 24:
                    dve.wait_ge(s_rb, it + 1)
                    ps = bank[1][:, :].rearrange("p (a q) -> p a q", a=GLA_HEADS)[:, :, 0:nq]
                    dve.tensor_tensor(os_[:, :, :, 0:nq], os_[:, :, :, 0:nq],
                                      ps.unsqueeze(2).to_broadcast([P, GLA_HEADS, 2, nq]), ALU.mult).then_inc(s_t1, 1)
                if s == 25:
                    dve.wait_ge(s_t1, it + 1)
                    dve.wait_ge(s_z2, it + 1)
                    dve.wait_ge(s_oast, 16 * it + 16)
                    for vh in range(2):
                        dve.scalar_tensor_tensor(out=ob[:, :, 0:nq].rearrange("p (a b) q -> p a b q", b=2)[:, :, vh],
                                                 in0=zs[:, :, 0:nq].rearrange("p (a b) q -> p a b q", b=2)[:, :, vh],
                                                 scalar=gn_half[:, vh:vh + 1], in1=os_[:, :, vh, 0:nq],
                                                 op0=ALU.mult, op1=ALU.mult).then_inc(s_og, 1)

            def remake(p, pieces):
                for j in pieces:
                    dve.wait_ge(s_uhi, NX + X_AGAIN * (p - 1) + j + 1)
                    for q in range(2):
                        k = 2 * j + q
                        i = dve.scalar_tensor_tensor(out=ul[0][:, k, :], in0=xa_slot[j % XA_SLOTS][:, q], scalar=pre(k),
                                                     in1=uh[0][:, k, :].bitcast(f32), op0=ALU.mult, op1=ALU.subtract)
                    i.then_inc(s_ulo, 1)

            def scale_gate(unit, p, m):
                dve.wait_ge(s_mg, 2 * unit + 2)
                ge(dve, s_th, unit - 1)
                if isinstance(unit, int) and unit < 2:
                    dve.wait_ge(s_st, 16 * N_P)
                if not isinstance(unit, int):
                    settle(dve)
                slot = m % 2
                dve.tensor_tensor(stage[:, slot * GAW:(slot + 1) * GAW], bank[6 + slot][:, 0:GAW],
                                  rows[:, p * GAW:(p + 1) * GAW] if isinstance(p, int) else rows[:, bass.ds(p * GAW, GAW)],
                                  ALU.mult).then_inc(s_gz, 1)

            def lo_branch(n):
                h, g, j = B_ORDER[n]
                k, w = h * HK + 2 * j, GRP[g][1]
                dve.wait_ge(s_bhi, n + 1)
                for q in range(2):
                    i = dve.tensor_tensor(bl[g][:, k + q, 0:w], b_slot[n % 4][:, q, 0:w], bh[g][:, k + q, 0:w].bitcast(f32), ALU.subtract)
                i.then_inc(s_blo, 1)

            def attend(it, p, m0, count, nxt=True, again=None, fresh=False):
                kts, nch, nq = shape_of(it)
                for steps, j in weave(2 * count, it):
                    m, h = m0 + j // 2, j % 2
                    unit = N_GATE * p + m
                    early = 0
                    while early < len(steps) and steps[early] not in LATE:
                        step(steps[early], it, nq, kts, nch)
                        early += 1
                    if h == 0:
                        if not (isinstance(unit, int) and unit == 0):
                            lo_w(PASS_GATE + unit, 1)
                            if m > 0:
                                scale_gate(unit - 1, p, m - 1)
                            else:
                                scale_gate(unit - 1, p - 1, N_GATE - 1)
                    else:
                        lo_w(PASS_GATE + unit + 1, 0)
                    for s in steps[early:]:
                        step(s, it, nq, kts, nch)
                    if fresh and j == 0:
                        remake(p, range(4, 8))
                    if again is not None and j == 2 * count - 1:
                        remake(again, range(0, 4))
                    if it is None:
                        for n in range(B_SPLITS[j], B_SPLITS[j + 1]):
                            lo_branch(n)

            sequence(dve, attend)
            scale_gate(GA * N_GATE - 1, GA - 1, N_GATE - 1)

            lo_w(PASS_BRANCH, 1)
            for n in range(B_EARLY, NB):
                lo_branch(n)

            def weigh(m, c):
                a, w = GRP[c]
                dve.wait_ge(s_mb, 6 * m + 1 + c)
                ge(dve, s_yg, 3 * m)
                dve.scalar_tensor_tensor(out=ya[:, a:a + w], in0=gate[:, 0, a:a + w], scalar=1.0, in1=bank[c][:, 0:w],
                                         op0=ALU.add, op1=ALU.mult).then_inc(s_ya, 1)

            def merge(m, c):
                a, w = GRP[c]
                dve.wait_ge(s_mb, 6 * m + 4 + c)
                dve.scalar_tensor_tensor(out=stage2[:, a:a + w], in0=gate[:, 1, a:a + w], scalar=1.0,
                                         in1=bank[3 + c][:, 0:w], op0=ALU.add, op1=ALU.mult).then_inc(s_y2, 1)
                dve.wait_ge(s_y2, 3 * m + c + 1)
                dve.wait_ge(s_ya, 3 * m + c + 1)
                dve.tensor_tensor(stage[:, a:a + w], ya[:, a:a + w], stage2[:, a:a + w], ALU.add).then_inc(s_yg, 1)

            def branch(m):
                dve.wait_ge(s_g[0], 16 * m + 16)
                for c in range(3):
                    weigh(m, c)
                lo_w(m + PASS_BRANCH + 1, 0)
                dve.wait_ge(s_g[1], 16 * m + 16)
                ge(dve, s_mst, 16 * m)
                for c in range(3):
                    merge(m, c)
                lo_w(m + PASS_BRANCH + 1, 1)

            dve.wait_ge(s_blo, NB)
            branch(0)
            with dve.Fori(1, N_OUT - 1) as m:
                branch(m)

            def lo_merged(*pieces):
                for n in pieces:
                    h, g, j = M_ORDER[n]
                    lo_piece(n, s_mhi, s_mlo, mh[g], ml[g], h * HK + 2 * j, GRP[g][1], lambda k: 0.5)

            last = N_OUT - 1
            dve.wait_ge(s_g[0], 16 * last + 16)
            weigh(last, 0)
            lo_merged(0)
            weigh(last, 1)
            lo_merged(1)
            weigh(last, 2)
            lo_w(PASS_OUT, 0)
            lo_merged(2, 3)
            dve.wait_ge(s_g[1], 16 * last + 16)
            dve.wait_ge(s_mst, 16 * last)
            merge(last, 0)
            lo_merged(4, 5)
            merge(last, 1)
            lo_w(PASS_OUT, 1)
            lo_merged(6, 7)
            merge(last, 2)

            def finish(g, k, n, slot):
                w = GRP[g][1]
                y, x = stage2[:, slot * GW:slot * GW + w], stage[:, slot * GW:slot * GW + w]
                ge(dve, s_yst[slot], 8 * (n - slot))
                settle(dve)
                dve.scalar_tensor_tensor(out=y.unsqueeze(1), in0=out_sb[g][:, bass.ds(k, 1), 0:w],
                                         scalar=norm_sb[:, 1, bass.ds(k, 1)], in1=rso[:, 0:w].unsqueeze(1),
                                         op0=ALU.mult, op1=ALU.mult).then_inc(s_fin, 1)
                dve.wait_ge(s_fin, 2 * n + 1)
                dve.wait_ge(s_xo[slot], 8 * (n - slot) + 16)
                dve.tensor_tensor(y, y, x, ALU.add).then_inc(s_fin, 1)

            def clear_sums(g):
                dve.memset(ssqo, 0.0).then_inc(s_ssz, 1)
                dve.wait_ge(s_ssz, g + 1)

            clear_sums(0)
            for g in range(3):
                w = GRP[g][1]

                def tile(m, r):
                    n = g * KT + m
                    behind = g > 0 and isinstance(m, int) and m == 0
                    if behind:
                        roots(g, GRP[g - 1][1], bank[6])
                        clear_sums(g)
                    if not isinstance(n, int) or n < 3 * KT - 1:
                        lo_w(PASS_OUT + n + 1, 0)
                    if behind:
                        spread(g, GRP[g - 1][1], bank[6:7], rso)
                        dve.wait_ge(s_rstd, 3 + g)
                    if g > 0:
                        finish(g - 1, m, (g - 1) * KT + m, r)
                    elif m > 0:
                        lo_merged(*merged_pieces(m))
                    if not isinstance(n, int) or n < 3 * KT - 1:
                        lo_w(PASS_OUT + n + 1, 1)
                    dve.wait_ge(s_oev2, n + 1)
                    settle(dve)
                    src = out_sb[g][:, bass.ds(m, 1), 0:w]
                    dve.tensor_tensor(sqo[:, 0:w].unsqueeze(1), src, src, ALU.mult).then_inc(s_sqo, 1)
                    dve.wait_ge(s_sqo, 2 * n + 1)
                    dve.tensor_tensor(ssqo[:, 0:w], ssqo[:, 0:w], sqo[:, 0:w], ALU.add).then_inc(s_sqo, 1)
                    dve.wait_ge(s_sqo, 2 * n + 2)

                if g == 0:
                    for m in range(KT):
                        tile(m, m % 2)
                else:
                    for m in range(2):
                        tile(m, m)
                    with dve.Fori(1, KT // 2 - 1) as i:
                        for r in range(2):
                            tile(2 * i + r, r)
                    for m in range(KT - 2, KT):
                        tile(m, m % 2)
            roots(3, GRP[2][1], bank[6])
            spread(3, GRP[2][1], bank[6:7], rso)
            dve.wait_ge(s_rstd, 6)
            w = GRP[2][1]
            for k in range(KT):
                dve.scalar_tensor_tensor(out=out_sb[2][:, k, 0:w], in0=out_sb[2][:, k, 0:w], scalar=norm_sb[:, 1, k:k + 1],
                                         in1=rso[:, 0:w], op0=ALU.mult, op1=ALU.mult).then_inc(s_sc2, 1)
                if k % 2 == 0:
                    dve.wait_ge(s_sc2, k + 1)
                    if k == 0:
                        dve.wait_ge(s_xl, 16 * KT // 4)
                    dve.tensor_tensor(out_sb[2][:, k, 0:w], out_sb[2][:, k, 0:w], x_last[:, k, 0:w], ALU.add).then_inc(s_add[0], 1)

        @block.tensor
        def _(pe):
            def products(out, h, hi_t, lo_t, w, done, start, stop):
                for k in range(HK):
                    for j, (wt, ut) in enumerate(((w_hi, hi_t), (w_hi, lo_t), (w_lo, hi_t))):
                        ins = pe.matmul(out[:, 0:w], wt[:, h, k, :], ut[:, h * HK + k, 0:w],
                                        start=start and k == 0 and j == 0, stop=stop and k == HK - 1 and j == 2)
                ins.then_inc(done, 1)

            pe.wait_ge(s_lrlo, 1)
            for h in range(2):
                pe.wait_ge(s_wlo, h + 1)
                for g in range(GA):
                    pe.wait_ge(s_ulo, 4 * (GA * h + g) + 4)
                    for k in range(HK):
                        for j, ut in enumerate((uh, ul)):
                            ins = pe.matmul(bank[4 + g][:, 0:GAW], wlr[:, h * HK + k, :], ut[g][:, h * HK + k, 0:GAW],
                                            start=h == 0 and k == 0 and j == 0, stop=h == 1 and k == HK - 1 and j == 1)
                    ins.then_inc(s_lrp, 1)
                    products(bank[g], h, uh[g], ul[g], GAW, s_mp, h == 0, h == 1)

            def token_sums(w, ps, sums):
                for i, t, size in blocks(w):
                    ins = pe.matmul(ps[0:size, i:i + 1], sums[:, t:t + size], ones[:, 0:1], start=True, stop=True)
                ins.then_inc(s_ones, 1)

            def spread_roots(n, w, ps):
                pe.wait_ge(s_dg, n + 1)
                for i, t, size in blocks(w):
                    ins = pe.matmul(ps[t // 512][:, t % 512:t % 512 + size], ones[0:size, :], diag[0:size, i, 0:size], start=True, stop=True)
                ins.then_inc(s_spread, 1)

            pe.wait_ge(s_cset, 4)
            pe.wait_ge(s_ssq, 2 * NX + 1)
            pe.wait_ge(s_lrc, GA)
            token_sums(TOKENS, bank[4], ssq[:].rearrange("p g t -> p (g t)"))
            spread_roots(0, TOKENS, bank[4:7])

            def project(tile):
                for h in range(2):
                    pe.wait_ge(s_wlo, 2 * tile + h + 1)
                    for g in range(GA):
                        if h == 0:
                            pe.wait_ge(s_ev, GA * (tile - 1) + g + 1)
                        products(bank[g], h, uh[g], ul[g], GAW, s_mp, h == 0, h == 1)

            def forget_products(n):
                a, b = FORGET[n]
                nq = P if b < N_IT else DEC
                ge(pe, s_labs, n)
                for i in range(b - a):
                    t = (a + i) * P
                    pe.matmul(bank[4 + i][0:nq, :], lr[:, t:t + nq], wup[:], start=True, stop=True).then_inc(s_lap, 1)

            for t in range(1, 1 + len(FORGET)):
                project(t)
                if t == 1:
                    pe.wait_ge(s_wup, 16)
                    pe.wait_ge(s_lr, 1)
                    pe.wait_ge(s_rstd, 3)
                forget_products(t - 1)
            with pe.Fori(1 + len(FORGET), N_P) as t:
                project(t)

            pe.wait_ge(s_labs, len(FORGET))
            pe.wait_ge(s_ev, GA * N_P)

            def step(s, it, nq, kts, nch):
                nk = (P, nq)
                first = isinstance(it, int) and it == 0
                final = isinstance(it, int) and it == N_IT - 1

                if s == 0:
                    pe.wait_ge(s_qa, 16 * it + 16)
                    ge(pe, s_tev, N_T * it)
                    for i in range(2):
                        ins = pe.transpose(bank[2][0:nq, i * P:(i + 1) * P], qa[:, T_V + i, 0:nq], ident[:])
                    ins.then_inc(s_pt, 1)
                    pe.wait_ge(s_kw, 32 * it + (64 if final else 32))
                if 2 <= s < 10:
                    u = s - 2
                    pe.wait_ge(s_pr, 8 * it + u + 1)
                    pe.wait_ge(s_tev, N_T * it + 1 + u)
                    dst = bank[2][:, :].rearrange("p (k i q) -> p k i q", k=2, i=2)
                    for kt in kts:
                        for i in range(2):
                            ins = pe.transpose(dst[0:nk[kt], kt, i, 0:nq], pb[0:nq, u % 2, i, kt * P:kt * P + nk[kt]], ident[0:nq, 0:nq])
                    ins.then_inc(s_pt, 1)
                if s < 8:
                    u = s
                    tile, half = tiles(u)
                    if u >= 2:
                        pe.wait_ge(s_a, 8 * it + u - 1)
                    elif u == 0:
                        ge(pe, s_oev, 2 * it)
                    else:
                        ge(pe, s_t1, it)
                    c0 = kts[0] * P
                    for i in range(2):
                        ins = pe.matmul(bank[u % 2][0:nq, :].rearrange("p (i k) -> p i k", i=2)[:, i, c0:P + nq],
                                        qa[:, tile + i, 0:nq], kw[:, half, tile // 4, c0:P + nq], start=True, stop=True)
                    ins.then_inc(s_sc, 1)
                if s in (4, 6, 8, 10):
                    gi = (s - 4) // 2
                    half, tt = gi % 2, gi // 2
                    g = 2 * tt + half
                    pe.wait_ge(s_tev, N_T * it + 3 + 2 * gi)
                    if gi == 0:
                        ge(pe, s_oev, 2 * it)
                        if final:
                            pe.wait_ge(s_vp, 16)
                    if gi == 2:
                        pe.wait_ge(s_oa, 2 * it + 1)
                    for kt in kts:
                        v = (v_prev, v_cur)[kt]
                        ins = pe.matmul(bank[3][half * HEAD_DIM:(half + 1) * HEAD_DIM, :].rearrange("p (j q) -> p j q", j=GROUP)[:, :, 0:nq],
                                        v[0:nk[kt], g * HEAD_DIM:(g + 1) * HEAD_DIM], pT[0:nk[kt], gi % 2, kt, :, 0:nq],
                                        start=kt == kts[0], stop=kt == kts[-1])
                    ins.then_inc(s_pv, 1)
                if s in (9, 11, 13, 15):
                    hh = (s - 9) // 2
                    if hh == 0:
                        pe.wait_ge(s_lcl, it + 1)
                        if first:
                            pe.wait_ge(s_dcy, 1)
                    d = slice(hh * GLA_DK, (hh + 1) * GLA_DK)
                    for c in range(nch):
                        if hh == 0:
                            pe.wait_ge(s_a, 8 * it + 7 + c)
                        else:
                            pe.wait_ge(s_ex, 8 * it + nch * (hh - 1) + c + 1)
                        pe.matmul(bank[c][:, :], lac_hi[0:nq, d], decay[0:nq, c], start=True, stop=False)
                        pe.matmul(bank[c][:, :], lac_lo[0:nq, d], decay[0:nq, c], start=False, stop=True).then_inc(s_e, 1)
                if s in (10, 12):
                    half = (s - 10) // 2
                    pe.wait_ge(s_gl, 16 * it + 16)
                    pe.wait_ge(s_tev, N_T * it + (9, 11)[half])
                    for i in range(4):
                        ins = pe.transpose(bank[2][0:nq, i * P:(i + 1) * P], gl[:, 8 + 4 * half + i, 0:nq], ident[:])
                    ins.then_inc(s_pt, 1)
                if s in (11, 13, 15, 17):
                    hh = (s - 11) // 2
                    pe.wait_ge(s_qk, 4 * it + hh + 1)
                    ge(pe, s_gm, 4 * it + hh)
                    for c in range(nch):
                        r = slice(c * CHUNK, (c + 1) * CHUNK)
                        for l in range(LEVELS):
                            pe.matmul(bank[4][r, l * CHUNK:(l + 1) * CHUNK], ke[:, hh % 2, c, l], qe[:, hh % 2, c, l], start=True, stop=True)
                        ins = pe.matmul(bank[4][r, 6 * CHUNK:7 * CHUNK], gl[:, 4 + hh, r], gl[:, hh, r], start=True, stop=True)
                    ins.then_inc(s_gs, 1)
                    pe.wait_ge(s_tev, N_T * it + (10, 12, 13, 14)[hh])
                    pe.transpose(bank[2][0:nq, 0:GLA_DK], kend[:, hh % 2, 0:nch].rearrange("p c t -> p (c t)"), ident[:]).then_inc(s_pt, 1)
                if s in ((14, 16, 18, 20) if nch == 2 else (14, 18)):
                    pair, c = (s - 14) // 4, (s - 14) // 2 % 2
                    n = nch * pair + c
                    b = (3, 0)[pair]
                    dst = bank[b][:, :].rearrange("p (a b t) -> p a b t", a=2, b=2)
                    if c == 0:
                        pe.wait_ge(s_gr, 4 * it + 2 * pair + 2)
                        pe.wait_ge(s_tev, N_T * it + (13, 15)[pair])
                        if pair == 0:
                            pe.wait_ge(s_oa, 2 * it + 2)
                            if final:
                                pe.wait_ge(s_sld, 16)
                            elif first:
                                pe.wait_ge(s_clr, 4)
                            else:
                                ge(pe, s_su, 8 * it)
                        else:
                            pe.wait_ge(s_ex, 8 * it + 4 * nch)
                        for i in range(2):
                            hh = 2 * pair + i
                            for vh in range(2):
                                v0 = hh * GLA_DV + vh * P
                                pe.matmul(dst[:, i, vh, 0:nq], vg[0:nq, v0:v0 + P],
                                          gsc[0:nq, hh, 0:nch].rearrange("p c t -> p (c t)"),
                                          start=i == 0 and vh == 0, stop=False, skip_group_check=True)
                    else:
                        pe.wait_ge(s_su, 8 * it + 2 * n)
                    for i in range(2):
                        hh = 2 * pair + i
                        for vh in range(2):
                            ins = pe.matmul(dst[:, i, vh, c * CHUNK:(c + 1) * CHUNK], st[:, c, hh, vh * P:(vh + 1) * P], qb[:, hh, c],
                                            start=False, stop=True, skip_group_check=True)
                    ins.then_inc(s_o, 1)
                    if n == 0:
                        ge(pe, s_var, it)
                    else:
                        pe.wait_ge(s_su, 8 * it + 2 * n)
                    for i in range(2):
                        hh = 2 * pair + i
                        ins = pe.matmul(bank[5][:, i * GLA_DV:(i + 1) * GLA_DV], kt_tok[0:nq, c, hh],
                                        vg[0:nq, hh * GLA_DV:(hh + 1) * GLA_DV], start=True, stop=True)
                    ins.then_inc(s_ds, 1)
                if s == 22:
                    pe.wait_ge(s_oev, 2 * it + 2)
                    pe.wait_ge(s_su, 8 * it + 4 * nch)
                    for hh in range(GLA_HEADS):
                        for vh in range(2):
                            ins = pe.matmul(bank[5][0:nq, hh:hh + 1], sq[:, hh, vh, 0:nq], ones[:, 0:1], start=vh == 0, stop=vh == 1)
                    ins.then_inc(s_rm, 1)
                if s == 24:
                    pe.wait_ge(s_gdg, it + 1)
                    pe.matmul(bank[1][:, :].rearrange("p (a q) -> p a q", a=GLA_HEADS)[:, :, 0:nq], ones[0:nq, :], gdiag[0:nq, :, 0:nq],
                              start=True, stop=True).then_inc(s_rb, 1)

            def attend(it, p, m0, count, nxt=True, again=None, fresh=False):
                kts, nch, nq = shape_of(it)
                for steps, j in weave(2 * count, it):
                    start = isinstance(it, int) and (it, j) == (0, 0)
                    if not start:
                        for s in steps:
                            step(s, it, nq, kts, nch)
                    m, h = m0 + j // 2, j % 2
                    unit = N_GATE * p + m
                    pe.wait_ge(s_wlo, 2 * (PASS_GATE + unit) + h + 1)
                    if fresh and j < 2:
                        pe.wait_ge(s_ulo, NX + X_AGAIN * (p - 1) + 4 * j + 4)
                    if h == 0:
                        ge(pe, s_gz, unit - 1)
                    products(bank[6 + m % 2], h, uh[0], ul[0], GAW, s_mg, h == 0, h == 1)
                    if start:
                        for s in steps:
                            step(s, it, nq, kts, nch)

            sequence(pe, attend)

            pe.wait_ge(s_t1, N_IT)
            pe.wait_ge(s_su, 8 * (N_IT - 1) + 4)

            def branch(m):
                for h in range(2):
                    pe.wait_ge(s_wlo, 2 * (m + PASS_BRANCH) + h + 1)
                    for g in range(3):
                        if isinstance(m, int):
                            pe.wait_ge(s_blo, 4 * (3 * h + g) + 4)
                        else:
                            pe.wait_ge((s_ya, s_yg)[h], 3 * (m - 1) + g + 1)
                        products(bank[3 * h + g], h, bh[g], bl[g], GRP[g][1], s_mb, True, True)

            branch(0)
            with pe.Fori(1, N_OUT) as m:
                branch(m)

            pe.wait_ge(s_ya, 3 * N_OUT)
            for g in range(3):
                def pair(i):
                    for r in range(2):
                        m = 2 * i + r
                        n = g * KT + m
                        start = isinstance(m, int) and m == 0
                        ge(pe, s_oev2, n - 1)
                        for h in range(2):
                            pe.wait_ge(s_wlo, 2 * (PASS_OUT + n) + h + 1)
                            if start:
                                pe.wait_ge(s_mlo, NG * g + NG // 2 * (h + 1))
                            products(bank[r], h, mh[g], ml[g], GRP[g][1], s_mo, h == 0, h == 1)
                            if start and g > 0:
                                if h == 0:
                                    pe.wait_ge(s_sqo, 2 * g * KT)
                                    token_sums(GRP[g - 1][1], bank[6], ssqo)
                                else:
                                    spread_roots(g, GRP[g - 1][1], bank[6:7])

                pair(0)
                with pe.Fori(1, KT // 2) as i:
                    pair(i)
            pe.wait_ge(s_sqo, 2 * 3 * KT)
            token_sums(GRP[2][1], bank[6], ssqo)
            spread_roots(3, GRP[2][1], bank[6:7])


def merged_pieces(m):
    return (7 + m, 8 + m) if m == KT - 1 else (7 + m,)


def shape_of(it):
    if it is None:
        return (), 0, 0
    if isinstance(it, int) and it == 0:
        return (1,), 2, P
    if isinstance(it, int) and it == N_IT - 1:
        return (0, 1), 1, DEC
    return (0, 1), 2, P


def tiles(u):
    tt, half, pr = u // 4, (u // 2) % 2, u % 2
    return 4 * tt + 2 * pr, half


def head0(u):
    tile, half = tiles(u)
    return GROUP * (2 * (tile // 4) + half) + tile % 4


def constants():
    import numpy as np
    ident = np.eye(P, dtype=np.float32)
    q, k = np.arange(P)[:, None], np.arange(2 * P)[None, :]
    seen = (k // CHUNK - q // CHUNK >= 0) & (k // CHUNK - q // CHUNK <= WINDOW // CHUNK)
    dist = np.where(seen, np.abs(q + WINDOW - k), -MASKED).astype(np.float32)
    s, t = np.arange(CHUNK)[:, None], np.arange(CHUNK)[None, :]
    decay = [(s <= t)]
    mask = []
    for w in (32, 16, 8, 4, 2, 1):
        ref = t // (2 * w) * 2 * w + w - 1
        right = t // w % 2 == 1
        decay.append(np.where(right, (s > ref) & (s <= t), (s > t) & (s <= ref)))
        mask.append((s // (2 * w) == t // (2 * w)) & (s // w % 2 == 0) & right)
    decay.append(s > t)
    mask.append(s == t)
    decay = np.concatenate(decay, 1).astype(np.float32)
    mask = np.concatenate(mask, 1).astype(np.float32)
    none = np.zeros_like(decay)
    decay = np.block([[decay, none], [none, decay]])
    return ident, dist, decay, np.concatenate([mask, mask], 0)


def kernel(x_prompt, x_sample, cache_k, cache_v, state_gla, norm_pre, norm_post, w_in, b_gate,
           attn_sinks, w_forget_up, b_forget, gla_norm, w_branch_attn, w_branch_gla, w_out):
    import numpy as np
    import concourse.bacc as bacc
    from concourse.bass_utils import run_bass_kernel_spmd

    asc = np.ascontiguousarray
    x = np.concatenate([np.asarray(x_prompt)[0], np.asarray(x_sample)[0]], 0)
    w = np.asarray(w_in)[0]
    cut = np.cumsum([0, 1024, 256, 256, 1024, 512, 512, 1024, 1024, 16, 2048, 2048])
    part = {n: w[:, cut[i]:cut[i + 1]] for i, n in enumerate(("q", "k", "v", "za", "gq", "gk", "gv", "zg", "lr", "ga", "gg"))}
    order = np.arange(HEADS * HEAD_DIM).reshape(2, 2, GROUP, HEAD_DIM).transpose(0, 2, 1, 3).reshape(-1)
    cols = np.concatenate([part["q"][:, order], part["v"], part["za"][:, order], part["k"], part["gq"], part["gk"],
                           part["gv"], part["zg"], part["ga"], part["gg"]], 1)
    branch = np.concatenate([np.asarray(w_branch_attn)[0][order], np.asarray(w_branch_gla)[0]], 0)

    def tiled(a):
        return a.reshape(KT, P, -1, P).transpose(2, 1, 0, 3).reshape(-1, P, KT * P)

    w_tiles = np.concatenate([tiled(cols), tiled(branch), tiled(np.asarray(w_out)[0])], 0)
    up = np.asarray(w_forget_up)[0]
    ident, dist, decay, mask = constants()

    def per_partition(a):
        return asc(a.reshape(-1, P).T)

    ins = {
        "xT": asc(x.T),
        "w_tiles": w_tiles,
        "w_lr": asc(part["lr"].reshape(KT, P, RANK).transpose(1, 0, 2)),
        "w_up": np.concatenate([up, up, np.asarray(b_forget)[0][None], np.zeros((P - 2 * RANK - 1, up.shape[1]), up.dtype)], 0),
        "norms": asc(np.stack([per_partition(np.asarray(norm_pre)[0]), per_partition(np.asarray(norm_post)[0])], 1)),
        "bgate": per_partition(np.asarray(b_gate)[0]),
        "sinks": asc(np.broadcast_to(np.asarray(attn_sinks)[0], (P, HEADS))),
        "gnorm": per_partition(np.asarray(gla_norm)[0]),
        "kT_cache": asc(np.asarray(cache_k)[0, 0].reshape(WINDOW, 2, P).transpose(1, 2, 0)),
        "v_cache": asc(np.asarray(cache_v)[0, 0].reshape(WINDOW, 2 * P)),
        "state_in": asc(np.asarray(state_gla)[0, 0]),
        "ident_c": ident, "dist_c": dist, "decay_c": decay, "mask_c": mask,
    }
    outs = {
        "yT": [D_MODEL, TOKENS], "k_prompt": [2, P, WINDOW], "v_prompt": [2, P, WINDOW],
        "state_prompt": [GLA_HEADS, GLA_DK, GLA_DV], "k_sample": [2, P, WINDOW],
        "v_old": [WINDOW - DEC, 2 * P], "v_new": [2, P, DEC], "state_sample": [GLA_HEADS, GLA_DK, GLA_DV],
    }
    nc = bacc.Bacc("TRN2", target_bir_lowering=False, num_devices=1)
    aps = {n: nc.dram_tensor("in_" + n, a.shape, mybir.dt.from_np(a.dtype), kind="ExternalInput").ap() for n, a in ins.items()}
    aps |= {n: nc.dram_tensor("out_" + n, shape, mybir.dt.float32, kind="ExternalOutput").ap() for n, shape in outs.items()}
    build_trunk(nc, **aps)
    r = run_bass_kernel_spmd(nc, [{"in_" + n: a for n, a in ins.items()}], core_ids=[0])
    got = {n: np.asarray(r.results[0]["out_" + n]) for n in outs}

    def rows(a):
        return asc(a.transpose(2, 0, 1).reshape(1, 1, a.shape[2], KV_HEADS, HEAD_DIM))

    y = got["yT"].T
    v_sample = np.concatenate([got["v_old"].reshape(1, 1, WINDOW - DEC, KV_HEADS, HEAD_DIM), rows(got["v_new"])], 2)
    return (asc(y[None, :SEQ]), asc(y[None, SEQ:]), rows(got["k_prompt"]), rows(got["v_prompt"]),
            got["state_prompt"][None, None], rows(got["k_sample"]), v_sample, got["state_sample"][None, None])
```
